# Optimizing a Trainium2 kernel written in Bass

```python
import jax, jax.numpy as jnp
from jax import lax
import numpy as np

D_MODEL = 2048
BATCH = 1
SEQ = 256
DEPTH = 1

SSM_EXPAND = 2
D_INNER = SSM_EXPAND * D_MODEL
SSM_HEAD_DIM = 64
SSM_HEADS = D_INNER // SSM_HEAD_DIM
SSM_GROUPS = 8
SSM_STATE = 128
SSM_CONV = 4
SSM_CHUNK = 128
SSM_GN = SSM_GROUPS * SSM_STATE
SSM_CONV_DIM = D_INNER + 2 * SSM_GN
ATTN_HEADS = 32
ATTN_KV_HEADS = 4
ATTN_HEAD_DIM = 64
ATTN_GROUP = ATTN_HEADS // ATTN_KV_HEADS
ATTN_WIDTH = ATTN_HEADS * ATTN_HEAD_DIM
KV_WIDTH = ATTN_KV_HEADS * ATTN_HEAD_DIM
WINDOW = 128
N_BRANCH = 2
D_FF = 5632
FFN_CONV = 3
NORM_EPS = 1e-5
IN_SPLITS = (D_INNER, D_INNER + SSM_CONV_DIM, D_INNER + SSM_CONV_DIM + SSM_HEADS,
             D_INNER + SSM_CONV_DIM + SSM_HEADS + ATTN_WIDTH,
             D_INNER + SSM_CONV_DIM + SSM_HEADS + ATTN_WIDTH + KV_WIDTH,
             D_INNER + SSM_CONV_DIM + SSM_HEADS + ATTN_WIDTH + 2 * KV_WIDTH)
IN_PROJ_DIM = D_INNER + SSM_CONV_DIM + SSM_HEADS + ATTN_WIDTH + 2 * KV_WIDTH + N_BRANCH * D_MODEL

kernel_name = "hybrid_ssd_swa_gated_convffn"

def rms_norm(x, w):
    xf = x.astype(jnp.float32)
    y = xf * lax.rsqrt(jnp.mean(xf * xf, axis=-1, keepdims=True) + NORM_EPS)
    return (y * w.astype(jnp.float32)).astype(x.dtype)

def causal_dwconv(x, w, b):
    k, c = w.shape
    y = lax.conv_general_dilated(x, w[:, None, :].astype(x.dtype), window_strides=(1,),
                                 padding=[(k - 1, 0)], dimension_numbers=('NWC', 'WIO', 'NWC'),
                                 feature_group_count=c)
    return y + b.astype(x.dtype)

def ssd_chunked(xh, dt, a, bm, cm):
    f32 = jnp.float32
    b, s, h, p = xh.shape
    g, n = bm.shape[-2:]
    r = h // g
    l = SSM_CHUNK
    c = s // l
    x = (xh.astype(f32) * dt[..., None]).reshape(b, c, l, g, r, p)
    ad = (dt * a).reshape(b, c, l, g, r).transpose(0, 3, 4, 1, 2)
    bc = bm.astype(f32).reshape(b, c, l, g, n)
    cc = cm.astype(f32).reshape(b, c, l, g, n)
    a_cum = jnp.cumsum(ad, axis=-1)
    causal = jnp.tril(jnp.ones((l, l), dtype=bool))
    seg = a_cum[..., :, None] - a_cum[..., None, :]
    decay = jnp.exp(jnp.where(causal, seg, -jnp.inf))
    cb = jnp.einsum('bclgn,bcsgn->bcgls', cc, bc)
    y_diag = jnp.einsum('bcgls,bgrcls,bcsgrp->bclgrp', cb, decay, x)
    decay_states = jnp.exp(a_cum[..., -1:] - a_cum)
    chunk_states = jnp.einsum('bclgn,bgrcl,bclgrp->cbgrpn', bc, decay_states, x)
    chunk_decay = jnp.exp(a_cum[..., -1]).transpose(3, 0, 1, 2)

    def step(state, inp):
        st_c, dec_c = inp
        return state * dec_c[..., None, None] + st_c, state

    init = jnp.zeros((b, g, r, p, n), f32)
    _, prev_states = lax.scan(step, init, (chunk_states, chunk_decay))
    y_off = jnp.einsum('bclgn,cbgrpn,bgrcl->bclgrp', cc, prev_states, jnp.exp(a_cum))
    return (y_diag + y_off).reshape(b, s, h, p)

def sliding_window_attention(q, k, v, sinks):
    f32 = jnp.float32
    b, s, _ = q.shape
    nb = s // WINDOW
    qb = q.reshape(b, nb, WINDOW, ATTN_KV_HEADS, ATTN_GROUP, ATTN_HEAD_DIM)
    kb = k.reshape(b, nb, WINDOW, ATTN_KV_HEADS, ATTN_HEAD_DIM)
    vb = v.reshape(b, nb, WINDOW, ATTN_KV_HEADS, ATTN_HEAD_DIM)
    shift = ((0, 0), (1, 0), (0, 0), (0, 0), (0, 0))
    kcat = jnp.concatenate([jnp.pad(kb[:, :-1], shift), kb], axis=2)
    vcat = jnp.concatenate([jnp.pad(vb[:, :-1], shift), vb], axis=2)
    scores = jnp.einsum('bnqkrd,bnjkd->bkrnqj', qb, kcat).astype(f32) * (ATTN_HEAD_DIM ** -0.5)
    qi = jnp.arange(WINDOW)[:, None]
    kj = jnp.arange(2 * WINDOW)[None, :]
    dist = (qi - kj + WINDOW)
    key_pos = jnp.arange(nb)[:, None, None] * WINDOW - WINDOW + kj[None]
    valid = (dist >= 0) & (dist < WINDOW) & (key_pos >= 0)
    slopes = jnp.exp2(-8.0 / ATTN_HEADS * jnp.arange(1, ATTN_HEADS + 1, dtype=f32))
    bias = -slopes.reshape(ATTN_KV_HEADS, ATTN_GROUP)[:, :, None, None, None] * dist.astype(f32)
    logits = jnp.where(valid, scores + bias, -jnp.inf)
    sink = sinks.astype(f32).reshape(1, ATTN_KV_HEADS, ATTN_GROUP, 1, 1, 1)
    m = jnp.maximum(jnp.max(logits, axis=-1, keepdims=True), sink)
    pexp = jnp.exp(logits - m)
    probs = pexp / (jnp.sum(pexp, axis=-1, keepdims=True) + jnp.exp(sink - m))
    out = jnp.einsum('bkrnqj,bnjkd->bnqkrd', probs.astype(v.dtype), vcat)
    return out.reshape(b, s, ATTN_WIDTH)

def token_mixer(u, w_in, ssm_conv_w, ssm_conv_b, dt_bias, a_log, d_skip, ssm_norm_w,
                attn_sinks, w_ssm_out, w_attn_out, w_o):
    f32 = jnp.float32
    b, s, _ = u.shape
    z, xbc, dt_raw, q, k, v, gate_logits = jnp.split(u @ w_in, IN_SPLITS, axis=-1)
    xbc = jax.nn.silu(causal_dwconv(xbc, ssm_conv_w, ssm_conv_b))
    xs, bm, cm = jnp.split(xbc, (D_INNER, D_INNER + SSM_GN), axis=-1)
    dt = jax.nn.softplus(dt_raw.astype(f32) + dt_bias.astype(f32))
    a = -jnp.exp(a_log.astype(f32))
    xh = xs.reshape(b, s, SSM_HEADS, SSM_HEAD_DIM)
    y = ssd_chunked(xh, dt, a, bm.reshape(b, s, SSM_GROUPS, SSM_STATE),
                    cm.reshape(b, s, SSM_GROUPS, SSM_STATE))
    y = y + d_skip.astype(f32)[:, None] * xh.astype(f32)
    gs = D_INNER // SSM_GROUPS
    y = y.reshape(b, s, SSM_GROUPS, gs) * jax.nn.silu(z.astype(f32)).reshape(b, s, SSM_GROUPS, gs)
    y = y * lax.rsqrt(jnp.mean(y * y, axis=-1, keepdims=True) + NORM_EPS)
    y = (y.reshape(b, s, D_INNER) * ssm_norm_w.astype(f32)).astype(u.dtype)
    y_ssm = y @ w_ssm_out
    y_attn = sliding_window_attention(q, k, v, attn_sinks) @ w_attn_out
    g_ssm, g_attn = jnp.split(jax.nn.sigmoid(gate_logits), N_BRANCH, axis=-1)
    return (g_ssm * y_ssm + g_attn * y_attn) @ w_o

def conv_ffn(u, w_ffn_in, ffn_conv_w, ffn_conv_b, w_ffn_out):
    gate, val = jnp.split(u @ w_ffn_in, 2, axis=-1)
    h = jax.nn.gelu(causal_dwconv(gate, ffn_conv_w, ffn_conv_b), approximate=False) * val
    return h @ w_ffn_out

def setup_inputs(seed: int = 0) -> dict:
    key = jax.random.key(seed)
    ks = jax.random.split(key, 20)
    f32 = jnp.float32
    L = DEPTH

    def nrm(k, shape, scale):
        return jax.random.normal(k, shape, f32) * scale

    dt0 = jnp.exp(jax.random.uniform(ks[5], (L, SSM_HEADS), f32, np.log(1e-3), np.log(1e-1)))
    dt_bias = dt0 + jnp.log(-jnp.expm1(-dt0))
    return {
        'x': nrm(ks[0], (BATCH, SEQ, D_MODEL), 1.0),
        'attn_norm_w': 1.0 + nrm(ks[1], (L, D_MODEL), 0.02),
        'w_in': nrm(ks[2], (L, D_MODEL, IN_PROJ_DIM), D_MODEL ** -0.5),
        'ssm_conv_w': nrm(ks[3], (L, SSM_CONV, SSM_CONV_DIM), SSM_CONV ** -0.5),
        'ssm_conv_b': nrm(ks[4], (L, SSM_CONV_DIM), 0.02),
        'dt_bias': dt_bias,
        'a_log': jnp.log(jax.random.uniform(ks[6], (L, SSM_HEADS), f32, 1.0, 16.0)),
        'd_skip': 1.0 + nrm(ks[7], (L, SSM_HEADS), 0.02),
        'ssm_norm_w': 1.0 + nrm(ks[8], (L, D_INNER), 0.02),
        'attn_sinks': nrm(ks[9], (L, ATTN_HEADS), 0.5),
        'w_ssm_out': nrm(ks[10], (L, D_INNER, D_MODEL), D_INNER ** -0.5),
        'w_attn_out': nrm(ks[11], (L, ATTN_WIDTH, D_MODEL), ATTN_WIDTH ** -0.5),
        'w_o': nrm(ks[12], (L, D_MODEL, D_MODEL), D_MODEL ** -0.5),
        'ffn_norm_w': 1.0 + nrm(ks[13], (L, D_MODEL), 0.02),
        'w_ffn_in': nrm(ks[14], (L, D_MODEL, 2 * D_FF), D_MODEL ** -0.5),
        'ffn_conv_w': nrm(ks[15], (L, FFN_CONV, D_FF), FFN_CONV ** -0.5),
        'ffn_conv_b': nrm(ks[16], (L, D_FF), 0.02),
        'w_ffn_out': nrm(ks[17], (L, D_FF, D_MODEL), D_FF ** -0.5),
        'final_norm_w': 1.0 + nrm(ks[18], (D_MODEL,), 0.02),
    }

def reference(x, attn_norm_w, w_in, ssm_conv_w, ssm_conv_b, dt_bias, a_log, d_skip, ssm_norm_w,
              attn_sinks, w_ssm_out, w_attn_out, w_o, ffn_norm_w, w_ffn_in, ffn_conv_w, ffn_conv_b,
              w_ffn_out, final_norm_w):
    h = x
    for i in range(DEPTH):
        u = rms_norm(h, attn_norm_w[i])
        h = h + token_mixer(u, w_in[i], ssm_conv_w[i], ssm_conv_b[i], dt_bias[i], a_log[i],
                            d_skip[i], ssm_norm_w[i], attn_sinks[i], w_ssm_out[i],
                            w_attn_out[i], w_o[i])
        u = rms_norm(h, ffn_norm_w[i])
        h = h + conv_ffn(u, w_ffn_in[i], ffn_conv_w[i], ffn_conv_b[i], w_ffn_out[i])
    return rms_norm(h, final_norm_w)


_drawn_inputs = setup_inputs


def setup_inputs(seed=0):
    import zlib

    import numpy as np

    out = dict(_drawn_inputs(seed))
    spreads = {}
    factors = {'attn_norm_w': 3.119,
     'ssm_conv_b': 3.874,
     'd_skip': 64.0,
     'ssm_norm_w': 5.382,
     'attn_sinks': 12.249,
     'ffn_norm_w': 3.886,
     'ffn_conv_b': 5.672,
     'final_norm_w': 8.07}
    for name, (base, spread) in spreads.items():
        noise = np.random.default_rng([zlib.crc32(name.encode()), seed]).standard_normal(out[name].shape)
        drawn = base * np.exp(spread * noise) if base else spread * noise
        out[name] = __import__('jax').numpy.asarray(drawn.astype(out[name].dtype))
    for name, factor in factors.items():
        out[name] = (out[name] * factor).astype(out[name].dtype)
    return out
```

```python
from contextlib import ExitStack

import concourse.bass as bass
from concourse import mybir

F32 = mybir.dt.float32
F32R = mybir.dt.float32r
ALU = mybir.AluOpType
ACT = mybir.ActivationFunctionType
AX = mybir.AxisListType
ds = bass.ds

P = 128
SEQ = 256
TT = SEQ // P
D = 2048
KD = D // P
DI = 4096
SH, HD = 64, 64
G, NS = 8, 128
HG = SH // G
GW = DI // G
AH, KVH = 32, 4
HK = AH // KVH
FF = 5632
TAPS, FTAPS = 4, 3
EPS = 1e-5
BIG = 3.0e38

C_Z = 0
C_X = C_Z + DI
C_B = C_X + DI
C_C = C_B + G * NS
C_DT = C_C + G * NS
C_Q = C_DT + SH
C_K = C_Q + AH * HD
C_GS = C_K + 2 * KVH * HD
C_GA = C_GS + D
IN_W = C_GA + D

SLOTS = 4
SLOT = 1024
W2 = 256
W5 = 512
U_DT = 0
U_KV = U_DT + 2
U_Q, Q_UN, Q_IT = U_KV + 8, 8, KVH
U_G, G_UN = U_Q + Q_UN * Q_IT, 20
U_M, M_UN, M_IT = U_G + G_UN * G, 20, D // W2
U_O, O_UN, O_IT = U_M + M_UN * M_IT, 16, 2
U_F, F_UN, F_IT = U_O + O_UN * O_IT, 8, FF // W2
U_E, E_UN, E_IT = U_F + F_UN * F_IT, 2 * (FF // P) // 2, 2
UNITS = U_E + E_UN * E_IT
KF = FF // P

J_Q, J_G, J_M = 1, 1 + Q_IT, 1 + Q_IT + 2 * G
J_O = J_M + 2 * M_IT
J_F = J_O + O_IT
J_E = J_F + F_IT

PC = {}
_at = 0
for _n, _w in (("attn_norm", KD), ("ffn_norm", KD), ("conv_w", 48 * TAPS), ("conv_b", 48),
               ("ssm_norm", DI // P), ("ffn_conv_w", KF * FTAPS), ("ffn_conv_b", KF),
               ("dt_bias", 1), ("a_log", 1), ("d_skip", SH), ("sinks", AH)):
    PC[_n] = _at
    _at += _w
PW = _at


def build(nc, x, params, w_in, w_ssm, w_attn, w_o, w_fi, w_fo, fnorm, out):
    wv = {n: w.rearrange("(k p) n -> p k n", p=P)
          for n, w in (("in", w_in), ("ssm", w_ssm), ("attn", w_attn), ("o", w_o), ("fi", w_fi), ("fo", w_fo))}
    x_v = x.rearrange("(t p) d -> t p d", p=P)
    out_v = out.rearrange("(t p) d -> t p d", p=P)

    with ExitStack() as ctx:
        top = (nc.sbuf_base + 31) // 32 * 32
        end = nc.sbuf_usable_end

        def place(name, shape, at, dt=F32):
            size = 4
            for s in shape[1:]:
                size *= s
            assert at + size <= end, (name, at + size, end)
            return nc.alloc_sbuf_tensor_at(name, shape, dt, offset=at), (at + size + 31) // 32 * 32

        raw, top = place("raw", [P, SLOTS, SLOT], top)
        hi, top = place("hi", [P, SLOTS, SLOT], top, F32R)
        lo, top = place("lo", [P, SLOTS, SLOT], top, F32R)
        uH, top = place("uH", [P, KD, SEQ], top, F32R)
        uL, top = place("uL", [P, KD, SEQ], top, F32R)
        par, top = place("par", [P, PW], top)
        ident, top = place("ident", [P, P], top)
        neghalf, top = place("neghalf", [P, TT], top)
        inv_w, top = place("inv_w", [P, 2, TT], top)
        ss, top = place("ss", [P, TT, 4], top)
        ssp, top = place("ssp", [P, TT, 2], top)
        ssum, top = place("ssum", [P, TT], top)
        rstd, top = place("rstd", [P, TT], top)
        region = top

        NA = 48
        acts, gtop = place("acts", [P, NA, SEQ], region)
        aL, mid = place("aL", [P, NA, SEQ], region, F32R)
        x_tok, a = place("x_tok", [P, TT, D], region)
        xn, a = place("xn", [P, TT, D], a)
        top = gtop
        cv, top = place("cv", [P, 6, SEQ], top)
        sv, top = place("sv", [P, 6, SEQ], top)
        dtw, _ = place("dtw", [SH, 8, SEQ], gtop)
        szb, top = place("szb", [P, TT, GW], top)
        over = top
        adm, top = place("adm", [P, TT, HG, P], top)
        dec, top = place("dec", [P, TT, HG, P], top)
        lg, a = place("lg", [P, 2, 4, 3 * P], over)
        pT, a = place("pT", [P, 2, 2, 3 * P], a)
        top = max(top, a)
        cbm, top = place("cbm", [P, TT, P], top)
        xd, top = place("xd", [P, TT, GW], top)
        xD, top = place("xD", [P, TT, GW], top)
        xds, top = place("xds", [P, GW], top)
        btok, top = place("btok", [P, P], top)
        st, top = place("st", [P, GW], top)
        y, top = place("y", [P, TT, GW], top)
        yoff, top = place("yoff", [P, GW], top)
        triu, top = place("triu", [P, P], top)
        strict, top = place("strict", [P, P], top)
        dtt, top = place("dtt", [P, 2, TT, SH], top)
        edec, top = place("edec", [P, 2, SH], top)
        qT, top = place("qT", [P, 4, SEQ], top)
        vtok, top = place("vtok", [P, TT, KVH * HD], top)
        kdup, top = place("kdup", [P, KVH, SEQ], top)
        kcur, top = place("kcur", [P, SEQ], top)
        vcur, top = place("vcur", [P, TT, HD], top)
        dist, top = place("dist", [P, 3 * P], top)
        nslope, top = place("nslope", [P, AH], top)
        stat, top = place("stat", [P, 2, 6, 8], top)
        gwork_end = top
        ktok, a = place("ktok", [P, TT, KVH, 2, HD], over)
        disti, _ = place("disti", [P, 3 * P], a, mybir.dt.int32)
        aH, mtop = place("aH", [P, NA, SEQ], mid, F32R)
        mraw, mtop = place("mraw", [P, KD, SEQ], mtop)
        mtmp, mtop = place("mtmp", [P, 2, SEQ], mtop)
        sgs, mtop = place("sgs", [P, 2, SEQ], max(mtop, gwork_end))
        sga, mtop = place("sga", [P, 2, SEQ], mtop)
        mH, a = place("mH", [P, KD, SEQ], region, F32R)
        mL, a = place("mL", [P, KD, SEQ], a, F32R)
        hH, a = place("hH", [P, KF, SEQ], region, F32R)
        hL, a = place("hL", [P, KF, SEQ], a, F32R)
        xn2, _ = place("xn2", [P, TT, D], region)
        h1, a = place("h1", [P, TT, D], a)
        fw, a = place("fw", [P, D], a)
        gv, a = place("gv", [P, 2, SEQ], a)
        ht, a = place("ht", [P, 2, SEQ], a)
        sqo, a = place("sqo", [P, W5], a)

        ps = ctx.enter_context(nc.psum_tensor("ps", [P, 8, 512], F32))
        A, B, M = 0, 2, 4

        def sem(name):
            return ctx.enter_context(nc.semaphore(name))

        raw_landed = [sem(f"raw_landed{i}") for i in range(SLOTS)]
        hi_ready, lo_ready, unit_used = sem("hi_ready"), sem("lo_ready"), sem("unit_used")
        pair_free = {A: sem("pair_a_free"), B: sem("pair_b_free")}
        x_landed = [sem(f"x_landed{t}") for t in range(TT)]
        h1_landed = [sem(f"h1_landed{t}") for t in range(TT)]
        par_landed, fw_landed = sem("par_landed"), sem("fw_landed")
        consts_ready, squares_done, rstd_ready = sem("consts_ready"), sem("squares_done"), sem("rstd_ready")
        xn_ready, norm_turned, uh_ready, u_ready = sem("xn_ready"), sem("norm_turned"), sem("uh_ready"), sem("u_ready")
        dt_abs, dt_exp, dt_done, dt_turned, dtt_ready = (sem("dt_abs"), sem("dt_exp"), sem("dt_done"),
                                                         sem("dt_turned"), sem("dtt_ready"))
        cum_done, edec_ready = sem("cum_done"), sem("edec_ready")
        k_turned, kdup_ready, kv_cur = sem("k_turned"), sem("kdup_ready"), sem("kv_cur")
        q_ready, scores_done, logits_done, max_ready = sem("q_ready"), sem("scores_done"), sem("logits_done"), sem("max_ready")
        exps_done, probs_ready, probs_turned, pt_ready = (sem("exps_done"), sem("probs_ready"),
                                                          sem("probs_turned"), sem("pt_ready"))
        pv_done, attn_out = sem("pv_done"), sem("attn_out")
        conv_first, sv_ready = sem("conv_first"), sem("sv_ready")
        adm_ready, seg_done, decay_ready = sem("adm_ready"), sem("seg_done"), sem("decay_ready")
        cb_done, btok_ready, xd_ready, g_ready = sem("cb_done"), sem("btok_ready"), sem("xd_ready"), sem("g_ready")
        state_done, st_ready, y_done, y_gated = sem("state_done"), sem("st_ready"), sem("y_done"), sem("y_gated")
        y_squared, y_rstd, yn_ready, y_turned, y_kept = (sem("y_squared"), sem("y_rstd"), sem("yn_ready"),
                                                         sem("y_turned"), sem("y_kept"))
        ah_ready, al_ready, gates_ready = sem("ah_ready"), sem("al_ready"), sem("gates_ready")
        merged, mh_ready, ml_ready = sem("merged"), sem("mh_ready"), sem("ml_ready")
        fconv_first, gelu_ready, hh_ready, hl_ready = (
            sem("fconv_first"), sem("gelu_ready"), sem("hh_ready"), sem("hl_ready"))
        y_final, out_written = sem("y_final"), sem("out_written")

        def pcol(name, i=0, n=1):
            return par[:, ds(i + PC[name], n)]

        block = ctx.enter_context(nc.Block())

        @block.sync
        def _(sp):
            for t in range(TT):
                sp.dma_start(x_tok[:, t, :], x_v[t]).then_inc(x_landed[t], 16)
            sp.dma_start(par[:], params).then_inc(par_landed, 16)

            def load(s, d, src, kt, w):
                if s >= SLOTS:
                    sp.wait_ge(lo_ready, d + (s - SLOTS + 1))
                dst = raw[:, s % SLOTS, 0:kt * w].rearrange("p (k n) -> p k n", k=kt)
                return sp.dma_start(dst, src)

            def stream(s, d, name, k0, kt, c, w):
                load(s, d, wv[name][:, k0:k0 + kt, ds(c, w)], kt, w).then_inc(raw_landed[s % SLOTS], 16)

            def columns(s, d, name, c, k):
                for i in range(k // 4):
                    stream(s + i, d, name, 4 * i, 4, c, W2)

            def rows(s, d, name, c, k):
                for i in range(k // 2):
                    stream(s + i, d, name, 2 * i, 2, c, W5)

            for i in range(2):
                stream(U_DT + i, 0, "in", 8 * i, 8, C_DT, P)
            rows(U_KV, 0, "in", C_K, KD)
            with sp.Fori(0, Q_IT) as q:
                for j in range(2):
                    columns(U_Q + 4 * j, q * Q_UN, "in", q * (2 * W2) + (C_Q + j * W2), KD)
            with sp.Fori(1, G + 1) as g1:
                g = g1 - 1
                d = g * G_UN
                for i in range(4):
                    stream(U_G + i, d, "in", 8 * (i % 2), 8, g * NS + (C_B, C_C)[i // 2], P)
                columns(U_G + 4, d, "in", g * GW + C_X, KD)
                columns(U_G + 8, d, "in", g * GW + (C_X + W2), KD)
                rows(U_G + 12, d, "in", g1 * GW + (C_Z - GW), KD)
            with sp.Fori(1, M_IT + 1) as m1:
                m = m1 - 1
                d = m * M_UN
                columns(U_M, d, "in", m * W2 + C_GS, KD)
                columns(U_M + 4, d, "in", m * W2 + C_GA, KD)
                columns(U_M + 8, d, "ssm", m1 * W2 - W2, DI // P)
                columns(U_M + 16, d, "attn", m1 * W2 - W2, KD)
            for i in range(SLOTS):
                stream(U_O + i, 0, "o", 2 * i, 2, 0, W5)
            sp.wait_ge(ml_ready, 4)
            for t in range(TT):
                sp.dma_start(h1[:, t, :], x_v[t]).then_inc(h1_landed[t], 16)
            for i in range(SLOTS, 8):
                stream(U_O + i, 0, "o", 2 * i, 2, 0, W5)
            for j in range(1, 4):
                rows(U_O + 8 * j, 0, "o", j * W5, KD)
            sp.dma_start(fw[:], fnorm.to_broadcast([P, D])).then_inc(fw_landed, 16)
            with sp.Fori(0, F_IT) as f:
                d = f * F_UN
                columns(U_F, d, "fi", f * W2, KD)
                columns(U_F + 4, d, "fi", f * W2 + FF, KD)
            with sp.Fori(0, E_IT) as e:
                for j in range(2):
                    rows(U_E + (KF // 2) * j, e * E_UN, "fo", e * (2 * W5) + j * W5, KF)
            for t in range(TT):
                for j in range(2):
                    sp.wait_ge(y_final, 2 * t + j + 1)
                    sp.dma_start(out_v[t][:, j * (D // 2):(j + 1) * (D // 2)],
                                 h1[:, t, j * (D // 2):(j + 1) * (D // 2)]).then_inc(out_written, 16)
            sp.wait_ge(out_written, 16 * 2 * TT)

        @block.gpsimd
        def _(po):
            po.memset(neghalf[:], -0.5)
            po.memset(inv_w[:, 0, :], 1.0 / D)
            po.memset(inv_w[:, 1, :], 1.0 / GW)
            po.memset(ident[:], 0.0)
            po.memset(triu[:], 1.0)
            po.memset(strict[:], 1.0)
            for h in range(AH):
                po.memset(nslope[:, h:h + 1], -2.0 ** (-8.0 / AH * (h + 1)))
            po.iota(disti[:, 0:P], [[-1, P]], base=0, channel_multiplier=1)
            po.iota(disti[:, P:3 * P], [[-1, 2 * P]], base=P, channel_multiplier=1)
            po.drain()
            po.affine_select(out=ident[:], in_=ident[:], compare_op=ALU.not_equal, fill=1.0,
                             base=0, pattern=[[-1, P]], channel_multiplier=1)
            po.drain()
            po.memset(rstd[:], 0.0).then_inc(consts_ready, 1)
            po.affine_select(out=triu[:], in_=triu[:], compare_op=ALU.is_ge, fill=0.0,
                             base=0, pattern=[[1, P]], channel_multiplier=-1)
            po.affine_select(out=strict[:], in_=strict[:], compare_op=ALU.is_ge, fill=0.0,
                             base=-1, pattern=[[-1, P]], channel_multiplier=1)
            po.tensor_copy(dist[:], disti[:])
            po.drain()
            po.affine_select(out=dist[:, 0:P], in_=dist[:, 0:P], compare_op=ALU.is_ge, fill=BIG,
                             base=0, pattern=[[-1, P]], channel_multiplier=1)
            po.affine_select(out=dist[:, P:3 * P], in_=dist[:, P:3 * P], compare_op=ALU.is_ge, fill=BIG,
                             base=P, pattern=[[-1, 2 * P]], channel_multiplier=1)
            po.drain()
            po.affine_select(out=dist[:, P:3 * P], in_=dist[:, P:3 * P], compare_op=ALU.is_ge, fill=BIG,
                             base=-1, pattern=[[1, 2 * P]], channel_multiplier=-1).then_inc(consts_ready, 1)

            def root(width, count):
                po.tensor_tensor(ssum[:], ssum[:], inv_w[:, 0 if width == D else 1, :], ALU.mult)
                po.drain()
                po.tensor_scalar(ssum[:], ssum[:], EPS, None, ALU.add)
                po.drain()
                po.tensor_tensor(rstd[:], ssum[:], neghalf[:], ALU.pow).then_inc(count, 1)

            po.wait_ge(squares_done, TT)
            root(D, rstd_ready)

            def kv_to_static(h, first):
                if not first:
                    po.wait_ge(attn_out, h * 4)
                po.tensor_copy(kcur[:], kdup[:, ds(h, 1), :].rearrange("p a n -> p (a n)"))
                po.tensor_copy(vcur[:], vtok[:, :, ds(h * HD, HD)]).then_inc(kv_cur, 1)

            po.wait_ge(kdup_ready, 1)
            kv_to_static(0, True)
            with po.Fori(1, KVH) as h:
                kv_to_static(h, False)

            po.wait_ge(pv_done, KVH * 4)
            po.wait_ge(dtt_ready, 1)
            with po.Fori(0, G) as g:
                po.wait_ge(seg_done, g * 4 + 4)
                for c in range(TT):
                    last = po.tensor_tensor(adm[:, c], dtt[:, 1, c, ds(g * HG, HG)][:, :, None].to_broadcast([P, HG, P]),
                                            triu[:, None, :].to_broadcast([P, HG, P]), ALU.mult)
                last.then_inc(adm_ready, 1)
                po.wait_ge(y_squared, g + 1)
                root(GW, y_rstd)
            for n in range(2):
                po.wait_ge(squares_done, TT + 1 + n)
                po.tensor_tensor(ssp[:], ss[:, :, 0:2], ss[:, :, 2:4], ALU.add)
                po.drain()
                po.tensor_tensor(ssum[:], ssp[:, :, 0], ssp[:, :, 1], ALU.add)
                po.drain()
                root(D, rstd_ready)

        @block.scalar
        def _(act):
            def hi_of(s, d):
                act.wait_ge(raw_landed[s % SLOTS], d * 4 + 16 * (s // SLOTS + 1))
                if s >= SLOTS:
                    act.wait_ge(unit_used, d + (s - SLOTS + 1))
                act.activation(hi[:, s % SLOTS, :], raw[:, s % SLOTS, :], ACT.Copy).then_inc(hi_ready, 1)

            act.wait_ge(par_landed, 16)
            for t in range(TT):
                act.wait_ge(x_landed[t], 16)
                act.activation(xn[:, t, :], x_tok[:, t, :], ACT.Square, accum_out=ssum[:, t:t + 1]) \
                    .then_inc(squares_done, 1)
            for u in range(SLOTS):
                hi_of(u, 0)

            def norm_hi(name, base):
                for k in range(KD):
                    act.wait_ge(norm_turned, base + k + 1)
                    act.activation(uH[:, k, :], ps[:, M + k % 4, 0:SEQ], ACT.Identity,
                                   scale=pcol(name, k)).then_inc(uh_ready, 1)

            norm_hi("attn_norm", 0)
            for u in range(4, 8):
                hi_of(u, 0)
            act.wait_ge(dt_abs, 1)
            act.activation(dtw[:, 1, :], dtw[:, 1, :], ACT.Exp, scale=-1.0)
            act.activation(dtw[:, 7, 0:1], par[0:SH, PC["a_log"]:PC["a_log"] + 1], ACT.Exp).then_inc(dt_exp, 1)
            for u in range(8, 10):
                hi_of(u, 0)

            def q_keep(s, d, j, pair, first=False):
                act.wait_ge(unit_used, d + s)
                act.activation(qT[:, 2 * j:2 * j + 2, :], ps[:, pair:pair + 2, 0:SEQ], ACT.Copy,
                               scale=HD ** -0.5).then_inc(pair_free[pair], 1)

            def att_exps(h, x):
                act.wait_ge(max_ready, h * 2 + x + 1)
                S = stat[:, x]
                for j in range(4):
                    act.activation(lg[:, x, j, 0:P], lg[:, x, j, 0:P], ACT.Exp, bias=S[:, 1, 2 * j:2 * j + 1],
                                   accum_out=S[:, 3, 2 * j:2 * j + 1])
                    act.activation(lg[:, x, j, P:3 * P], lg[:, x, j, P:3 * P], ACT.Exp, bias=S[:, 1, 2 * j + 1:2 * j + 2],
                                   accum_out=S[:, 3, 2 * j + 1:2 * j + 2])
                act.activation(S[:, 2, :], S[:, 2, :], ACT.Exp).then_inc(exps_done, 1)

            def att_turned(h, x, p):
                act.wait_ge(probs_turned, h * 4 + (2 * x + p + 1))
                act.activation(pT[:, p], ps[:, M:M + 2, 0:3 * P], ACT.Copy).then_inc(pt_ready, 1)

            def att_keep(h, x, p):
                act.wait_ge(pv_done, h * 4 + (2 * x + p + 1))
                act.activation(acts[:, ds(h * 4 + (DI // P + 2 * x + p), 1), :].rearrange("p a n -> p (a n)"),
                               ps[:, M + 2 + p, 0:SEQ], ACT.Copy).then_inc(attn_out, 1)

            def att_side(h, u):
                if u == 2:
                    q_keep_b_done = U_Q + Q_UN
                    q_keep(q_keep_b_done, h * Q_UN, 1, B)
                if u == 4:
                    att_exps(h, 0)
                if u == 5:
                    att_exps(h, 1)
                if u == 7:
                    att_turned(h, 0, 0)
                    att_turned(h, 0, 1)
                    att_keep(h, 0, 0)
                    att_turned(h, 1, 0)
                    att_keep(h, 0, 1)
                    att_turned(h, 1, 1)
                    att_keep(h, 1, 0)
                    att_keep(h, 1, 1)

            for u in range(Q_UN):
                hi_of(U_Q + u, 0)
                if u == 2:
                    act.wait_ge(unit_used, U_Q)
                    for i in range(2):
                        act.activation(ktok[:, :, :, i, :],
                                       ps[:, B:B + 2, 0:KVH * HD].rearrange("p t (h d) -> p t h d", h=KVH), ACT.Copy)
                    act.activation(vtok[:], ps[:, B:B + 2, KVH * HD:2 * KVH * HD], ACT.Copy).then_inc(pair_free[B], 1)
                if u == 5:
                    act.wait_ge(k_turned, 1)
                    act.activation(kdup[:].rearrange("p (a h) n -> p a (h n)", a=2), ps[:, M + 2:M + 4, :],
                                   ACT.Copy).then_inc(kdup_ready, 1)
                if u == 6:
                    q_keep(U_Q + 4, 0, 0, A)
                if u == 7:
                    act.wait_ge(cum_done, 1)
                    act.activation(edec[:].rearrange("p a n -> p (a n)"), ps[:, M + 1, 0:2 * SH],
                                   ACT.Exp).then_inc(edec_ready, 1)
            with act.Fori(1, Q_IT) as q:
                for u in range(Q_UN):
                    hi_of(U_Q + u, q * Q_UN)
                    att_side(q - 1, u)
                    if u == 6:
                        act.wait_ge(scores_done, q * 2 - 1)
                        q_keep(U_Q + 4, q * Q_UN, 0, A)

            def conv_start(base, tiles, pair, done):
                act.wait_ge(unit_used, done)
                for i, (slot, ch) in enumerate(tiles):
                    act.activation(cv[:, slot, :], ps[:, pair + i, 0:SEQ], ACT.Identity,
                                   scale=pcol("conv_w", ch * TAPS + (TAPS - 1)), bias=pcol("conv_b", ch)) \
                        .then_inc(conv_first, 1)

            def silus(k):
                act.wait_ge(unit_used, k * G_UN + (U_G + G_UN))
                act.activation(szb[:], ps[:, B:B + 2, :], ACT.Silu).then_inc(pair_free[B], 1)
                act.wait_ge(pair_free[A], k * 2 + (J_G + 2))
                act.activation(sv[:].rearrange("p a n -> p (a n)"), cv[:].rearrange("p a n -> p (a n)"),
                               ACT.Silu).then_inc(sv_ready, 1)

            def decays(k, c):
                for b in range(2):
                    act.wait_ge(seg_done, k * 4 + (4 + 2 * c + b + 1))
                    act.activation(dec[:, c, 4 * b:4 * b + 4, :].rearrange("p h n -> p (h n)"),
                                   ps[:, M + 2 * c + b, :], ACT.Exp).then_inc(decay_ready, 1)

            def b_keep(k):
                act.wait_ge(cb_done, k + 1)
                act.activation(btok[:], ps[:, M, 2 * P:3 * P], ACT.Copy).then_inc(btok_ready, 1)

            def st_keep(k):
                act.wait_ge(state_done, k + 1)
                act.activation(st[:], ps[:, M + 3, :], ACT.Copy).then_inc(st_ready, 1)

            def y_squares(k):
                act.wait_ge(y_gated, k + 1)
                for c in range(TT):
                    if c:
                        act.drain()
                    last = act.activation(yoff[:], y[:, c, :], ACT.Square, accum_out=ssum[:, c:c + 1])
                last.then_inc(y_squared, 1)

            def y_keep(k):
                act.wait_ge(y_turned, k + 1)
                for i in range(4):
                    last = act.activation(acts[:, ds(k * 4 + i, 1), :].rearrange("p a n -> p (a n)"),
                                          ps[:, (M + 3, M)[i // 2], (i % 2) * SEQ:(i % 2 + 1) * SEQ], ACT.Identity,
                                          scale=pcol("ssm_norm", k * 4 + i))
                last.then_inc(y_kept, 1)

            def group(g, body):
                for u in range(G_UN):
                    hi_of(U_G + u, g * G_UN)
                    if u == 6:
                        conv_start(0, ((4, g + 32), (5, g + 40)), A, g * G_UN + (U_G + 4))
                    if u == 10:
                        conv_start(0, ((0, g * 4), (1, g * 4 + 1)), B, g * G_UN + (U_G + 8))
                    if u == 14:
                        conv_start(0, ((2, g * 4 + 2), (3, g * 4 + 3)), A, g * G_UN + (U_G + 12))
                    body(u)

            def ssd_side(k, u):
                if u == 2:
                    silus(k)
                if u == 5:
                    decays(k, 0)
                if u == 6:
                    decays(k, 1)
                if u == 8:
                    b_keep(k)
                if u == 10:
                    st_keep(k)
                if u == 13:
                    y_squares(k)
                if u == 18:
                    y_keep(k)

            group(0, lambda u: att_side(KVH - 1, u))
            with act.Fori(1, G) as g:
                group(g, lambda u: ssd_side(g - 1, u))

            def gate(s, d, pair, dst):
                act.wait_ge(unit_used, d + s)
                act.activation(dst[:], ps[:, pair:pair + 2, 0:SEQ], ACT.Sigmoid).then_inc(pair_free[pair], 1)

            k = G - 1
            for u in range(8):
                hi_of(U_M + u, 0)
                if u == 2:
                    silus(k)
                if u == 4:
                    decays(k, 0)
                    decays(k, 1)
                if u == 6:
                    b_keep(k)
                    st_keep(k)
            y_squares(k)
            gate(U_M + 4, 0, A, sgs)
            y_keep(k)
            for u in range(8, 12):
                hi_of(U_M + u, 0)
            gate(U_M + 8, 0, B, sga)
            act.drain()
            for i in range(12):
                act.activation(aH[:, 4 * i:4 * i + 4, :], acts[:, 4 * i:4 * i + 4, :], ACT.Copy).then_inc(ah_ready, 1)
            for u in range(12, M_UN):
                hi_of(U_M + u, 0)
            with act.Fori(1, M_IT) as m:
                for u in range(M_UN):
                    hi_of(U_M + u, m * M_UN)
                    if u == 6:
                        gate(U_M + 4, m * M_UN, A, sgs)
                    if u == 10:
                        gate(U_M + 8, m * M_UN, B, sga)

            for u in range(SLOTS):
                hi_of(U_O + u, 0)
            act.wait_ge(merged, M_IT)
            for i in range(4):
                act.activation(mH[:, 4 * i:4 * i + 4, :], mraw[:, 4 * i:4 * i + 4, :], ACT.Copy).then_inc(mh_ready, 1)

            def square_panel(pair, n, cols, j):
                act.wait_ge(pair_free[pair], n)
                for t in range(TT):
                    if t:
                        act.drain()
                    last = act.activation(sqo[:], h1[:, t, cols], ACT.Square, accum_out=ss[:, t, j:j + 1])
                return last

            for j in range(4):
                for u in range(8):
                    if 8 * j + u >= SLOTS:
                        hi_of(U_O + 8 * j + u, 0)
                    if u == 3 and j:
                        square_panel((A, B)[(j - 1) % 2], J_O + (j - 1) // 2 + 1, slice((j - 1) * W5, j * W5), j - 1)
            for u in range(SLOTS):
                hi_of(U_F + u, 0)
            square_panel(B, J_O + 2, slice(3 * W5, D), 3).then_inc(squares_done, 1)
            norm_hi("ffn_norm", KD)

            def gate_start(f):
                act.wait_ge(unit_used, f * F_UN + (U_F + 4))
                for i in range(2):
                    act.activation(gv[:, i, :], ps[:, A + i, 0:SEQ], ACT.Identity,
                                   scale=pcol("ffn_conv_w", f * (2 * FTAPS) + (i * FTAPS + FTAPS - 1)),
                                   bias=pcol("ffn_conv_b", f * 2 + i)).then_inc(fconv_first, 1)

            def gelu(f):
                act.wait_ge(pair_free[A], f + (J_F + 1))
                act.activation(gv[:], gv[:], ACT.Gelu).then_inc(gelu_ready, 1)

            def h_hi(f):
                act.wait_ge(pair_free[B], f + (J_F + 1))
                act.activation(hH[:, ds(f * 2, 2), :], ht[:], ACT.Copy).then_inc(hh_ready, 1)

            for u in range(F_UN):
                if u >= SLOTS:
                    hi_of(U_F + u, 0)
                if u == 6:
                    gate_start(0)
                if u == 7:
                    gelu(0)
            with act.Fori(1, F_IT) as f:
                for u in range(F_UN):
                    hi_of(U_F + u, f * F_UN)
                    if u == 3:
                        h_hi(f - 1)
                    if u == 6:
                        gate_start(f)
                    if u == 7:
                        gelu(f)

            for u in range(SLOTS):
                hi_of(U_E + u, 0)
            h_hi(F_IT - 1)

            half = E_UN // 2
            for e in range(E_IT):
                for u in range(E_UN):
                    if e or u >= SLOTS:
                        hi_of(U_E + e * E_UN + u, 0)
                    n = 2 * e + u // half
                    if u % half == 4 and n:
                        square_panel((A, B)[(n - 1) % 2], J_E + (n - 1) // 2 + 1, slice((n - 1) * W5, n * W5), n - 1)
            square_panel(B, J_E + 2, slice(3 * W5, D), 3).then_inc(squares_done, 1)

        @block.vector
        def _(ve):
            def lo_of(s, d):
                ve.wait_ge(hi_ready, d + (s + 1))
                ve.tensor_tensor(lo[:, s % SLOTS, :], raw[:, s % SLOTS, :], hi[:, s % SLOTS, :].bitcast(F32),
                                 ALU.subtract).then_inc(lo_ready, 1)

            ve.wait_ge(rstd_ready, 1)
            for t in range(TT):
                ve.wait_ge(x_landed[t], 16)
                ve.tensor_scalar(xn[:, t, :], x_tok[:, t, :], rstd[:, t:t + 1], None, ALU.mult).then_inc(xn_ready, 1)
            for u in range(SLOTS):
                lo_of(u, 0)

            def norm_lo(name, base):
                for k in range(KD):
                    ve.wait_ge(uh_ready, base + k + 1)
                    ve.scalar_tensor_tensor(out=uL[:, k, :], in0=ps[:, M + k % 4, 0:SEQ], scalar=pcol(name, k),
                                            in1=uH[:, k, :].bitcast(F32), op0=ALU.mult,
                                            op1=ALU.subtract).then_inc(u_ready, 1)

            norm_lo("attn_norm", 0)
            for u in range(4, 6):
                lo_of(u, 0)
            W = lambda i: dtw[:, i, :]
            ve.wait_ge(unit_used, U_KV)
            ve.tensor_scalar(W(0), ps[0:SH, A, 0:SEQ], par[0:SH, PC["dt_bias"]:PC["dt_bias"] + 1], None,
                             ALU.add).then_inc(pair_free[A], 1)
            ve.drain()
            ve.scalar_tensor_tensor(out=W(1), in0=W(0), scalar=-1.0, in1=W(0), op0=ALU.mult,
                                    op1=ALU.max).then_inc(dt_abs, 1)
            ve.tensor_scalar(W(2), W(0), 0.0, None, ALU.max)
            for u in range(6, 8):
                lo_of(u, 0)
            ve.wait_ge(dt_exp, 1)
            ve.tensor_scalar(W(3), W(1), 2.0, None, ALU.add)
            ve.drain()
            ve.reciprocal(W(4), W(3))
            ve.drain()
            ve.tensor_tensor(W(3), W(1), W(4), ALU.mult)
            ve.drain()
            ve.tensor_tensor(W(4), W(3), W(3), ALU.mult)
            ve.drain()
            ve.tensor_scalar(W(5), W(4), 1.0 / 17, None, ALU.mult)
            ve.drain()
            for n in (15, 13, 11, 9, 7, 5, 3):
                ve.scalar_tensor_tensor(out=W(5), in0=W(5), scalar=1.0 / n, in1=W(4), op0=ALU.add, op1=ALU.mult)
                ve.drain()
            ve.scalar_tensor_tensor(out=W(5), in0=W(5), scalar=1.0, in1=W(3), op0=ALU.add, op1=ALU.mult)
            ve.drain()
            ve.scalar_tensor_tensor(out=W(0), in0=W(5), scalar=2.0, in1=W(2), op0=ALU.mult, op1=ALU.add)
            ve.drain()
            ve.tensor_scalar(W(6), W(0), dtw[:, 7, 0:1], -1.0, ALU.mult, ALU.mult).then_inc(dt_done, 1)
            for u in range(8, 10):
                lo_of(u, 0)
            ve.wait_ge(consts_ready, 2)
            for u in range(Q_UN):
                lo_of(U_Q + u, 0)
                if u == 4:
                    ve.wait_ge(dt_turned, 1)
                    ve.tensor_copy(dtt[:].rearrange("p a c n -> p (a c n)"), ps[:, M, 0:2 * TT * SH]).then_inc(dtt_ready, 1)

            def att_logits(h, x):
                S = stat[:, x]
                ve.wait_ge(scores_done, h * 2 + (x + 1))
                for j in range(4):
                    last = ve.scalar_tensor_tensor(out=lg[:, x, j, :], in0=dist[:],
                                                   scalar=nslope[:, ds(h * HK + (4 * x + j), 1)],
                                                   in1=ps[:, M + j, 0:3 * P], op0=ALU.mult, op1=ALU.add)
                last.then_inc(logits_done, 1)
                ve.drain()
                mx = S[:, 0, :].rearrange("p (j b) -> p j b", b=2)
                ve.tensor_reduce(mx[:, :, 0:1], lg[:, x, :, 0:P], op=ALU.max, axis=AX.X)
                ve.tensor_reduce(mx[:, :, 1:2], lg[:, x, :, P:3 * P], op=ALU.max, axis=AX.X)
                ve.drain()
                sink = par[:, ds(h * HK + (PC["sinks"] + 4 * x), 4)][:, :, None].to_broadcast([P, 4, 2])
                ve.tensor_tensor(S[:, 4, :].rearrange("p (j b) -> p j b", b=2), mx, sink, ALU.max)
                ve.drain()
                ve.tensor_scalar(S[:, 1, :], S[:, 4, :], -1.0, None, ALU.mult)
                ve.tensor_tensor(S[:, 2, :].rearrange("p (j b) -> p j b", b=2), sink,
                                 S[:, 4, :].rearrange("p (j b) -> p j b", b=2), ALU.subtract).then_inc(max_ready, 1)

            def att_probs(h, x):
                S = stat[:, x]
                ve.wait_ge(exps_done, h * 2 + (x + 1))
                ve.tensor_tensor(S[:, 4, :], S[:, 3, :], S[:, 2, :], ALU.add)
                ve.drain()
                ve.reciprocal(S[:, 5, :], S[:, 4, :])
                ve.drain()
                r = S[:, 5, :].rearrange("p (j b) -> p j b", b=2)
                ve.tensor_tensor(lg[:, x, :, 0:P], lg[:, x, :, 0:P], r[:, :, 0:1].to_broadcast([P, 4, P]), ALU.mult)
                ve.tensor_tensor(lg[:, x, :, P:3 * P], lg[:, x, :, P:3 * P], r[:, :, 1:2].to_broadcast([P, 4, 2 * P]),
                                 ALU.mult).then_inc(probs_ready, 1)

            def att_side(h, u):
                if u == 2:
                    att_logits(h, 0)
                if u == 3:
                    att_logits(h, 1)
                if u == 5:
                    att_probs(h, 0)
                if u == 6:
                    att_probs(h, 1)

            with ve.Fori(1, Q_IT) as q:
                for u in range(Q_UN):
                    lo_of(U_Q + u, q * Q_UN)
                    att_side(q - 1, u)

            def conv_rest(n0, tiles, pair):
                ve.wait_ge(conv_first, n0 + 2)
                for tap in range(TAPS - 1):
                    sh = TAPS - 1 - tap
                    for i, (slot, ch) in enumerate(tiles):
                        last = ve.scalar_tensor_tensor(out=cv[:, slot, sh:SEQ], in0=ps[:, pair + i, 0:SEQ - sh],
                                                       scalar=pcol("conv_w", ch * TAPS + tap), in1=cv[:, slot, sh:SEQ],
                                                       op0=ALU.mult, op1=ALU.add)
                        if tap == TAPS - 2 and i == 1:
                            last.then_inc(pair_free[pair], 1)
                    ve.drain()

            def group(g, body):
                for u in range(G_UN):
                    lo_of(U_G + u, g * G_UN)
                    if u == 6:
                        conv_rest(g * 6, ((4, g + 32), (5, g + 40)), A)
                    if u == 10:
                        conv_rest(g * 6 + 2, ((0, g * 4), (1, g * 4 + 1)), B)
                    if u == 14:
                        conv_rest(g * 6 + 4, ((2, g * 4 + 2), (3, g * 4 + 3)), A)
                    body(u)

            def heads(t):
                return t.rearrange("p (h d) -> p h d", h=HG)

            def bc(t):
                return t[:, :, None].to_broadcast([P, HG, HD])

            def ssd_inputs(k):
                ve.wait_ge(btok_ready, k + 1)
                ve.tensor_tensor(cbm[:], ps[:, M, 0:2 * P].rearrange("p (c n) -> p c n", c=TT),
                                 triu[:, None, :].to_broadcast([P, TT, P]), ALU.mult)
                for c in range(TT):
                    ve.tensor_tensor(heads(xd[:, c, :]), heads(ps[:, M + 1 + c, :]), bc(dtt[:, 0, c, ds(k * HG, HG)]), ALU.mult)
                    ve.tensor_tensor(heads(xD[:, c, :]), heads(ps[:, M + 1 + c, :]),
                                     bc(par[:, ds(k * HG + PC["d_skip"], HG)]), ALU.mult)
                ve.drain()
                ve.tensor_tensor(heads(xds[:]), heads(xd[:, 0, :]), bc(edec[:, 1, ds(k * HG, HG)]), ALU.mult) \
                    .then_inc(xd_ready, 1)
                ve.wait_ge(decay_ready, k * 4 + 4)
                for c in range(TT):
                    last = ve.tensor_tensor(dec[:, c], dec[:, c], cbm[:, c, None, :].to_broadcast([P, HG, P]), ALU.mult)
                last.then_inc(g_ready, 1)

            def ssd_outputs(k):
                ve.wait_ge(y_done, k + 1)
                ve.tensor_tensor(heads(yoff[:]), heads(ps[:, M + 2, :]), bc(edec[:, 0, ds(k * HG, HG)]), ALU.mult)
                ve.tensor_tensor(y[:, 0, :], ps[:, M, :], xD[:, 0, :], ALU.add)
                ve.tensor_tensor(xD[:, 1, :], ps[:, M + 1, :], xD[:, 1, :], ALU.add)
                ve.drain()
                ve.tensor_tensor(y[:, 1, :], yoff[:], xD[:, 1, :], ALU.add)
                ve.drain()
                ve.tensor_tensor(y[:], y[:], szb[:], ALU.mult).then_inc(y_gated, 1)

            def ssd_scale(k):
                ve.wait_ge(y_rstd, k + 1)
                for c in range(TT):
                    last = ve.tensor_scalar(y[:, c, :], y[:, c, :], rstd[:, c:c + 1], None, ALU.mult)
                last.then_inc(yn_ready, 1)

            def ssd_side(k, u):
                if u == 8:
                    ssd_inputs(k)
                if u == 12:
                    ssd_outputs(k)
                if u == 16:
                    ssd_scale(k)

            group(0, lambda u: att_side(KVH - 1, u))
            with ve.Fori(1, G) as g:
                group(g, lambda u: ssd_side(g - 1, u))

            k = G - 1
            for u in range(8):
                lo_of(U_M + u, 0)
                if u == 5:
                    ssd_inputs(k)
            ssd_outputs(k)
            ssd_scale(k)
            for u in range(8, 12):
                lo_of(U_M + u, 0)
            for i in range(12):
                ve.wait_ge(ah_ready, i + 1)
                ve.tensor_tensor(aL[:, 4 * i:4 * i + 4, :], acts[:, 4 * i:4 * i + 4, :],
                                 aH[:, 4 * i:4 * i + 4, :].bitcast(F32), ALU.subtract).then_inc(al_ready, 1)

            def merge_ssm(m):
                ve.wait_ge(unit_used, m * M_UN + (U_M + 16))
                ve.tensor_tensor(mraw[:, ds(m * 2, 2), :], ps[:, A:A + 2, 0:SEQ], sgs[:], ALU.mult) \
                    .then_inc(pair_free[A], 1)

            def merge_attn(m):
                ve.wait_ge(unit_used, m * M_UN + (U_M + M_UN))
                ve.tensor_tensor(mtmp[:], ps[:, B:B + 2, 0:SEQ], sga[:], ALU.mult).then_inc(pair_free[B], 1)
                ve.drain()
                ve.tensor_tensor(mraw[:, ds(m * 2, 2), :], mraw[:, ds(m * 2, 2), :], mtmp[:], ALU.add) \
                    .then_inc(merged, 1)

            for u in range(12, M_UN):
                lo_of(U_M + u, 0)
                if u == 18:
                    merge_ssm(0)
            with ve.Fori(1, M_IT) as m:
                for u in range(M_UN):
                    lo_of(U_M + u, m * M_UN)
                    if u == 2:
                        merge_attn(m - 1)
                    if u == 18:
                        merge_ssm(m)

            for u in range(SLOTS - 1):
                lo_of(U_O + u, 0)
            merge_attn(M_IT - 1)
            lo_of(U_O + SLOTS - 1, 0)
            for i in range(4):
                ve.wait_ge(mh_ready, i + 1)
                ve.tensor_tensor(mL[:, 4 * i:4 * i + 4, :], mraw[:, 4 * i:4 * i + 4, :],
                                 mH[:, 4 * i:4 * i + 4, :].bitcast(F32), ALU.subtract).then_inc(ml_ready, 1)

            def add_panel(done, pair, cols):
                ve.wait_ge(unit_used, done)
                ve.tensor_tensor(h1[:, :, cols], h1[:, :, cols], ps[:, pair:pair + 2, :], ALU.add) \
                    .then_inc(pair_free[pair], 1)

            for j in range(4):
                for u in range(8):
                    if 8 * j + u >= SLOTS:
                        lo_of(U_O + 8 * j + u, 0)
                    if u == 2 and j:
                        if j == 1:
                            for t in range(TT):
                                ve.wait_ge(h1_landed[t], 16)
                        add_panel(U_O + 8 * j, (A, B)[(j - 1) % 2], slice((j - 1) * W5, j * W5))
            for u in range(SLOTS - 1):
                lo_of(U_F + u, 0)
            add_panel(U_F, B, slice(3 * W5, D))
            lo_of(U_F + SLOTS - 1, 0)

            ve.wait_ge(rstd_ready, 2)
            for t in range(TT):
                ve.tensor_scalar(xn2[:, t, :], h1[:, t, :], rstd[:, t:t + 1], None, ALU.mult).then_inc(xn_ready, 1)
            norm_lo("ffn_norm", KD)

            def gate_rest(f):
                ve.wait_ge(fconv_first, f * 2 + 2)
                for tap in range(FTAPS - 1):
                    sh = FTAPS - 1 - tap
                    for i in range(2):
                        last = ve.scalar_tensor_tensor(out=gv[:, i, sh:SEQ], in0=ps[:, A + i, 0:SEQ - sh],
                                                       scalar=pcol("ffn_conv_w", f * (2 * FTAPS) + (i * FTAPS + tap)),
                                                       in1=gv[:, i, sh:SEQ], op0=ALU.mult, op1=ALU.add)
                        if tap == FTAPS - 2 and i == 1:
                            last.then_inc(pair_free[A], 1)
                    ve.drain()

            def h_of(f):
                ve.wait_ge(unit_used, f * F_UN + (U_F + F_UN))
                ve.wait_ge(gelu_ready, f + 1)
                ve.tensor_tensor(ht[:], ps[:, B:B + 2, 0:SEQ], gv[:], ALU.mult).then_inc(pair_free[B], 1)

            def h_lo(f):
                ve.wait_ge(hh_ready, f + 1)
                ve.tensor_tensor(hL[:, ds(f * 2, 2), :], ht[:], hH[:, ds(f * 2, 2), :].bitcast(F32),
                                 ALU.subtract).then_inc(hl_ready, 1)

            for u in range(F_UN):
                if u >= SLOTS:
                    lo_of(U_F + u, 0)
                if u == 6:
                    gate_rest(0)
            with ve.Fori(1, F_IT) as f:
                for u in range(F_UN):
                    lo_of(U_F + u, f * F_UN)
                    if u == 2:
                        h_of(f - 1)
                    if u == 4:
                        h_lo(f - 1)
                    if u == 6:
                        gate_rest(f)

            for u in range(SLOTS - 1):
                lo_of(U_E + u, 0)
            h_of(F_IT - 1)
            lo_of(U_E + SLOTS - 1, 0)
            h_lo(F_IT - 1)

            half = E_UN // 2
            for e in range(E_IT):
                for u in range(E_UN):
                    if e or u >= SLOTS:
                        lo_of(U_E + e * E_UN + u, 0)
                    n = 2 * e + u // half
                    if u % half == 3 and n:
                        add_panel(U_E + half * n, (A, B)[(n - 1) % 2], slice((n - 1) * W5, n * W5))
            add_panel(UNITS, B, slice(3 * W5, D))

            ve.wait_ge(rstd_ready, 3)
            ve.wait_ge(fw_landed, 16)
            for t in range(TT):
                for j in range(2):
                    c = slice(j * (D // 2), (j + 1) * (D // 2))
                    ve.scalar_tensor_tensor(out=h1[:, t, c], in0=h1[:, t, c], scalar=rstd[:, t:t + 1], in1=fw[:, c],
                                            op0=ALU.mult, op1=ALU.mult).then_inc(y_final, 1)

        @block.tensor
        def _(pe):
            def passes(out, w, x, start, stop):
                pe.matmul(out, w[0], x[0], start=start, stop=False)
                pe.matmul(out, w[0], x[1], start=False, stop=False)
                return pe.matmul(out, w[1], x[0], start=False, stop=stop)

            def columns(s, d, pair, xs, k, kt0, kt, w=W2, avail=None):
                pe.wait_ge(lo_ready, d + (s + 1))
                sl = s % SLOTS
                v = [t[:, sl, :].rearrange("p (k n) -> p k n", n=w) for t in (hi, lo)]
                for i in range(kt):
                    kk = kt0 + i
                    if avail:
                        avail(kk)
                    for c in range(w // P):
                        last = passes(ps[:, pair + c, 0:SEQ], [t[:, i, c * P:(c + 1) * P] for t in v],
                                      [t[:, kk, :] for t in xs], kk == 0, kk == k - 1)
                last.then_inc(unit_used, 1)

            def rows(s, d, pair, xs, k, kt0):
                pe.wait_ge(lo_ready, d + (s + 1))
                sl = s % SLOTS
                v = [t[:, sl, :].rearrange("p (k n) -> p k n", n=W5) for t in (hi, lo)]
                for i in range(2):
                    kk = kt0 + i
                    for t in range(TT):
                        last = passes(ps[:, pair + t, :], [a[:, kk, t * P:(t + 1) * P] for a in xs],
                                      [w[:, i, :] for w in v], kk == 0, kk == k - 1)
                last.then_inc(unit_used, 1)

            def job(pair, n):
                pe.wait_ge(pair_free[pair], n)

            U = (uH, uL)

            def turn_norm(src, base):
                for k in range(KD):
                    if base + k >= 4:
                        pe.wait_ge(u_ready, base + k - 3)
                    for t in range(TT):
                        if k == 0:
                            pe.wait_ge(xn_ready, base // KD * TT + t + 1)
                        last = pe.transpose(ps[:, M + k % 4, t * P:(t + 1) * P], src[:, t, k * P:(k + 1) * P], ident[:])
                    last.then_inc(norm_turned, 1)

            pe.wait_ge(consts_ready, 1)
            turn_norm(xn, 0)
            for i in range(2):
                columns(U_DT + i, 0, A, U, KD, 8 * i, 8, w=P, avail=lambda kk: pe.wait_ge(u_ready, kk + 1))
            for i in range(8):
                rows(U_KV + i, 0, B, U, KD, 2 * i)

            def turn_dt():
                pe.wait_ge(dt_done, 1)
                for a, w in ((0, 0), (1, 6)):
                    for c in range(TT):
                        o = (a * TT + c) * SH
                        last = pe.transpose(ps[:, M, o:o + SH], dtw[:, w, c * P:(c + 1) * P], ident[0:SH, 0:SH])
                last.then_inc(dt_turned, 1)

            def turn_keys():
                pe.wait_ge(pair_free[B], 1)
                for h in range(KVH):
                    for t in range(TT):
                        o = (h % 2) * SEQ + t * P
                        src = ktok[:, t, h].rearrange("p a d -> p (a d)")
                        last = pe.transpose(ps[:, M + 2 + h // 2, o:o + P], src, ident[:])
                last.then_inc(k_turned, 1)

            def cumulate():
                pe.wait_ge(dtt_ready, 1)
                pe.matmul(ps[:, M + 1, 0:SH], triu[:], dtt[:, 1, 1, :], start=True, stop=True)
                pe.matmul(ps[:, M + 1, SH:2 * SH], strict[:], dtt[:, 1, 0, :], start=True, stop=True).then_inc(cum_done, 1)

            for u in range(Q_UN):
                if u % 4 == 0:
                    job((A, B)[u // 4], 1)
                columns(U_Q + u, 0, (A, B)[u // 4], U, KD, 4 * (u % 4), 4)
                if u == 0:
                    turn_dt()
                if u == 1:
                    turn_keys()
                if u == 5:
                    cumulate()

            def scores(h, x):
                pe.wait_ge(pair_free[(A, B)[x]], h + 2)
                if x == 0:
                    pe.wait_ge(kv_cur, h + 1)
                    pe.wait_ge(edec_ready, 1)
                else:
                    pe.wait_ge(logits_done, h * 2 + 1)
                for j in range(4):
                    r = slice((j % 2) * HD, (j % 2) * HD + HD)
                    q = qT[r, 2 * x + j // 2, :]
                    pe.matmul(ps[:, M + j, 0:P], q[:, 0:P], kcur[r, 0:P], start=True, stop=True)
                    last = pe.matmul(ps[:, M + j, P:3 * P], q[:, P:SEQ], kcur[r, :], start=True, stop=True)
                last.then_inc(scores_done, 1)

            def turn_probs(h, x, p):
                pe.wait_ge(probs_ready, h * 2 + (x + 1))
                if p == 0 and x == 0:
                    pe.wait_ge(logits_done, h * 2 + 2)
                else:
                    pe.wait_ge(pt_ready, h * 4 + (2 * x + p))
                for i in range(2):
                    for c in range(3):
                        last = pe.transpose(ps[:, M + i, c * P:(c + 1) * P], lg[:, x, 2 * p + i, c * P:(c + 1) * P], ident[:])
                last.then_inc(probs_turned, 1)

            def values(h, x, p):
                pe.wait_ge(pt_ready, h * 4 + (2 * x + p + 1))
                if x:
                    pe.wait_ge(attn_out, h * 4 + (p + 1))
                for i in range(2):
                    r = slice(i * HD, i * HD + HD)
                    pe.matmul(ps[r, M + 2 + p, 0:SEQ], vcur[:, 0, :], pT[:, p, i, 0:SEQ], start=True, stop=False)
                    last = pe.matmul(ps[r, M + 2 + p, P:SEQ], vcur[:, 1, :], pT[:, p, i, SEQ:3 * P], start=False, stop=True)
                last.then_inc(pv_done, 1)

            def att_before(h, u):
                if u == 0:
                    scores(h, 0)
                if u == 2:
                    scores(h, 1)
                if u == 4:
                    turn_probs(h, 0, 0)
                if u == 5:
                    turn_probs(h, 0, 1)
                    values(h, 0, 0)
                if u == 6:
                    turn_probs(h, 1, 0)
                    values(h, 0, 1)
                if u == 7:
                    turn_probs(h, 1, 1)
                    values(h, 1, 0)
                    values(h, 1, 1)

            with pe.Fori(1, Q_IT) as q:
                for u in range(Q_UN):
                    att_before(q - 1, u)
                    if u % 4 == 0:
                        job((A, B)[u // 4], q + 1)
                    columns(U_Q + u, q * Q_UN, (A, B)[u // 4], U, KD, 4 * (u % 4), 4)

            def seg(k, c):
                pe.wait_ge(adm_ready, k + 1)
                for b in range(2):
                    last = pe.matmul(ps[:, M + 2 * c + b, :], strict[:],
                                     adm[:, c, 4 * b:4 * b + 4, :].rearrange("p h n -> p (h n)"), start=True, stop=True)
                    last.then_inc(seg_done, 1)

            def turn_x(k):
                pe.wait_ge(sv_ready, k + 1)
                pe.wait_ge(decay_ready, k * 4 + 3)
                for c in range(TT):
                    pe.matmul(ps[:, M, c * P:(c + 1) * P], sv[:, 4, c * P:(c + 1) * P], sv[:, 5, c * P:(c + 1) * P],
                              start=True, stop=True)
                pe.transpose(ps[:, M, 2 * P:3 * P], sv[:, 4, 0:P], ident[:])
                for c in range(TT):
                    for i in range(4):
                        last = pe.transpose(ps[:, M + 1 + c, i * P:(i + 1) * P], sv[:, i, c * P:(c + 1) * P], ident[:])
                last.then_inc(cb_done, 1)

            def state(k):
                pe.wait_ge(btok_ready, k + 1)
                pe.wait_ge(xd_ready, k + 1)
                pe.wait_ge(decay_ready, k * 4 + 4)
                pe.matmul(ps[:, M + 3, :], btok[:], xds[:], start=True, stop=True).then_inc(state_done, 1)

            def y_of(k):
                pe.wait_ge(g_ready, k + 1)
                for c in range(TT):
                    for h in range(HG):
                        pe.matmul(ps[:, M + c, h * HD:(h + 1) * HD], dec[:, c, h, :], xd[:, c, h * HD:(h + 1) * HD],
                                  start=True, stop=True)
                pe.wait_ge(st_ready, k + 1)
                pe.matmul(ps[:, M + 2, :], sv[:, 5, P:SEQ], st[:], start=True, stop=True).then_inc(y_done, 1)

            def turn_y(k):
                pe.wait_ge(yn_ready, k + 1)
                for i in range(4):
                    for c in range(TT):
                        o = (i % 2) * SEQ + c * P
                        last = pe.transpose(ps[:, (M + 3, M)[i // 2], o:o + P], y[:, c, i * P:(i + 1) * P], ident[:])
                last.then_inc(y_turned, 1)

            def ssd_after(k, u, kept=True):
                if u == 1:
                    if kept:
                        pe.wait_ge(y_kept, k + 1)
                    seg(k, 0)
                if u == 2:
                    seg(k, 1)
                if u == 4:
                    turn_x(k)
                if u == 6:
                    state(k)
                if u == 8:
                    y_of(k)
                if u == 13:
                    turn_y(k)

            def group(g, before, after):
                for u in range(G_UN):
                    before(u)
                    if u == 0:
                        job(A, g * 2 + J_G)
                    if u == 4:
                        job(B, g * 2 + J_G)
                    if u == 8:
                        job(A, g * 2 + (J_G + 1))
                    if u == 12:
                        job(B, g * 2 + (J_G + 1))
                    if u < 4:
                        columns(U_G + u, g * G_UN, A + u // 2, U, KD, 8 * (u % 2), 8, w=P)
                    elif u < 12:
                        columns(U_G + u, g * G_UN, (A, B, A)[u // 4], U, KD, 4 * (u % 4), 4)
                    else:
                        rows(U_G + u, g * G_UN, B, U, KD, 2 * (u - 12))
                    after(u)

            group(0, lambda u: att_before(KVH - 1, u), lambda u: None)
            pe.wait_ge(attn_out, KVH * 4)
            pe.sem_inc(seg_done, 4)
            pe.sem_inc(y_kept, 1)
            with pe.Fori(1, G) as g:
                group(g, lambda u: None, lambda u: ssd_after(g - 1, u))

            k = G - 1
            AO = (aH, aL)
            for u in range(8):
                if u == 0:
                    job(A, J_M)
                if u == 4:
                    job(B, J_M)
                columns(U_M + u, 0, (A, B)[u // 4], U, KD, 4 * (u % 4), 4)
                if u == 1:
                    pe.wait_ge(y_kept, k + 1)
                    seg(k, 0)
                    seg(k, 1)
                if u == 3:
                    turn_x(k)
                if u == 5:
                    state(k)
                if u == 6:
                    y_of(k)
            turn_y(k)

            def branches(d, first):
                for u in range(8, M_UN):
                    if u == 8:
                        job(A, d[1] + (J_M + 1))
                    if u == 16:
                        job(B, d[1] + (J_M + 1))
                    if first:
                        pe.wait_ge(al_ready, u - 7)
                    ssm = u < 16
                    columns(U_M + u, d[0], (A, B)[not ssm], AO if ssm else (aH[:, 32:48, :], aL[:, 32:48, :]),
                            (32, 16)[not ssm], 4 * (u - 8 if ssm else u - 16), 4)

            branches((0, 0), True)
            with pe.Fori(1, M_IT) as m:
                for u in range(8):
                    if u % 4 == 0:
                        job((A, B)[u // 4], m * 2 + J_M)
                    columns(U_M + u, m * M_UN, (A, B)[u // 4], U, KD, 4 * (u % 4), 4)
                branches((m * M_UN, m * 2), False)

            for j in range(4):
                job((A, B)[j % 2], J_O + j // 2)
                for u in range(8):
                    if j == 0:
                        pe.wait_ge(ml_ready, u // 2 + 1)
                    rows(U_O + 8 * j + u, 0, (A, B)[j % 2], (mH, mL), KD, 2 * u)

            turn_norm(xn2, KD)
            for u in range(F_UN):
                if u % 4 == 0:
                    job((A, B)[u // 4], J_F)
                columns(U_F + u, 0, (A, B)[u // 4], U, KD, 4 * (u % 4), 4,
                        avail=(lambda kk: pe.wait_ge(u_ready, KD + kk + 1)) if u < 4 else None)
            with pe.Fori(1, F_IT) as f:
                for u in range(F_UN):
                    if u % 4 == 0:
                        job((A, B)[u // 4], f + J_F)
                    columns(U_F + u, f * F_UN, (A, B)[u // 4], U, KD, 4 * (u % 4), 4)

            half = E_UN // 2
            for n in range(4):
                job((A, B)[n % 2], J_E + n // 2)
                for u in range(half):
                    if n == 0 and u >= half - 1:
                        pe.wait_ge(hl_ready, F_IT)
                    elif n == 0 and u == 0:
                        pe.wait_ge(hl_ready, F_IT - 1)
                    rows(U_E + half * n + u, 0, (A, B)[n % 2], (hH, hL), KF, 2 * u)


def kernel(**inputs):
    import numpy as np
    import concourse.bacc as bacc
    from concourse.bass_utils import run_bass_kernel_spmd

    a = {n: np.ascontiguousarray(v) for n, v in inputs.items()}

    def channels(v, tiles):
        return v.reshape(tiles, P, -1).transpose(1, 0, 2).reshape(P, -1)

    def heads(v):
        return np.concatenate([v.reshape(SH, 1), np.zeros((P - SH, 1), np.float32)])

    params = np.ascontiguousarray(np.concatenate([
        channels(a["attn_norm_w"][0], KD), channels(a["ffn_norm_w"][0], KD),
        channels(a["ssm_conv_w"][0].T, 48), channels(a["ssm_conv_b"][0], 48),
        channels(a["ssm_norm_w"][0], DI // P), channels(a["ffn_conv_w"][0].T, KF), channels(a["ffn_conv_b"][0], KF),
        heads(a["dt_bias"][0]), heads(a["a_log"][0]),
        np.broadcast_to(a["d_skip"], (P, SH)), np.broadcast_to(a["attn_sinks"], (P, AH))], axis=1))
    feeds = {
        "x": a["x"].reshape(SEQ, D), "params": params, "w_in": a["w_in"][0], "w_ssm_out": a["w_ssm_out"][0],
        "w_attn_out": a["w_attn_out"][0], "w_o": a["w_o"][0], "w_ffn_in": a["w_ffn_in"][0],
        "w_ffn_out": a["w_ffn_out"][0], "final_norm_w": a["final_norm_w"].reshape(1, D),
    }
    nc = bacc.Bacc("TRN2", target_bir_lowering=False, num_devices=1)
    args = [nc.dram_tensor(n, v.shape, mybir.dt.from_np(v.dtype), kind="ExternalInput").ap() for n, v in feeds.items()]
    out = nc.dram_tensor("out", (SEQ, D), F32, kind="ExternalOutput").ap()
    build(nc, *args, out)
    r = run_bass_kernel_spmd(nc, [feeds], core_ids=[0])
    return r.results[0]["out"].reshape(1, SEQ, D)
```

```python
from contextlib import ExitStack

import concourse.bass as bass
from concourse import mybir

F32 = mybir.dt.float32
F32R = mybir.dt.float32r
ALU = mybir.AluOpType
ACT = mybir.ActivationFunctionType
AX = mybir.AxisListType
ds = bass.ds

P = 128
SEQ = 256
TT = SEQ // P
D = 2048
KD = D // P
DI = 4096
SH, HD = 64, 64
G, NS = 8, 128
HG = SH // G
GW = DI // G
AH, KVH = 32, 4
HK = AH // KVH
FF = 5632
TAPS, FTAPS = 4, 3
EPS = 1e-5
BIG = 3.0e38

C_Z = 0
C_X = C_Z + DI
C_B = C_X + DI
C_C = C_B + G * NS
C_DT = C_C + G * NS
C_Q = C_DT + SH
C_K = C_Q + AH * HD
C_GS = C_K + 2 * KVH * HD
C_GA = C_GS + D
IN_W = C_GA + D

SLOTS = 4
SLOT = 1024
W2 = 256
W5 = 512
U_DT = 0
U_KV = U_DT + 2
U_G, G_UN = U_KV + 8, 20
U_X, X_UN = U_G + G_UN * G, 16
U_Q, Q_UN = U_X + X_UN, 8
U_M, M_UN, M_IT = U_Q + Q_UN * (KVH - 1), 20, D // W2
U_O = U_M + M_UN * (M_IT - 1) + 12
U_F, F_UN, F_IT = U_O + 32, 8, FF // W2
U_E, E_UN, E_IT = U_F + F_UN * F_IT, 2 * (FF // P) // 2, 2
UNITS = U_E + E_UN * E_IT
KF = FF // P

J_G = 1
J_X = J_G + 2 * G
J_Q = J_X + 2
J_M = J_Q + KVH - 1
J_O = J_M + 2 * (M_IT - 1) + 1
J_F = J_O + 2
J_E = J_F + F_IT

PC = {}
_at = 0
for _n, _w in (("attn_norm", KD), ("ffn_norm", KD), ("conv_w", 48 * TAPS), ("conv_b", 48),
               ("ssm_norm", DI // P), ("ffn_conv_w", KF * FTAPS), ("ffn_conv_b", KF),
               ("dt_bias", 1), ("a_log", 1), ("d_skip", SH), ("sinks", AH)):
    PC[_n] = _at
    _at += _w
PW = _at


def build(nc, x, params, w_in, w_ssm, w_attn, w_o, w_fi, w_fo, fnorm, out):
    wv = {n: w.rearrange("(k p) n -> p k n", p=P)
          for n, w in (("in", w_in), ("ssm", w_ssm), ("attn", w_attn), ("o", w_o), ("fi", w_fi), ("fo", w_fo))}
    x_v = x.rearrange("(t p) d -> t p d", p=P)
    out_v = out.rearrange("(t p) d -> t p d", p=P)

    with ExitStack() as ctx:
        top = (nc.sbuf_base + 31) // 32 * 32
        end = nc.sbuf_usable_end

        def place(name, shape, at, dt=F32):
            size = 4
            for s in shape[1:]:
                size *= s
            assert at + size <= end, (name, at + size, end)
            return nc.alloc_sbuf_tensor_at(name, shape, dt, offset=at), (at + size + 31) // 32 * 32

        raw, top = place("raw", [P, SLOTS, SLOT], top)
        hi, top = place("hi", [P, SLOTS, SLOT], top, F32R)
        lo, top = place("lo", [P, SLOTS, SLOT], top, F32R)
        uH, top = place("uH", [P, KD, SEQ], top, F32R)
        uL, top = place("uL", [P, KD, SEQ], top, F32R)
        par, top = place("par", [P, PW], top)
        ident, top = place("ident", [P, P], top)
        neghalf, top = place("neghalf", [P, TT], top)
        inv_w, top = place("inv_w", [P, 2, TT], top)
        ss, top = place("ss", [P, TT, 4], top)
        ssp, top = place("ssp", [P, TT, 2], top)
        ssum, top = place("ssum", [P, TT], top)
        rstd, top = place("rstd", [P, TT], top)
        region = top

        KB, NA, NSM = 1024, 48, DI // P
        acts, _ = place("acts", [P, NA, SEQ], region)
        aL, _ = place("aL", [P, NA, SEQ], region, F32R)
        aHs, _ = place("aHs", [P, NSM, SEQ], region + 48 * KB, F32R)
        aHa, _ = place("aHa", [P, NA - NSM, SEQ], region + 80 * KB, F32R)
        mraw, _ = place("mraw", [P, KD, SEQ], region + 96 * KB)
        sgs, a = place("sgs", [P, 2, SEQ], region + 112 * KB)
        sga, a = place("sga", [P, 2, SEQ], a)
        mtmp, tail = place("mtmp", [P, 2, SEQ], a)
        x_tok, a = place("x_tok", [P, TT, D], region)
        xn, a = place("xn", [P, TT, D], a)
        lg, a = place("lg", [P, 4, 2, 3 * P], region + 80 * KB)
        kcur, a = place("kcur", [P, SEQ], a)
        vcur, a = place("vcur", [P, TT, HD], a)
        dist, a = place("dist", [P, 3 * P], a)
        nslope, a = place("nslope", [P, AH], a)
        stat, a = place("stat", [P, 4, 6, 4], a)
        assert a <= region + 96 * KB
        kdup, a = place("kdup", [P, KVH, SEQ], region + 96 * KB)
        vtok, a = place("vtok", [P, TT, KVH * HD], a)
        qT, a = place("qT", [P, 4, SEQ], a)
        pT, a = place("pT", [P, 2, 2 * 3 * P], a)
        assert a <= region + 112 * KB
        admH, a = place("admH", [P, TT, HG, P], region + 32 * KB, F32R)
        admL, a = place("admL", [P, TT, HG, P], a, F32R)
        assert a <= region + 48 * KB
        cv, a = place("cv", [P, 6, SEQ], region + 48 * KB)
        sv, a = place("sv", [P, 6, SEQ], a)
        dtw, _ = place("dtw", [SH, 8, SEQ], a)
        szb, a = place("szb", [P, TT, GW], a)
        dec, a = place("dec", [P, TT, HG, P], a)
        xd, a = place("xd", [P, TT, GW], a)
        xD, a = place("xD", [P, TT, GW], a)
        assert a <= region + 80 * KB
        y, a = place("y", [P, TT, GW], region + 80 * KB)
        yoff, a = place("yoff", [P, GW], a)
        xds, a = place("xds", [P, GW], a)
        st, a = place("st", [P, GW], a)
        cbm, a = place("cbm", [P, TT, P], a)
        btok, a = place("btok", [P, P], a)
        assert a <= region + 92 * KB
        ktok, a = place("ktok", [P, TT, KVH, 2, HD], region + 80 * KB)
        disti, _ = place("disti", [P, 3 * P], a, mybir.dt.int32)
        triu, a = place("triu", [P, P], tail)
        strict, a = place("strict", [P, P], a)
        strictR, a = place("strictR", [P, P], a, F32R)
        dtt, a = place("dtt", [P, 2, TT, SH], a)
        dttH, a = place("dttH", [P, TT, SH], a, F32R)
        dttL, a = place("dttL", [P, TT, SH], a, F32R)
        edec, a = place("edec", [P, 2, SH], a)
        mH, a = place("mH", [P, KD, SEQ], region, F32R)
        mL, a = place("mL", [P, KD, SEQ], a, F32R)
        hH, a = place("hH", [P, KF, SEQ], region, F32R)
        hL, a = place("hL", [P, KF, SEQ], a, F32R)
        xn2, _ = place("xn2", [P, TT, D], region)
        h1, a = place("h1", [P, TT, D], a)
        fw, a = place("fw", [P, D], a)
        gv, a = place("gv", [P, 2, SEQ], a)
        ht, a = place("ht", [P, 2, SEQ], a)
        sqo, a = place("sqo", [P, W5], a)

        ps = ctx.enter_context(nc.psum_tensor("ps", [P, 8, 512], F32))
        A, B, M = 0, 2, 4

        def sem(name):
            return ctx.enter_context(nc.semaphore(name))

        raw_landed = [sem(f"raw_landed{i}") for i in range(SLOTS)]
        hi_ready, lo_ready, unit_used = sem("hi_ready"), sem("lo_ready"), sem("unit_used")
        pair_free = {A: sem("pair_a_free"), B: sem("pair_b_free")}
        x_landed = [sem(f"x_landed{t}") for t in range(TT)]
        h1_landed = [sem(f"h1_landed{t}") for t in range(TT)]
        par_landed, fw_landed = sem("par_landed"), sem("fw_landed")
        consts_ready, squares_done, rstd_ready = sem("consts_ready"), sem("squares_done"), sem("rstd_ready")
        xn_ready, norm_turned, uh_ready, u_ready = sem("xn_ready"), sem("norm_turned"), sem("uh_ready"), sem("u_ready")
        dt_abs, dt_exp, dt_done, dt_turned, dtt_ready = (sem("dt_abs"), sem("dt_exp"), sem("dt_done"),
                                                         sem("dt_turned"), sem("dtt_ready"))
        cum_done, edec_ready = sem("cum_done"), sem("edec_ready")
        k_turned, kdup_ready, k_cur, v_cur = sem("k_turned"), sem("kdup_ready"), sem("k_cur"), sem("v_cur")
        scores_done, logits_done, max_ready = sem("scores_done"), sem("logits_done"), sem("max_ready")
        exps_done, probs_ready, probs_turned, pt_ready = (sem("exps_done"), sem("probs_ready"),
                                                          sem("probs_turned"), sem("pt_ready"))
        pv_done, attn_out = sem("pv_done"), sem("attn_out")
        split_ready, conv_first, sv_ready = sem("dta_split_ready"), sem("conv_first"), sem("sv_ready")
        adm_ready, seg_done, decay_ready = sem("adm_ready"), sem("seg_done"), sem("decay_ready")
        cb_done, btok_ready, xd_ready, g_ready = sem("cb_done"), sem("btok_ready"), sem("xd_ready"), sem("g_ready")
        state_done, st_ready, y_done, y_gated = sem("state_done"), sem("st_ready"), sem("y_done"), sem("y_gated")
        y_squared, y_rstd, yn_ready, y_turned, y_kept = (sem("y_squared"), sem("y_rstd"), sem("yn_ready"),
                                                         sem("y_turned"), sem("y_kept"))
        ah_ready, al_ready = sem("ah_ready"), sem("al_ready")
        merged, mh_ready, ml_ready = sem("merged"), sem("mh_ready"), sem("ml_ready")
        fconv_first, gelu_ready, hh_ready, hl_ready = (
            sem("fconv_first"), sem("gelu_ready"), sem("hh_ready"), sem("hl_ready"))
        y_final, out_written = sem("y_final"), sem("out_written")

        def pcol(name, i=0, n=1):
            return par[:, ds(i + PC[name], n)]

        block = ctx.enter_context(nc.Block())

        @block.sync
        def _(sp):
            for t in range(TT):
                sp.dma_start(x_tok[:, t, :], x_v[t]).then_inc(x_landed[t], 16)
            sp.dma_start(par[:], params).then_inc(par_landed, 16)

            def load(s, d, src, kt, w):
                if s >= SLOTS:
                    sp.wait_ge(lo_ready, d + (s - SLOTS + 1))
                dst = raw[:, s % SLOTS, 0:kt * w].rearrange("p (k n) -> p k n", k=kt)
                return sp.dma_start(dst, src)

            def stream(s, d, name, k0, kt, c, w):
                load(s, d, wv[name][:, k0:k0 + kt, ds(c, w)], kt, w).then_inc(raw_landed[s % SLOTS], 16)

            def columns(s, d, name, c, k):
                for i in range(k // 4):
                    stream(s + i, d, name, 4 * i, 4, c, W2)

            def rows(s, d, name, c, k):
                for i in range(k // 2):
                    stream(s + i, d, name, 2 * i, 2, c, W5)

            for i in range(2):
                stream(U_DT + i, 0, "in", 8 * i, 8, C_DT, P)
            rows(U_KV, 0, "in", C_K, KD)
            with sp.Fori(1, G + 1) as g1:
                d = (g1 - 1) * G_UN
                for i in range(4):
                    stream(U_G + i, d, "in", 8 * (i % 2), 8, g1 * NS + ((C_B, C_C)[i // 2] - NS), P)
                columns(U_G + 4, d, "in", g1 * GW + (C_X - GW), KD)
                columns(U_G + 8, d, "in", g1 * GW + (C_X - GW + W2), KD)
                rows(U_G + 12, d, "in", g1 * GW + (C_Z - GW), KD)
            columns(U_X, 0, "in", C_Q, KD)
            columns(U_X + 4, 0, "in", C_Q + W2, KD)
            columns(U_X + 8, 0, "in", C_GS, KD)
            columns(U_X + 12, 0, "in", C_GA, KD)
            with sp.Fori(1, KVH) as q:
                for j in range(2):
                    columns(U_Q + 4 * j, (q - 1) * Q_UN, "in", q * (2 * W2) + (C_Q + j * W2), KD)
            with sp.Fori(1, M_IT) as m1:
                d = (m1 - 1) * M_UN
                columns(U_M, d, "ssm", m1 * W2 - W2, DI // P)
                columns(U_M + 8, d, "in", m1 * W2 + C_GS, KD)
                columns(U_M + 12, d, "attn", m1 * W2 - W2, KD)
                columns(U_M + 16, d, "in", m1 * W2 + C_GA, KD)
            last = U_M + (M_IT - 1) * M_UN
            columns(last, 0, "ssm", D - W2, DI // P)
            columns(last + 8, 0, "attn", D - W2, KD)
            rows(U_O, 0, "o", 0, KD)
            sp.wait_ge(ml_ready, 4)
            for t in range(TT):
                sp.dma_start(h1[:, t, :], x_v[t]).then_inc(h1_landed[t], 16)
            for j in range(1, 4):
                rows(U_O + 8 * j, 0, "o", j * W5, KD)
            sp.dma_start(fw[:], fnorm.to_broadcast([P, D])).then_inc(fw_landed, 16)
            with sp.Fori(0, F_IT) as f:
                d = f * F_UN
                columns(U_F, d, "fi", f * W2, KD)
                columns(U_F + 4, d, "fi", f * W2 + FF, KD)
            with sp.Fori(0, E_IT) as e:
                for j in range(2):
                    rows(U_E + (KF // 2) * j, e * E_UN, "fo", e * (2 * W5) + j * W5, KF)
            for t in range(TT):
                for j in range(2):
                    sp.wait_ge(y_final, 2 * t + j + 1)
                    sp.dma_start(out_v[t][:, j * (D // 2):(j + 1) * (D // 2)],
                                 h1[:, t, j * (D // 2):(j + 1) * (D // 2)]).then_inc(out_written, 16)
            sp.wait_ge(out_written, 16 * 2 * TT)

        @block.gpsimd
        def _(po):
            po.memset(neghalf[:], -0.5)
            po.memset(inv_w[:, 0, :], 1.0 / D)
            po.memset(inv_w[:, 1, :], 1.0 / GW)
            po.memset(ident[:], 0.0)
            po.memset(triu[:], 1.0)
            po.memset(strict[:], 1.0)
            for h in range(AH):
                po.memset(nslope[:, h:h + 1], -2.0 ** (-8.0 / AH * (h + 1)))
            po.iota(disti[:, 0:P], [[-1, P]], base=0, channel_multiplier=1)
            po.iota(disti[:, P:3 * P], [[-1, 2 * P]], base=P, channel_multiplier=1)
            po.drain()
            po.affine_select(out=ident[:], in_=ident[:], compare_op=ALU.not_equal, fill=1.0,
                             base=0, pattern=[[-1, P]], channel_multiplier=1)
            po.drain()
            po.memset(rstd[:], 0.0).then_inc(consts_ready, 1)
            po.affine_select(out=triu[:], in_=triu[:], compare_op=ALU.is_ge, fill=0.0,
                             base=0, pattern=[[1, P]], channel_multiplier=-1)
            po.affine_select(out=strict[:], in_=strict[:], compare_op=ALU.is_ge, fill=0.0,
                             base=-1, pattern=[[-1, P]], channel_multiplier=1)
            po.tensor_copy(dist[:], disti[:])
            po.drain()
            po.tensor_copy(strictR[:], strict[:])
            po.drain()
            po.affine_select(out=dist[:, 0:P], in_=dist[:, 0:P], compare_op=ALU.is_ge, fill=BIG,
                             base=0, pattern=[[-1, P]], channel_multiplier=1)
            po.affine_select(out=dist[:, P:3 * P], in_=dist[:, P:3 * P], compare_op=ALU.is_ge, fill=BIG,
                             base=P, pattern=[[-1, 2 * P]], channel_multiplier=1)
            po.drain()
            po.affine_select(out=dist[:, P:3 * P], in_=dist[:, P:3 * P], compare_op=ALU.is_ge, fill=BIG,
                             base=-1, pattern=[[1, 2 * P]], channel_multiplier=-1).then_inc(consts_ready, 1)

            def root(width, count):
                po.tensor_tensor(ssum[:], ssum[:], inv_w[:, 0 if width == D else 1, :], ALU.mult)
                po.drain()
                po.tensor_scalar(ssum[:], ssum[:], EPS, None, ALU.add)
                po.drain()
                po.tensor_tensor(rstd[:], ssum[:], neghalf[:], ALU.pow).then_inc(count, 1)

            po.wait_ge(squares_done, TT)
            root(D, rstd_ready)

            po.wait_ge(split_ready, 1)
            with po.Fori(0, G) as g:
                po.wait_ge(seg_done, g * 2 + 2)
                for parts, adm in ((dttH, admH), (dttL, admL)):
                    for c in range(TT):
                        last = po.tensor_tensor(adm[:, c], parts[:, c, ds(g * HG, HG)].bitcast(F32)[:, :, None].to_broadcast([P, HG, P]),
                                                triu[:, None, :].to_broadcast([P, HG, P]), ALU.mult)
                last.then_inc(adm_ready, 1)
                po.wait_ge(y_squared, g + 1)
                root(GW, y_rstd)

            def k_static(h):
                po.tensor_copy(kcur[:], kdup[:, ds(h, 1), :].rearrange("p a n -> p (a n)")).then_inc(k_cur, 1)

            def v_static(h):
                po.tensor_copy(vcur[:], vtok[:, :, ds(h * HD, HD)]).then_inc(v_cur, 1)

            po.wait_ge(kdup_ready, 1)
            k_static(0)
            v_static(0)
            with po.Fori(1, KVH) as h:
                po.wait_ge(scores_done, h * 4)
                k_static(h)
                po.wait_ge(pv_done, h * 4)
                v_static(h)
            for n in range(2):
                po.wait_ge(squares_done, TT + 1 + n)
                po.tensor_tensor(ssp[:], ss[:, :, 0:2], ss[:, :, 2:4], ALU.add)
                po.drain()
                po.tensor_tensor(ssum[:], ssp[:, :, 0], ssp[:, :, 1], ALU.add)
                po.drain()
                root(D, rstd_ready)

        @block.scalar
        def _(act):
            def hi_of(s, d):
                act.wait_ge(raw_landed[s % SLOTS], d * 4 + 16 * (s // SLOTS + 1))
                if s >= SLOTS:
                    act.wait_ge(unit_used, d + (s - SLOTS + 1))
                act.activation(hi[:, s % SLOTS, :], raw[:, s % SLOTS, :], ACT.Copy).then_inc(hi_ready, 1)

            act.wait_ge(par_landed, 16)
            for t in range(TT):
                act.wait_ge(x_landed[t], 16)
                act.activation(xn[:, t, :], x_tok[:, t, :], ACT.Square, accum_out=ssum[:, t:t + 1]) \
                    .then_inc(squares_done, 1)
            for u in range(SLOTS):
                hi_of(u, 0)

            def norm_hi(name, base):
                for k in range(KD):
                    act.wait_ge(norm_turned, base + k + 1)
                    act.activation(uH[:, k, :], ps[:, M + k % 4, 0:SEQ], ACT.Identity,
                                   scale=pcol(name, k)).then_inc(uh_ready, 1)

            norm_hi("attn_norm", 0)
            for u in range(4, 8):
                hi_of(u, 0)
            act.wait_ge(dt_abs, 1)
            act.activation(dtw[:, 1, :], dtw[:, 1, :], ACT.Exp, scale=-1.0)
            act.activation(dtw[:, 7, 0:1], par[0:SH, PC["a_log"]:PC["a_log"] + 1], ACT.Exp).then_inc(dt_exp, 1)
            for u in range(8, 10):
                hi_of(u, 0)

            def q_keep(s, d, j, pair):
                act.wait_ge(unit_used, d + s)
                act.activation(qT[:, 2 * j:2 * j + 2, :], ps[:, pair:pair + 2, 0:SEQ], ACT.Copy,
                               scale=HD ** -0.5).then_inc(pair_free[pair], 1)

            def att_exps(h, i):
                act.wait_ge(max_ready, h * 4 + (i + 1))
                S = stat[:, i]
                for j in range(2):
                    act.activation(lg[:, i, j, 0:P], lg[:, i, j, 0:P], ACT.Exp, bias=S[:, 1, 2 * j:2 * j + 1],
                                   accum_out=S[:, 3, 2 * j:2 * j + 1])
                    act.activation(lg[:, i, j, P:3 * P], lg[:, i, j, P:3 * P], ACT.Exp, bias=S[:, 1, 2 * j + 1:2 * j + 2],
                                   accum_out=S[:, 3, 2 * j + 1:2 * j + 2])
                act.activation(S[:, 2, :], S[:, 2, :], ACT.Exp).then_inc(exps_done, 1)

            def att_turned(h, i):
                act.wait_ge(probs_turned, h * 4 + (i + 1))
                act.activation(pT[:, i % 2], ps[:, M + 2:M + 4, :].rearrange("p b n -> p (b n)")[:, 0:6 * P],
                               ACT.Copy).then_inc(pt_ready, 1)

            def att_keep(h, i):
                act.wait_ge(pv_done, h * 4 + (i + 1))
                act.activation(acts[:, ds(h * 4 + (NSM + i), 1), :].rearrange("p a n -> p (a n)"),
                               ps[:, M + 3, SEQ:2 * SEQ], ACT.Copy).then_inc(attn_out, 1)

            def att_side(h, u, older=True, newer=True):
                if u == 1 and older:
                    att_keep(h - 1, 1)
                    att_turned(h - 1, 2)
                    att_exps(h - 1, 3)
                if u == 3:
                    if older:
                        att_keep(h - 1, 2)
                        att_turned(h - 1, 3)
                    if newer:
                        att_exps(h, 0)
                if u == 5:
                    if older:
                        att_keep(h - 1, 3)
                    if newer:
                        att_turned(h, 0)
                        att_exps(h, 1)
                if u == 7 and newer:
                    att_keep(h, 0)
                    att_turned(h, 1)
                    att_exps(h, 2)

            def conv_start(base, tiles, pair, done):
                act.wait_ge(unit_used, done)
                for i, (slot, ch) in enumerate(tiles):
                    act.activation(cv[:, slot, :], ps[:, pair + i, 0:SEQ], ACT.Identity,
                                   scale=pcol("conv_w", ch * TAPS + (TAPS - 1)), bias=pcol("conv_b", ch)) \
                        .then_inc(conv_first, 1)

            def silus(k):
                act.wait_ge(unit_used, k * G_UN + (U_G + G_UN))
                act.activation(szb[:], ps[:, B:B + 2, :], ACT.Silu).then_inc(pair_free[B], 1)
                act.wait_ge(pair_free[A], k * 2 + (J_G + 2))
                act.activation(sv[:].rearrange("p a n -> p (a n)"), cv[:].rearrange("p a n -> p (a n)"),
                               ACT.Silu).then_inc(sv_ready, 1)

            def decays(k, c):
                act.wait_ge(seg_done, k * 2 + (2 + c + 1))
                for b in range(2):
                    act.activation(dec[:, c, 4 * b:4 * b + 4, :].rearrange("p h n -> p (h n)"),
                                   ps[:, M + 2 * c + b, :], ACT.Exp).then_inc(decay_ready, 1)

            def b_keep(k):
                act.wait_ge(cb_done, k + 1)
                act.activation(btok[:], ps[:, M, 2 * P:3 * P], ACT.Copy).then_inc(btok_ready, 1)

            def st_keep(k):
                act.wait_ge(state_done, k + 1)
                act.activation(st[:], ps[:, M + 3, :], ACT.Copy).then_inc(st_ready, 1)

            def y_squares(k):
                act.wait_ge(y_gated, k + 1)
                for c in range(TT):
                    if c:
                        act.drain()
                    last = act.activation(yoff[:], y[:, c, :], ACT.Square, accum_out=ssum[:, c:c + 1])
                last.then_inc(y_squared, 1)

            def y_keep(k):
                act.wait_ge(y_turned, k + 1)
                for i in range(4):
                    last = act.activation(acts[:, ds(k * 4 + i, 1), :].rearrange("p a n -> p (a n)"),
                                          ps[:, M + 2 + i // 2, (i % 2) * SEQ:(i % 2 + 1) * SEQ], ACT.Identity,
                                          scale=pcol("ssm_norm", k * 4 + i))
                last.then_inc(y_kept, 1)

            def group(g, body):
                for u in range(G_UN):
                    hi_of(U_G + u, g * G_UN)
                    if u == 6:
                        conv_start(0, ((4, g + 32), (5, g + 40)), A, g * G_UN + (U_G + 4))
                    if u == 10:
                        conv_start(0, ((0, g * 4), (1, g * 4 + 1)), B, g * G_UN + (U_G + 8))
                    if u == 14:
                        conv_start(0, ((2, g * 4 + 2), (3, g * 4 + 3)), A, g * G_UN + (U_G + 12))
                    body(u)

            def ssd_side(k, u):
                if u == 2:
                    silus(k)
                if u == 5:
                    decays(k, 0)
                if u == 6:
                    decays(k, 1)
                if u == 8:
                    b_keep(k)
                if u == 11:
                    st_keep(k)
                if u == 14:
                    y_squares(k)
                if u == 19:
                    y_keep(k)

            def keys_side(u):
                if u == 2:
                    act.wait_ge(unit_used, U_G)
                    for i in range(2):
                        act.activation(ktok[:, :, :, i, :],
                                       ps[:, B:B + 2, 0:KVH * HD].rearrange("p t (h d) -> p t h d", h=KVH), ACT.Copy)
                    act.activation(vtok[:], ps[:, B:B + 2, KVH * HD:2 * KVH * HD], ACT.Copy).then_inc(pair_free[B], 1)
                if u == 5:
                    act.wait_ge(k_turned, 1)
                    act.activation(kdup[:].rearrange("p (a h) n -> p a (h n)", a=2), ps[:, M + 2:M + 4, :],
                                   ACT.Copy).then_inc(kdup_ready, 1)
                if u == 9:
                    act.wait_ge(cum_done, 1)
                    act.activation(edec[:].rearrange("p a n -> p (a n)"), ps[:, M + 1, 0:2 * SH],
                                   ACT.Exp).then_inc(edec_ready, 1)

            group(0, keys_side)
            with act.Fori(1, G) as g:
                group(g, lambda u: ssd_side(g - 1, u))

            def gate(done, pair, dst, used=None):
                act.wait_ge(unit_used, done)
                if used is not None:
                    act.wait_ge(pair_free[A], used)
                act.activation(dst[:], ps[:, pair:pair + 2, 0:SEQ], ACT.Sigmoid).then_inc(pair_free[pair], 1)

            for u in range(X_UN):
                hi_of(U_X + u, 0)
                ssd_side(G - 1, u)
                if u == 6:
                    q_keep(U_X + 4, 0, 0, A)
                if u == 10:
                    q_keep(U_X + 8, 0, 1, B)
                if u == 15:
                    gate(U_X + 12, A, sgs)

            def q_block(h, body):
                for u in range(Q_UN):
                    hi_of(U_Q + u, h * Q_UN)
                    if u == 6:
                        act.wait_ge(scores_done, h * 4 + 2)
                        q_keep(U_Q + 4, h * Q_UN, 0, A)
                    body(u)

            def q_rest(h, u):
                if u == 2:
                    act.wait_ge(scores_done, h * 4)
                    q_keep(U_Q, h * Q_UN, 1, B)

            def first_head(u):
                if u == 2:
                    y_keep(G - 1)
                    gate(U_Q, B, sga)
                att_side(0, u, older=False)

            q_block(0, first_head)

            def later_head(h, u):
                q_rest(h, u)
                att_side(h, u)
                if u % 2 == 0:
                    c = ds(h * 16 + (2 * u - 16), 4)
                    act.activation(aHs[:, c, :], acts[:, c, :], ACT.Copy).then_inc(ah_ready, 1)

            with act.Fori(1, KVH - 1) as h:
                q_block(h, lambda u: later_head(h, u))

            def merge_gates(m, u):
                if u == 14:
                    gate(m * M_UN + (U_M + 12), B, sgs, m * 2 + (J_M + 1))

            def merge_gate_rest(m, u):
                if u == 2:
                    gate(m * M_UN + U_M, B, sga, m * 2 + J_M)

            def attn_hi(i):
                act.activation(aHa[:, 4 * i:4 * i + 4, :], acts[:, NSM + 4 * i:NSM + 4 * i + 4, :],
                               ACT.Copy).then_inc(ah_ready, 1)

            for u in range(M_UN):
                hi_of(U_M + u, 0)
                if u < 8:
                    q_rest(KVH - 1, u)
                    att_side(KVH - 1, u)
                elif u < 11:
                    att_side(KVH, u - 8, newer=False)
                    if u > 8:
                        attn_hi(u - 9)
                elif u == 11:
                    att_keep(KVH - 1, 2)
                    att_turned(KVH - 1, 3)
                    att_keep(KVH - 1, 3)
                elif u < 14:
                    act.drain()
                    attn_hi(u - 10)
                merge_gates(0, u)
            with act.Fori(1, M_IT - 1) as m:
                for u in range(M_UN):
                    hi_of(U_M + u, m * M_UN)
                    merge_gate_rest(m, u)
                    merge_gates(m, u)
            m = M_IT - 1
            for u in range(12):
                hi_of(U_M + m * M_UN + u, 0)
                merge_gate_rest(m, u)

            def merged_hi(i):
                act.activation(mH[:, 4 * i:4 * i + 4, :], mraw[:, 4 * i:4 * i + 4, :], ACT.Copy).then_inc(mh_ready, 1)

            act.wait_ge(merged, M_IT - 1)
            act.wait_ge(unit_used, U_O - 4)
            for i in range(3):
                merged_hi(i)
            for u in range(SLOTS):
                hi_of(U_O + u, 0)
            act.wait_ge(merged, M_IT)
            merged_hi(3)

            def square_panel(pair, n, cols, j):
                act.wait_ge(pair_free[pair], n)
                for t in range(TT):
                    if t:
                        act.drain()
                    last = act.activation(sqo[:], h1[:, t, cols], ACT.Square, accum_out=ss[:, t, j:j + 1])
                return last

            for j in range(4):
                for u in range(8):
                    if 8 * j + u >= SLOTS:
                        hi_of(U_O + 8 * j + u, 0)
                    if u == 3 and j:
                        square_panel((A, B)[(j - 1) % 2], J_O + (j - 1) // 2 + 1, slice((j - 1) * W5, j * W5), j - 1)
            for u in range(SLOTS):
                hi_of(U_F + u, 0)
            square_panel(B, J_O + 2, slice(3 * W5, D), 3).then_inc(squares_done, 1)
            norm_hi("ffn_norm", KD)

            def gate_start(f):
                act.wait_ge(unit_used, f * F_UN + (U_F + 4))
                for i in range(2):
                    act.activation(gv[:, i, :], ps[:, A + i, 0:SEQ], ACT.Identity,
                                   scale=pcol("ffn_conv_w", f * (2 * FTAPS) + (i * FTAPS + FTAPS - 1)),
                                   bias=pcol("ffn_conv_b", f * 2 + i)).then_inc(fconv_first, 1)

            def gelu(f):
                act.wait_ge(pair_free[A], f + (J_F + 1))
                act.activation(gv[:], gv[:], ACT.Gelu).then_inc(gelu_ready, 1)

            def h_hi(f):
                act.wait_ge(pair_free[B], f + (J_F + 1))
                act.activation(hH[:, ds(f * 2, 2), :], ht[:], ACT.Copy).then_inc(hh_ready, 1)

            for u in range(F_UN):
                if u >= SLOTS:
                    hi_of(U_F + u, 0)
                if u == 6:
                    gate_start(0)
                if u == 7:
                    gelu(0)
            with act.Fori(1, F_IT) as f:
                for u in range(F_UN):
                    hi_of(U_F + u, f * F_UN)
                    if u == 3:
                        h_hi(f - 1)
                    if u == 6:
                        gate_start(f)
                    if u == 7:
                        gelu(f)

            for u in range(SLOTS):
                hi_of(U_E + u, 0)
            h_hi(F_IT - 1)

            half = E_UN // 2
            for e in range(E_IT):
                for u in range(E_UN):
                    if e or u >= SLOTS:
                        hi_of(U_E + e * E_UN + u, 0)
                    n = 2 * e + u // half
                    if u % half == 4 and n:
                        square_panel((A, B)[(n - 1) % 2], J_E + (n - 1) // 2 + 1, slice((n - 1) * W5, n * W5), n - 1)
            square_panel(B, J_E + 2, slice(3 * W5, D), 3).then_inc(squares_done, 1)

        @block.vector
        def _(ve):
            def lo_of(s, d):
                ve.wait_ge(hi_ready, d + (s + 1))
                ve.tensor_tensor(lo[:, s % SLOTS, :], raw[:, s % SLOTS, :], hi[:, s % SLOTS, :].bitcast(F32),
                                 ALU.subtract).then_inc(lo_ready, 1)

            ve.wait_ge(rstd_ready, 1)
            for t in range(TT):
                ve.wait_ge(x_landed[t], 16)
                ve.tensor_scalar(xn[:, t, :], x_tok[:, t, :], rstd[:, t:t + 1], None, ALU.mult).then_inc(xn_ready, 1)
            for u in range(SLOTS):
                lo_of(u, 0)

            def norm_lo(name, base):
                for k in range(KD):
                    ve.wait_ge(uh_ready, base + k + 1)
                    ve.scalar_tensor_tensor(out=uL[:, k, :], in0=ps[:, M + k % 4, 0:SEQ], scalar=pcol(name, k),
                                            in1=uH[:, k, :].bitcast(F32), op0=ALU.mult,
                                            op1=ALU.subtract).then_inc(u_ready, 1)

            norm_lo("attn_norm", 0)
            for u in range(4, 6):
                lo_of(u, 0)
            W = lambda i: dtw[:, i, :]
            ve.wait_ge(unit_used, U_KV)
            ve.tensor_scalar(W(0), ps[0:SH, A, 0:SEQ], par[0:SH, PC["dt_bias"]:PC["dt_bias"] + 1], None,
                             ALU.add).then_inc(pair_free[A], 1)
            ve.drain()
            ve.scalar_tensor_tensor(out=W(1), in0=W(0), scalar=-1.0, in1=W(0), op0=ALU.mult,
                                    op1=ALU.max).then_inc(dt_abs, 1)
            ve.tensor_scalar(W(2), W(0), 0.0, None, ALU.max)
            for u in range(6, 8):
                lo_of(u, 0)
            ve.wait_ge(dt_exp, 1)
            ve.tensor_scalar(W(3), W(1), 2.0, None, ALU.add)
            ve.drain()
            ve.reciprocal(W(4), W(3))
            ve.drain()
            ve.tensor_tensor(W(3), W(1), W(4), ALU.mult)
            ve.drain()
            ve.tensor_tensor(W(4), W(3), W(3), ALU.mult)
            ve.drain()
            ve.tensor_scalar(W(5), W(4), 1.0 / 17, None, ALU.mult)
            ve.drain()
            for n in (15, 13, 11, 9, 7, 5, 3):
                ve.scalar_tensor_tensor(out=W(5), in0=W(5), scalar=1.0 / n, in1=W(4), op0=ALU.add, op1=ALU.mult)
                ve.drain()
            ve.scalar_tensor_tensor(out=W(5), in0=W(5), scalar=1.0, in1=W(3), op0=ALU.add, op1=ALU.mult)
            ve.drain()
            ve.scalar_tensor_tensor(out=W(0), in0=W(5), scalar=2.0, in1=W(2), op0=ALU.mult, op1=ALU.add)
            ve.drain()
            ve.tensor_scalar(W(6), W(0), dtw[:, 7, 0:1], -1.0, ALU.mult, ALU.mult).then_inc(dt_done, 1)
            for u in range(8, 10):
                lo_of(u, 0)
            ve.wait_ge(consts_ready, 2)

            def keys_side(u):
                if u == 4:
                    ve.wait_ge(dt_turned, 1)
                    ve.tensor_copy(dtt[:].rearrange("p a c n -> p (a c n)"), ps[:, M, 0:2 * TT * SH]).then_inc(dtt_ready, 1)
                    ve.drain()
                    ve.tensor_copy(dttH[:], dtt[:, 1])
                    ve.drain()
                    ve.tensor_tensor(dttL[:], dtt[:, 1], dttH[:].bitcast(F32), ALU.subtract).then_inc(split_ready, 1)

            def pairs(t):
                return t.rearrange("p (j b) -> p j b", b=2)

            def att_logits(h, i):
                S = stat[:, i]
                ve.wait_ge(scores_done, h * 4 + (i + 1))
                for j in range(2):
                    last = ve.scalar_tensor_tensor(out=lg[:, i, j, :], in0=dist[:],
                                                   scalar=nslope[:, ds(h * HK + (2 * i + j), 1)],
                                                   in1=ps[:, M + j, 0:3 * P], op0=ALU.mult, op1=ALU.add)
                last.then_inc(logits_done, 1)
                ve.drain()
                mx = pairs(S[:, 0, :])
                ve.tensor_reduce(mx[:, :, 0:1], lg[:, i, :, 0:P], op=ALU.max, axis=AX.X)
                ve.tensor_reduce(mx[:, :, 1:2], lg[:, i, :, P:3 * P], op=ALU.max, axis=AX.X)
                ve.drain()
                sink = par[:, ds(h * HK + (PC["sinks"] + 2 * i), 2)][:, :, None].to_broadcast([P, 2, 2])
                ve.tensor_tensor(pairs(S[:, 4, :]), mx, sink, ALU.max)
                ve.drain()
                ve.tensor_scalar(S[:, 1, :], S[:, 4, :], -1.0, None, ALU.mult)
                ve.tensor_tensor(pairs(S[:, 2, :]), sink, pairs(S[:, 4, :]), ALU.subtract).then_inc(max_ready, 1)

            def att_probs(h, i):
                S = stat[:, i]
                ve.wait_ge(exps_done, h * 4 + (i + 1))
                ve.tensor_tensor(S[:, 4, :], S[:, 3, :], S[:, 2, :], ALU.add)
                ve.drain()
                ve.reciprocal(S[:, 5, :], S[:, 4, :])
                ve.drain()
                r = pairs(S[:, 5, :])
                ve.tensor_tensor(lg[:, i, :, 0:P], lg[:, i, :, 0:P], r[:, :, 0:1].to_broadcast([P, 2, P]), ALU.mult)
                ve.tensor_tensor(lg[:, i, :, P:3 * P], lg[:, i, :, P:3 * P], r[:, :, 1:2].to_broadcast([P, 2, 2 * P]),
                                 ALU.mult).then_inc(probs_ready, 1)

            def att_side(h, u, older=True, newer=True):
                if u == 0 and older:
                    att_probs(h - 1, 2)
                    att_logits(h - 1, 3)
                if u == 2:
                    if older:
                        att_probs(h - 1, 3)
                    if newer:
                        att_logits(h, 0)
                if u == 4 and newer:
                    att_probs(h, 0)
                    att_logits(h, 1)
                if u == 6 and newer:
                    att_probs(h, 1)
                    att_logits(h, 2)

            def conv_rest(n0, tiles, pair):
                ve.wait_ge(conv_first, n0 + 2)
                for tap in range(TAPS - 1):
                    sh = TAPS - 1 - tap
                    for i, (slot, ch) in enumerate(tiles):
                        last = ve.scalar_tensor_tensor(out=cv[:, slot, sh:SEQ], in0=ps[:, pair + i, 0:SEQ - sh],
                                                       scalar=pcol("conv_w", ch * TAPS + tap), in1=cv[:, slot, sh:SEQ],
                                                       op0=ALU.mult, op1=ALU.add)
                        if tap == TAPS - 2 and i == 1:
                            last.then_inc(pair_free[pair], 1)
                    ve.drain()

            def group(g, body):
                for u in range(G_UN):
                    lo_of(U_G + u, g * G_UN)
                    if u == 6:
                        conv_rest(g * 6, ((4, g + 32), (5, g + 40)), A)
                    if u == 10:
                        conv_rest(g * 6 + 2, ((0, g * 4), (1, g * 4 + 1)), B)
                    if u == 14:
                        conv_rest(g * 6 + 4, ((2, g * 4 + 2), (3, g * 4 + 3)), A)
                    body(u)

            def heads(t):
                return t.rearrange("p (h d) -> p h d", h=HG)

            def bc(t):
                return t[:, :, None].to_broadcast([P, HG, HD])

            def ssd_inputs(k):
                ve.wait_ge(btok_ready, k + 1)
                ve.tensor_tensor(cbm[:], ps[:, M, 0:2 * P].rearrange("p (c n) -> p c n", c=TT),
                                 triu[:, None, :].to_broadcast([P, TT, P]), ALU.mult)
                for c in range(TT):
                    ve.tensor_tensor(heads(xd[:, c, :]), heads(ps[:, M + 1 + c, :]), bc(dtt[:, 0, c, ds(k * HG, HG)]), ALU.mult)
                    ve.tensor_tensor(heads(xD[:, c, :]), heads(ps[:, M + 1 + c, :]),
                                     bc(par[:, ds(k * HG + PC["d_skip"], HG)]), ALU.mult)
                ve.drain()
                ve.tensor_tensor(heads(xds[:]), heads(xd[:, 0, :]), bc(edec[:, 1, ds(k * HG, HG)]), ALU.mult) \
                    .then_inc(xd_ready, 1)
                ve.wait_ge(decay_ready, k * 4 + 4)
                for c in range(TT):
                    last = ve.tensor_tensor(dec[:, c], dec[:, c], cbm[:, c, None, :].to_broadcast([P, HG, P]), ALU.mult)
                last.then_inc(g_ready, 1)

            def ssd_outputs(k):
                ve.wait_ge(y_done, k + 1)
                ve.tensor_tensor(heads(yoff[:]), heads(ps[:, M + 2, :]), bc(edec[:, 0, ds(k * HG, HG)]), ALU.mult)
                ve.tensor_tensor(y[:, 0, :], ps[:, M, :], xD[:, 0, :], ALU.add)
                ve.tensor_tensor(xD[:, 1, :], ps[:, M + 1, :], xD[:, 1, :], ALU.add)
                ve.drain()
                ve.tensor_tensor(y[:, 1, :], yoff[:], xD[:, 1, :], ALU.add)
                ve.drain()
                ve.tensor_tensor(y[:], y[:], szb[:], ALU.mult).then_inc(y_gated, 1)

            def ssd_scale(k):
                ve.wait_ge(y_rstd, k + 1)
                for c in range(TT):
                    last = ve.tensor_scalar(y[:, c, :], y[:, c, :], rstd[:, c:c + 1], None, ALU.mult)
                last.then_inc(yn_ready, 1)

            def ssd_side(k, u):
                if u == 8:
                    ssd_inputs(k)
                if u == 13:
                    ssd_outputs(k)
                if u == 17:
                    ssd_scale(k)

            group(0, keys_side)
            with ve.Fori(1, G) as g:
                group(g, lambda u: ssd_side(g - 1, u))
            for u in range(X_UN):
                lo_of(U_X + u, 0)
                ssd_side(G - 1, u)
            ssd_scale(G - 1)

            def branch_lo(n, dst, src, h):
                ve.wait_ge(ah_ready, n)
                ve.tensor_tensor(dst, src, h.bitcast(F32), ALU.subtract).then_inc(al_ready, 1)

            for u in range(Q_UN):
                lo_of(U_Q + u, 0)
                att_side(0, u, older=False)
            with ve.Fori(1, KVH - 1) as h:
                for u in range(Q_UN):
                    lo_of(U_Q + u, h * Q_UN)
                    att_side(h, u)
                    if u % 2 == 1:
                        c = ds(h * 16 + (2 * (u - 1) - 16), 4)
                        branch_lo(h * 4 + ((u + 1) // 2 - 4), aL[:, c, :], acts[:, c, :], aHs[:, c, :])

            def merge_ssm(m, u):
                if u == 10:
                    ve.wait_ge(unit_used, m * M_UN + (U_M + 8))
                    ve.tensor_tensor(mraw[:, ds(m * 2, 2), :], ps[:, A:A + 2, 0:SEQ], sgs[:], ALU.mult) \
                        .then_inc(pair_free[A], 1)

            def merge_attn(m, done, pair):
                ve.wait_ge(unit_used, done)
                ve.tensor_tensor(mtmp[:], ps[:, pair:pair + 2, 0:SEQ], sga[:], ALU.mult).then_inc(pair_free[pair], 1)
                ve.drain()
                ve.tensor_tensor(mraw[:, ds(m * 2, 2), :], mraw[:, ds(m * 2, 2), :], mtmp[:], ALU.add) \
                    .then_inc(merged, 1)

            for u in range(M_UN):
                lo_of(U_M + u, 0)
                if u < 8:
                    att_side(KVH - 1, u)
                elif u == 8:
                    att_side(KVH, 0, newer=False)
                elif u == 9:
                    att_probs(KVH - 1, 3)
                merge_ssm(0, u)
                if 10 <= u < 14:
                    i = u - 10
                    c = slice(NSM + 4 * i, NSM + 4 * i + 4)
                    branch_lo(9 + i, aL[:, c, :], acts[:, c, :], aHa[:, 4 * i:4 * i + 4, :])
                if u == 18:
                    merge_attn(0, U_M + 16, A)
            with ve.Fori(1, M_IT - 1) as m:
                for u in range(M_UN):
                    lo_of(U_M + u, m * M_UN)
                    merge_ssm(m, u)
                    if u == 18:
                        merge_attn(m, m * M_UN + (U_M + 16), A)
            m = M_IT - 1
            for u in range(12):
                lo_of(U_M + m * M_UN + u, 0)
                merge_ssm(m, u)

            def merged_lo(i):
                ve.wait_ge(mh_ready, i + 1)
                ve.tensor_tensor(mL[:, 4 * i:4 * i + 4, :], mraw[:, 4 * i:4 * i + 4, :],
                                 mH[:, 4 * i:4 * i + 4, :].bitcast(F32), ALU.subtract).then_inc(ml_ready, 1)

            for i in range(3):
                merged_lo(i)
            for u in range(SLOTS - 1):
                lo_of(U_O + u, 0)
            merge_attn(m, U_O, B)
            lo_of(U_O + SLOTS - 1, 0)
            merged_lo(3)

            def add_panel(done, pair, cols):
                ve.wait_ge(unit_used, done)
                ve.tensor_tensor(h1[:, :, cols], h1[:, :, cols], ps[:, pair:pair + 2, :], ALU.add) \
                    .then_inc(pair_free[pair], 1)

            for j in range(4):
                for u in range(8):
                    if 8 * j + u >= SLOTS:
                        lo_of(U_O + 8 * j + u, 0)
                    if u == 2 and j:
                        if j == 1:
                            for t in range(TT):
                                ve.wait_ge(h1_landed[t], 16)
                        add_panel(U_O + 8 * j, (A, B)[(j - 1) % 2], slice((j - 1) * W5, j * W5))
            for u in range(SLOTS - 1):
                lo_of(U_F + u, 0)
            add_panel(U_F, B, slice(3 * W5, D))
            lo_of(U_F + SLOTS - 1, 0)

            ve.wait_ge(rstd_ready, 2)
            for t in range(TT):
                ve.tensor_scalar(xn2[:, t, :], h1[:, t, :], rstd[:, t:t + 1], None, ALU.mult).then_inc(xn_ready, 1)
            norm_lo("ffn_norm", KD)

            def gate_rest(f):
                ve.wait_ge(fconv_first, f * 2 + 2)
                for tap in range(FTAPS - 1):
                    sh = FTAPS - 1 - tap
                    for i in range(2):
                        last = ve.scalar_tensor_tensor(out=gv[:, i, sh:SEQ], in0=ps[:, A + i, 0:SEQ - sh],
                                                       scalar=pcol("ffn_conv_w", f * (2 * FTAPS) + (i * FTAPS + tap)),
                                                       in1=gv[:, i, sh:SEQ], op0=ALU.mult, op1=ALU.add)
                        if tap == FTAPS - 2 and i == 1:
                            last.then_inc(pair_free[A], 1)
                    ve.drain()

            def h_of(f):
                ve.wait_ge(unit_used, f * F_UN + (U_F + F_UN))
                ve.wait_ge(gelu_ready, f + 1)
                ve.tensor_tensor(ht[:], ps[:, B:B + 2, 0:SEQ], gv[:], ALU.mult).then_inc(pair_free[B], 1)

            def h_lo(f):
                ve.wait_ge(hh_ready, f + 1)
                ve.tensor_tensor(hL[:, ds(f * 2, 2), :], ht[:], hH[:, ds(f * 2, 2), :].bitcast(F32),
                                 ALU.subtract).then_inc(hl_ready, 1)

            for u in range(F_UN):
                if u >= SLOTS:
                    lo_of(U_F + u, 0)
                if u == 6:
                    gate_rest(0)
            with ve.Fori(1, F_IT) as f:
                for u in range(F_UN):
                    lo_of(U_F + u, f * F_UN)
                    if u == 2:
                        h_of(f - 1)
                    if u == 4:
                        h_lo(f - 1)
                    if u == 6:
                        gate_rest(f)

            for u in range(SLOTS - 1):
                lo_of(U_E + u, 0)
            h_of(F_IT - 1)
            lo_of(U_E + SLOTS - 1, 0)
            h_lo(F_IT - 1)

            half = E_UN // 2
            for e in range(E_IT):
                for u in range(E_UN):
                    if e or u >= SLOTS:
                        lo_of(U_E + e * E_UN + u, 0)
                    n = 2 * e + u // half
                    if u % half == 3 and n:
                        add_panel(U_E + half * n, (A, B)[(n - 1) % 2], slice((n - 1) * W5, n * W5))
            add_panel(UNITS, B, slice(3 * W5, D))

            ve.wait_ge(rstd_ready, 3)
            ve.wait_ge(fw_landed, 16)
            for t in range(TT):
                for j in range(2):
                    c = slice(j * (D // 2), (j + 1) * (D // 2))
                    ve.scalar_tensor_tensor(out=h1[:, t, c], in0=h1[:, t, c], scalar=rstd[:, t:t + 1], in1=fw[:, c],
                                            op0=ALU.mult, op1=ALU.mult).then_inc(y_final, 1)

        @block.tensor
        def _(pe):
            def passes(out, w, x, start, stop):
                pe.matmul(out, w[0], x[0], start=start, stop=False)
                pe.matmul(out, w[0], x[1], start=False, stop=False)
                return pe.matmul(out, w[1], x[0], start=False, stop=stop)

            def columns(s, d, pair, xs, k, kt0, kt, w=W2, avail=None):
                pe.wait_ge(lo_ready, d + (s + 1))
                sl = s % SLOTS
                v = [t[:, sl, :].rearrange("p (k n) -> p k n", n=w) for t in (hi, lo)]
                for i in range(kt):
                    kk = kt0 + i
                    if avail:
                        avail(kk)
                    for c in range(w // P):
                        last = passes(ps[:, pair + c, 0:SEQ], [t[:, i, c * P:(c + 1) * P] for t in v],
                                      [t[:, kk, :] for t in xs], kk == 0, kk == k - 1)
                last.then_inc(unit_used, 1)

            def rows(s, d, pair, xs, k, kt0):
                pe.wait_ge(lo_ready, d + (s + 1))
                sl = s % SLOTS
                v = [t[:, sl, :].rearrange("p (k n) -> p k n", n=W5) for t in (hi, lo)]
                for i in range(2):
                    kk = kt0 + i
                    for t in range(TT):
                        last = passes(ps[:, pair + t, :], [a[:, kk, t * P:(t + 1) * P] for a in xs],
                                      [w[:, i, :] for w in v], kk == 0, kk == k - 1)
                last.then_inc(unit_used, 1)

            def job(pair, n):
                pe.wait_ge(pair_free[pair], n)

            U = (uH, uL)

            def turn_norm(src, base):
                for k in range(KD):
                    if base + k >= 4:
                        pe.wait_ge(u_ready, base + k - 3)
                    for t in range(TT):
                        if k == 0:
                            pe.wait_ge(xn_ready, base // KD * TT + t + 1)
                        last = pe.transpose(ps[:, M + k % 4, t * P:(t + 1) * P], src[:, t, k * P:(k + 1) * P], ident[:])
                    last.then_inc(norm_turned, 1)

            pe.wait_ge(consts_ready, 1)
            turn_norm(xn, 0)
            for i in range(2):
                columns(U_DT + i, 0, A, U, KD, 8 * i, 8, w=P, avail=lambda kk: pe.wait_ge(u_ready, kk + 1))
            for i in range(8):
                rows(U_KV + i, 0, B, U, KD, 2 * i)

            def turn_dt():
                pe.wait_ge(dt_done, 1)
                for a, w in ((0, 0), (1, 6)):
                    for c in range(TT):
                        o = (a * TT + c) * SH
                        last = pe.transpose(ps[:, M, o:o + SH], dtw[:, w, c * P:(c + 1) * P], ident[0:SH, 0:SH])
                last.then_inc(dt_turned, 1)

            def turn_keys():
                pe.wait_ge(pair_free[B], 1)
                for h in range(KVH):
                    for t in range(TT):
                        o = (h % 2) * SEQ + t * P
                        src = ktok[:, t, h].rearrange("p a d -> p (a d)")
                        last = pe.transpose(ps[:, M + 2 + h // 2, o:o + P], src, ident[:])
                last.then_inc(k_turned, 1)

            def cumulate():
                pe.wait_ge(dtt_ready, 1)
                pe.matmul(ps[:, M + 1, 0:SH], triu[:], dtt[:, 1, 1, :], start=True, stop=True)
                pe.matmul(ps[:, M + 1, SH:2 * SH], strict[:], dtt[:, 1, 0, :], start=True, stop=True).then_inc(cum_done, 1)


            def scores(h, i):
                if i % 2 == 0:
                    pe.wait_ge(pair_free[(A, B)[i // 2]], h + J_Q)
                if i == 0:
                    pe.wait_ge(k_cur, h + 1)
                if i or not isinstance(h, int) or h:
                    pe.wait_ge(logits_done, h * 4 + i)
                for blk, cols, keys in ((0, slice(0, P), slice(0, P)), (1, slice(P, 3 * P), slice(0, SEQ))):
                    for j in range(2):
                        r = slice(j * HD, j * HD + HD)
                        last = pe.matmul(ps[:, M + j, cols], qT[r, i, blk * P:(blk + 1) * P], kcur[r, keys],
                                         start=True, stop=True)
                last.then_inc(scores_done, 1)

            def turn_probs(h, i):
                pe.wait_ge(probs_ready, h * 4 + (i + 1))
                if i or not isinstance(h, int) or h:
                    pe.wait_ge(attn_out, h * 4 + i)
                else:
                    pe.wait_ge(y_kept, G + 1)
                for j in range(2):
                    for c in range(3):
                        o = (3 * j + c) * P
                        last = pe.transpose(ps[:, M + 2 + o // 512, o % 512:o % 512 + P],
                                            lg[:, i, j, c * P:(c + 1) * P], ident[:])
                last.then_inc(probs_turned, 1)

            def values(h, i):
                pe.wait_ge(pt_ready, h * 4 + (i + 1))
                if i == 0:
                    pe.wait_ge(v_cur, h + 1)
                for j in range(2):
                    r = slice(j * HD, j * HD + HD)
                    p = pT[:, i % 2, j * 3 * P:(j + 1) * 3 * P]
                    pe.matmul(ps[r, M + 3, SEQ:2 * SEQ], vcur[:, 0, :], p[:, 0:SEQ], start=True, stop=False)
                    last = pe.matmul(ps[r, M + 3, SEQ + P:2 * SEQ], vcur[:, 1, :], p[:, SEQ:3 * P], start=False, stop=True)
                last.then_inc(pv_done, 1)

            def att_before(h, u, older=True):
                if u == 0:
                    if older:
                        values(h - 1, 2)
                    scores(h, 0)
                if u == 1 and older:
                    turn_probs(h - 1, 3)
                if u == 2:
                    if older:
                        values(h - 1, 3)
                    scores(h, 1)
                if u == 3:
                    turn_probs(h, 0)
                if u == 4:
                    values(h, 0)
                    scores(h, 2)
                if u == 5:
                    turn_probs(h, 1)
                if u == 6:
                    values(h, 1)
                    scores(h, 3)
                if u == 7:
                    turn_probs(h, 2)

            def seg(k, c):
                if c == 0:
                    pe.wait_ge(adm_ready, k + 1)
                else:
                    pe.wait_ge(y_kept, k + 1)
                for b in range(2):
                    out = ps[:, M + 2 * c + b, :]
                    part = [t[:, c, 4 * b:4 * b + 4, :].rearrange("p h n -> p (h n)") for t in (admH, admL)]
                    pe.matmul(out, strictR[:], part[0], start=True, stop=False)
                    last = pe.matmul(out, strictR[:], part[1], start=False, stop=True)
                last.then_inc(seg_done, 1)

            def turn_x(k):
                pe.wait_ge(sv_ready, k + 1)
                pe.wait_ge(decay_ready, k * 4 + 3)
                for c in range(TT):
                    pe.matmul(ps[:, M, c * P:(c + 1) * P], sv[:, 4, c * P:(c + 1) * P], sv[:, 5, c * P:(c + 1) * P],
                              start=True, stop=True)
                pe.transpose(ps[:, M, 2 * P:3 * P], sv[:, 4, 0:P], ident[:])
                for c in range(TT):
                    for i in range(4):
                        last = pe.transpose(ps[:, M + 1 + c, i * P:(i + 1) * P], sv[:, i, c * P:(c + 1) * P], ident[:])
                last.then_inc(cb_done, 1)

            def state(k):
                pe.wait_ge(btok_ready, k + 1)
                pe.wait_ge(xd_ready, k + 1)
                pe.wait_ge(decay_ready, k * 4 + 4)
                pe.matmul(ps[:, M + 3, :], btok[:], xds[:], start=True, stop=True).then_inc(state_done, 1)

            def y_of(k):
                pe.wait_ge(g_ready, k + 1)
                for c in range(TT):
                    for h in range(HG):
                        pe.matmul(ps[:, M + c, h * HD:(h + 1) * HD], dec[:, c, h, :], xd[:, c, h * HD:(h + 1) * HD],
                                  start=True, stop=True)
                pe.wait_ge(st_ready, k + 1)
                pe.matmul(ps[:, M + 2, :], sv[:, 5, P:SEQ], st[:], start=True, stop=True).then_inc(y_done, 1)

            def turn_y(k):
                pe.wait_ge(yn_ready, k + 1)
                for i in range(4):
                    for c in range(TT):
                        o = (i % 2) * SEQ + c * P
                        last = pe.transpose(ps[:, M + 2 + i // 2, o:o + P], y[:, c, i * P:(i + 1) * P], ident[:])
                last.then_inc(y_turned, 1)

            def ssd_after(k, u):
                if u == 1:
                    seg(k, 0)
                if u == 2:
                    seg(k, 1)
                if u == 4:
                    turn_x(k)
                if u == 7:
                    state(k)
                if u == 9:
                    y_of(k)
                if u == 15:
                    turn_y(k)

            def keys_after(u):
                if u == 0:
                    turn_dt()
                if u == 1:
                    turn_keys()
                if u == 5:
                    cumulate()

            def group(g, after):
                for u in range(G_UN):
                    if u == 0:
                        job(A, g * 2 + J_G)
                    if u == 4:
                        job(B, g * 2 + J_G)
                    if u == 8:
                        job(A, g * 2 + (J_G + 1))
                    if u == 12:
                        job(B, g * 2 + (J_G + 1))
                    if u < 4:
                        columns(U_G + u, g * G_UN, A + u // 2, U, KD, 8 * (u % 2), 8, w=P)
                    elif u < 12:
                        columns(U_G + u, g * G_UN, (A, B, A)[u // 4], U, KD, 4 * (u % 4), 4)
                    else:
                        rows(U_G + u, g * G_UN, B, U, KD, 2 * (u - 12))
                    after(u)

            group(0, keys_after)
            pe.wait_ge(edec_ready, 1)
            pe.wait_ge(kdup_ready, 1)
            pe.sem_inc(seg_done, 2)
            pe.sem_inc(y_kept, 1)
            with pe.Fori(1, G) as g:
                group(g, lambda u: ssd_after(g - 1, u))

            def quarter(s, d, u, pair, n, xs=U, k=KD):
                if u == 0:
                    job(pair, n)
                columns(s + u, d, pair, xs, k, 4 * u, 4)

            for u in range(X_UN):
                quarter(U_X + u - u % 4, 0, u % 4, (A, B)[u // 4 % 2], J_X + u // 8)
                ssd_after(G - 1, u)
            for u in range(Q_UN):
                att_before(0, u, older=False)
                quarter(U_Q + u - u % 4, 0, u % 4, (A, B)[u // 4], J_Q)
            with pe.Fori(1, KVH - 1) as h:
                for u in range(Q_UN):
                    att_before(h, u)
                    quarter(U_Q + u - u % 4, h * Q_UN, u % 4, (A, B)[u // 4], h + J_Q)

            SSM, ATT = (aHs, aL[:, 0:NSM, :]), (aHa, aL[:, NSM:NA, :])

            def merge(d, j, u):
                if u < 8:
                    quarter(U_M, d, u, A, j + J_M, SSM, NSM)
                elif u < 12:
                    quarter(U_M + 8, d, u - 8, B, j + J_M)
                elif u < 16:
                    quarter(U_M + 12, d, u - 12, A, j + (J_M + 1), ATT)
                else:
                    quarter(U_M + 16, d, u - 16, B, j + (J_M + 1))

            for u in range(M_UN):
                if u < 8:
                    att_before(KVH - 1, u)
                    pe.wait_ge(al_ready, u + 1)
                elif u == 8:
                    values(KVH - 1, 2)
                elif u == 10:
                    turn_probs(KVH - 1, 3)
                elif u == 11:
                    values(KVH - 1, 3)
                elif 12 <= u < 16:
                    pe.wait_ge(al_ready, u - 3)
                merge(0, 0, u)
            with pe.Fori(1, M_IT - 1) as m:
                for u in range(M_UN):
                    merge(m * M_UN, m * 2, u)
            last = (M_IT - 1) * M_UN
            for u in range(8):
                merge(last, 2 * (M_IT - 1), u)
            for u in range(4):
                quarter(U_M + last + 8, 0, u, B, J_O - 1, ATT)

            for j in range(4):
                job((A, B)[j % 2], J_O + j // 2)
                for u in range(8):
                    if j == 0:
                        pe.wait_ge(ml_ready, u // 2 + 1)
                    rows(U_O + 8 * j + u, 0, (A, B)[j % 2], (mH, mL), KD, 2 * u)

            turn_norm(xn2, KD)
            for u in range(F_UN):
                if u % 4 == 0:
                    job((A, B)[u // 4], J_F)
                columns(U_F + u, 0, (A, B)[u // 4], U, KD, 4 * (u % 4), 4,
                        avail=(lambda kk: pe.wait_ge(u_ready, KD + kk + 1)) if u < 4 else None)
            with pe.Fori(1, F_IT) as f:
                for u in range(F_UN):
                    if u % 4 == 0:
                        job((A, B)[u // 4], f + J_F)
                    columns(U_F + u, f * F_UN, (A, B)[u // 4], U, KD, 4 * (u % 4), 4)

            half = E_UN // 2
            for n in range(4):
                job((A, B)[n % 2], J_E + n // 2)
                for u in range(half):
                    if n == 0 and u >= half - 1:
                        pe.wait_ge(hl_ready, F_IT)
                    elif n == 0 and u == 0:
                        pe.wait_ge(hl_ready, F_IT - 1)
                    rows(U_E + half * n + u, 0, (A, B)[n % 2], (hH, hL), KF, 2 * u)


def kernel(**inputs):
    import numpy as np
    import concourse.bacc as bacc
    from concourse.bass_utils import run_bass_kernel_spmd

    a = {n: np.ascontiguousarray(v) for n, v in inputs.items()}

    def channels(v, tiles):
        return v.reshape(tiles, P, -1).transpose(1, 0, 2).reshape(P, -1)

    def heads(v):
        return np.concatenate([v.reshape(SH, 1), np.zeros((P - SH, 1), np.float32)])

    params = np.ascontiguousarray(np.concatenate([
        channels(a["attn_norm_w"][0], KD), channels(a["ffn_norm_w"][0], KD),
        channels(a["ssm_conv_w"][0].T, 48), channels(a["ssm_conv_b"][0], 48),
        channels(a["ssm_norm_w"][0], DI // P), channels(a["ffn_conv_w"][0].T, KF), channels(a["ffn_conv_b"][0], KF),
        heads(a["dt_bias"][0]), heads(a["a_log"][0]),
        np.broadcast_to(a["d_skip"], (P, SH)), np.broadcast_to(a["attn_sinks"], (P, AH))], axis=1))
    feeds = {
        "x": a["x"].reshape(SEQ, D), "params": params, "w_in": a["w_in"][0], "w_ssm_out": a["w_ssm_out"][0],
        "w_attn_out": a["w_attn_out"][0], "w_o": a["w_o"][0], "w_ffn_in": a["w_ffn_in"][0],
        "w_ffn_out": a["w_ffn_out"][0], "final_norm_w": a["final_norm_w"].reshape(1, D),
    }
    nc = bacc.Bacc("TRN2", target_bir_lowering=False, num_devices=1)
    args = [nc.dram_tensor(n, v.shape, mybir.dt.from_np(v.dtype), kind="ExternalInput").ap() for n, v in feeds.items()]
    out = nc.dram_tensor("out", (SEQ, D), F32, kind="ExternalOutput").ap()
    build(nc, *args, out)
    r = run_bass_kernel_spmd(nc, [feeds], core_ids=[0])
    return r.results[0]["out"].reshape(1, SEQ, D)
```

```python
from contextlib import ExitStack

import concourse.bass as bass
from concourse import mybir

F32 = mybir.dt.float32
F32R = mybir.dt.float32r
ALU = mybir.AluOpType
ACT = mybir.ActivationFunctionType
AX = mybir.AxisListType
ds = bass.ds

P = 128
SEQ = 256
TT = SEQ // P
D = 2048
KD = D // P
DI = 4096
SH, HD = 64, 64
G, NS = 8, 128
HG = SH // G
GW = DI // G
AH, KVH = 32, 4
HK = AH // KVH
FF = 5632
TAPS, FTAPS = 4, 3
EPS = 1e-5
BIG = 3.0e38

C_Z = 0
C_X = C_Z + DI
C_B = C_X + DI
C_C = C_B + G * NS
C_DT = C_C + G * NS
C_Q = C_DT + SH
C_K = C_Q + AH * HD
C_GS = C_K + 2 * KVH * HD
C_GA = C_GS + D

SLOTS = 4
SLOT = 1024
W2 = 256
W5 = 512
U_DT = 0
U_KV = U_DT + 2
U_G, G_UN = U_KV + 8, 20
U_X, X_UN = U_G + G_UN * G, 16
U_Q, Q_UN = U_X + X_UN, 8
U_M, M_UN, M_IT = U_Q + Q_UN * (KVH - 1), 20, D // W2
U_O = U_M + M_UN * (M_IT - 1) + 12
U_F, F_UN, F_IT = U_O + 32, 8, FF // W2
U_E, E_UN, E_IT = U_F + F_UN * F_IT, 2 * (FF // P) // 2, 2
UNITS = U_E + E_UN * E_IT
KF = FF // P
OUT_COLS = slice(0, 5 * D // 8), slice(5 * D // 8, D)

J_G = 1
J_X = J_G + 2 * G
J_Q = J_X + 2
J_M = J_Q + KVH - 1
J_O = J_M + 2 * (M_IT - 1) + 1

PC = {}
_at = 0
for _n, _w in (("attn_norm", KD), ("ffn_norm", KD), ("conv_w", 48 * TAPS), ("conv_b", 48),
               ("ssm_norm", DI // P), ("ffn_conv_w", KF * FTAPS), ("ffn_conv_b", KF),
               ("dt_bias", 1), ("a_log", 1), ("d_skip", SH), ("sinks", AH)):
    PC[_n] = _at
    _at += _w
PW = _at


def build(nc, x, params, w_in, w_ssm, w_attn, w_o, w_fi, w_fo, fnorm, out):
    wv = {n: w.rearrange("(k p) n -> p k n", p=P)
          for n, w in (("in", w_in), ("ssm", w_ssm), ("attn", w_attn), ("o", w_o), ("fi", w_fi), ("fo", w_fo))}
    x_v = x.rearrange("(t p) d -> t p d", p=P)
    out_v = out.rearrange("(t p) d -> t p d", p=P)

    with ExitStack() as ctx:
        top = (nc.sbuf_base + 31) // 32 * 32
        end = nc.sbuf_usable_end

        def place(name, shape, at, dt=F32):
            size = 4
            for s in shape[1:]:
                size *= s
            assert at + size <= end, (name, at + size, end)
            return nc.alloc_sbuf_tensor_at(name, shape, dt, offset=at), (at + size + 31) // 32 * 32

        raw, top = place("raw", [P, SLOTS, SLOT], top)
        hi, top = place("hi", [P, SLOTS, SLOT], top, F32R)
        lo, top = place("lo", [P, SLOTS, SLOT], top, F32R)
        u_at = top
        uH, top = place("uH", [P, KD, SEQ], top, F32R)
        uL, top = place("uL", [P, KD, SEQ], top, F32R)
        par, top = place("par", [P, PW], top)
        ident, top = place("ident", [P, P], top)
        neghalf, top = place("neghalf", [P, TT], top)
        inv_w, top = place("inv_w", [P, TT], top)
        ss, top = place("ss", [P, TT, 4], top)
        ssum, top = place("ssum", [P, TT], top)
        rstd, top = place("rstd", [P, TT], top)
        rstd1, top = place("rstd1", [P, TT], top)
        rb, top = place("rb", [P, TT, P], top)
        rt, top = place("rt", [P, SEQ], top)
        region = top

        KB, NA, NSM = 1024, 48, DI // P
        acts, _ = place("acts", [P, NA, SEQ], region)
        aL, _ = place("aL", [P, NA, SEQ], region, F32R)
        aHs, _ = place("aHs", [P, NSM, SEQ], region + 48 * KB, F32R)
        aHa, _ = place("aHa", [P, NA - NSM, SEQ], region + 80 * KB, F32R)
        mraw, _ = place("mraw", [P, KD, SEQ], region + 96 * KB)
        sgs, a = place("sgs", [P, 2, SEQ], region + 112 * KB)
        sga, a = place("sga", [P, 2, SEQ], a)
        mtmp, tail = place("mtmp", [P, 2, SEQ], a)
        x_tok, a = place("x_tok", [P, TT, D], region)
        xsq, a = place("xsq", [P, D // 2], a)
        lg, a = place("lg", [P, 4, 2, 3 * P], region + 80 * KB)
        kcur, a = place("kcur", [P, SEQ], a)
        vcur, a = place("vcur", [P, TT, HD], a)
        dist, a = place("dist", [P, 3 * P], a)
        nslope, a = place("nslope", [P, AH], a)
        stat, a = place("stat", [P, 4, 6, 4], a)
        assert a <= region + 96 * KB
        kdup, a = place("kdup", [P, KVH, SEQ], region + 96 * KB)
        vtok, a = place("vtok", [P, TT, KVH * HD], a)
        qT, a = place("qT", [P, 4, SEQ], a)
        pT, a = place("pT", [P, 2, 2 * 3 * P], a)
        assert a <= region + 112 * KB
        admH, a = place("admH", [P, TT, HG, P], region + 32 * KB, F32R)
        admL, a = place("admL", [P, TT, HG, P], a, F32R)
        assert a <= region + 48 * KB
        cv, a = place("cv", [P, 6, SEQ], region + 48 * KB)
        sv, a = place("sv", [P, 6, SEQ], a)
        dtw, _ = place("dtw", [SH, 8, SEQ], a)
        szb, a = place("szb", [P, TT, GW], a)
        dec, a = place("dec", [P, TT, HG, P], a)
        xd, a = place("xd", [P, TT, GW], a)
        xD, a = place("xD", [P, TT, GW], a)
        assert a <= region + 80 * KB
        y, a = place("y", [P, TT, GW], region + 80 * KB)
        yoff, a = place("yoff", [P, GW], a)
        xds, a = place("xds", [P, GW], a)
        st, a = place("st", [P, GW], a)
        cbm, a = place("cbm", [P, TT, P], a)
        btok, a = place("btok", [P, P], a)
        assert a <= region + 92 * KB
        ktok, a = place("ktok", [P, TT, KVH, 2, HD], region + 80 * KB)
        disti, _ = place("disti", [P, 3 * P], a, mybir.dt.int32)
        cs, _ = place("cs", [P, 2, SEQ], region + 112 * KB)
        triu, a = place("triu", [P, P], tail)
        strict, a = place("strict", [P, P], a)
        strictR, a = place("strictR", [P, P], a, F32R)
        dtt, a = place("dtt", [P, 2, TT, SH], a)
        dttH, a = place("dttH", [P, TT, SH], a, F32R)
        dttL, a = place("dttL", [P, TT, SH], a, F32R)
        edec, a = place("edec", [P, 2, SH], a)
        mH, a = place("mH", [P, KD, SEQ], region, F32R)
        mL, a = place("mL", [P, KD, SEQ], a, F32R)
        hH, a = place("hH", [P, KF, SEQ], region, F32R)
        hL, a = place("hL", [P, KF, SEQ], a, F32R)
        h1, a = place("h1", [P, TT, D], a)
        fw, a = place("fw", [P, D], a)
        gv, a = place("gv", [P, 2, SEQ], a)
        ht, a = place("ht", [P, 2, SEQ], a)
        sqo, a = place("sqo", [P, W5], a)
        gs, a = place("gs", [P, 2, SEQ], a)
        yw, _ = place("yw", [P, TT, D], u_at)

        ps = ctx.enter_context(nc.psum_tensor("ps", [P, 8, 512], F32))
        A, B, M = 0, 2, 4

        def sem(name):
            return ctx.enter_context(nc.semaphore(name))

        raw_landed = [sem(f"raw_landed{i}") for i in range(SLOTS)]
        hi_ready, lo_ready, unit_used = sem("hi_ready"), sem("lo_ready"), sem("unit_used")
        pair_free = {A: sem("pair_a_free"), B: sem("pair_b_free")}
        x_landed = [[sem(f"x_landed{t}{j}") for j in range(2)] for t in range(TT)]
        h1_landed = [sem(f"h1_landed{t}") for t in range(TT)]
        par_landed, fw_landed = sem("par_landed"), sem("fw_landed")
        consts_ready, squares_done = sem("consts_ready"), sem("squares_done")
        mean_ready, rstd_ready = sem("mean_ready"), sem("rstd_ready")
        panel_added, rb_ready, rt_turned = sem("panel_added"), sem("rb_ready"), sem("rt_turned")
        norm_turned, uh_ready, u_ready = sem("norm_turned"), sem("uh_ready"), sem("u_ready")
        dt_abs, dt_exp, dt_done, dt_turned, dtt_ready = (sem("dt_abs"), sem("dt_exp"), sem("dt_done"),
                                                         sem("dt_turned"), sem("dtt_ready"))
        cum_done, edec_ready = sem("cum_done"), sem("edec_ready")
        k_turned, kdup_ready, k_cur, v_cur = sem("k_turned"), sem("kdup_ready"), sem("k_cur"), sem("v_cur")
        q_scaled = sem("q_scaled")
        scores_done, logits_done, max_ready = sem("scores_done"), sem("logits_done"), sem("max_ready")
        exps_done, probs_ready, probs_turned, pt_ready = (sem("exps_done"), sem("probs_ready"),
                                                          sem("probs_turned"), sem("pt_ready"))
        pv_done, attn_out = sem("pv_done"), sem("attn_out")
        split_ready, sv_ready = sem("dta_split_ready"), sem("sv_ready")
        conv_first, conv_done = sem("conv_first"), sem("conv_done")
        adm_ready, seg_done, decay_ready = sem("adm_ready"), sem("seg_done"), sem("decay_ready")
        x_turned, btok_ready, xd_ready, g_ready = sem("x_turned"), sem("btok_ready"), sem("xd_ready"), sem("g_ready")
        state_done, st_ready, y_done, y_gated = sem("state_done"), sem("st_ready"), sem("y_done"), sem("y_gated")
        y_squared, y_rstd, yn_ready, y_turned, y_kept = (sem("y_squared"), sem("y_rstd"), sem("yn_ready"),
                                                         sem("y_turned"), sem("y_kept"))
        ah_ready, al_ready = sem("ah_ready"), sem("al_ready")
        sgs_ready, sga_ready = sem("sgs_ready"), sem("sga_ready")
        merged, mh_ready, ml_ready = sem("merged"), sem("mh_ready"), sem("ml_ready")
        gs_ready, fconv_first, fconv_done, gelu_ready = (
            sem("gs_ready"), sem("fconv_first"), sem("fconv_done"), sem("gelu_ready"))
        ht_ready, hh_ready, hl_ready = sem("ht_ready"), sem("hh_ready"), sem("hl_ready")
        tile0_done = sem("tile0_done")
        y_final, out_written = (sem("y_final_vector"), sem("y_final_scalar")), sem("out_written")

        def pcol(name, i=0, n=1):
            return par[:, ds(i + PC[name], n)]

        block = ctx.enter_context(nc.Block())

        @block.sync
        def _(sp):
            def load_x(j):
                for t in range(TT):
                    c = slice(j * (D // 2), (j + 1) * (D // 2))
                    sp.dma_start(x_tok[:, t, c], x_v[t][:, c]).then_inc(x_landed[t][j], 16)

            def load(s, d, src, kt, w):
                if s >= SLOTS:
                    sp.wait_ge(lo_ready, d + (s - SLOTS + 1))
                dst = raw[:, s % SLOTS, 0:kt * w].rearrange("p (k n) -> p k n", k=kt)
                return sp.dma_start(dst, src)

            def stream(s, d, name, k0, kt, c, w):
                load(s, d, wv[name][:, k0:k0 + kt, ds(c, w)], kt, w).then_inc(raw_landed[s % SLOTS], 16)

            def columns(s, d, name, c, k):
                for i in range(k // 4):
                    stream(s + i, d, name, 4 * i, 4, c, W2)

            def rows(s, d, name, c, k):
                for i in range(k // 2):
                    stream(s + i, d, name, 2 * i, 2, c, W5)

            for i in range(2):
                load_x(i)
                if i == 0:
                    sp.dma_start(par[:], params).then_inc(par_landed, 16)
                stream(U_DT + i, 0, "in", 8 * i, 8, C_DT, P)
            rows(U_KV, 0, "in", C_K, KD)
            with sp.Fori(1, G + 1) as g1:
                d = (g1 - 1) * G_UN
                for i in range(4):
                    stream(U_G + i, d, "in", 8 * (i % 2), 8, g1 * NS + ((C_B, C_C)[i // 2] - NS), P)
                columns(U_G + 4, d, "in", g1 * GW + (C_X - GW), KD)
                columns(U_G + 8, d, "in", g1 * GW + (C_X - GW + W2), KD)
                rows(U_G + 12, d, "in", g1 * GW + (C_Z - GW), KD)
            columns(U_X, 0, "in", C_Q, KD)
            columns(U_X + 4, 0, "in", C_Q + W2, KD)
            columns(U_X + 8, 0, "in", C_GS, KD)
            columns(U_X + 12, 0, "in", C_GA, KD)
            with sp.Fori(1, KVH) as q:
                for j in range(2):
                    columns(U_Q + 4 * j, (q - 1) * Q_UN, "in", q * (2 * W2) + (C_Q + j * W2), KD)
            with sp.Fori(1, M_IT) as m1:
                d = (m1 - 1) * M_UN
                columns(U_M, d, "ssm", m1 * W2 - W2, DI // P)
                columns(U_M + 8, d, "in", m1 * W2 + C_GS, KD)
                columns(U_M + 12, d, "attn", m1 * W2 - W2, KD)
                columns(U_M + 16, d, "in", m1 * W2 + C_GA, KD)
            last = U_M + (M_IT - 1) * M_UN
            columns(last, 0, "ssm", D - W2, DI // P)
            columns(last + 8, 0, "attn", D - W2, KD)
            rows(U_O, 0, "o", 0, KD)
            sp.wait_ge(ml_ready, 4)
            for t in range(TT):
                sp.dma_start(h1[:, t, :], x_v[t]).then_inc(h1_landed[t], 16)
            for j in range(1, 4):
                rows(U_O + 8 * j, 0, "o", j * W5, KD)
            sp.dma_start(fw[:], fnorm.to_broadcast([P, D])).then_inc(fw_landed, 16)
            with sp.Fori(0, F_IT) as f:
                d = f * F_UN
                columns(U_F, d, "fi", f * W2, KD)
                columns(U_F + 4, d, "fi", f * W2 + FF, KD)
            with sp.Fori(0, E_IT) as e:
                for j in range(2):
                    rows(U_E + (KF // 2) * j, e * E_UN, "fo", e * (2 * W5) + j * W5, KF)
            for t in range(TT):
                for j in range(2):
                    sp.wait_ge(y_final[j], t + 1)
                    sp.dma_start(out_v[t][:, OUT_COLS[j]], yw[:, t, OUT_COLS[j]]).then_inc(out_written, 16)
            sp.wait_ge(out_written, 16 * 2 * TT)

        @block.gpsimd
        def _(po):
            po.memset(neghalf[:], -0.5)
            po.memset(inv_w[:], 1.0 / GW)
            po.memset(ident[:], 0.0)
            po.memset(triu[:], 1.0)
            po.memset(strict[:], 1.0)
            for h in range(AH):
                po.memset(nslope[:, h:h + 1], -2.0 ** (-8.0 / AH * (h + 1)))
            po.iota(disti[:, 0:P], [[-1, P]], base=0, channel_multiplier=1)
            po.iota(disti[:, P:3 * P], [[-1, 2 * P]], base=P, channel_multiplier=1)
            po.drain()
            po.affine_select(out=ident[:], in_=ident[:], compare_op=ALU.not_equal, fill=1.0,
                             base=0, pattern=[[-1, P]], channel_multiplier=1)
            po.drain()
            po.memset(rstd[:], 0.0).then_inc(consts_ready, 1)
            po.affine_select(out=triu[:], in_=triu[:], compare_op=ALU.is_ge, fill=0.0,
                             base=0, pattern=[[1, P]], channel_multiplier=-1)
            po.affine_select(out=strict[:], in_=strict[:], compare_op=ALU.is_ge, fill=0.0,
                             base=-1, pattern=[[-1, P]], channel_multiplier=1)
            po.tensor_copy(dist[:], disti[:])
            po.drain()
            po.tensor_copy(strictR[:], strict[:])
            po.drain()
            po.affine_select(out=dist[:, 0:P], in_=dist[:, 0:P], compare_op=ALU.is_ge, fill=BIG,
                             base=0, pattern=[[-1, P]], channel_multiplier=1)
            po.affine_select(out=dist[:, P:3 * P], in_=dist[:, P:3 * P], compare_op=ALU.is_ge, fill=BIG,
                             base=P, pattern=[[-1, 2 * P]], channel_multiplier=1)
            po.drain()
            po.affine_select(out=dist[:, P:3 * P], in_=dist[:, P:3 * P], compare_op=ALU.is_ge, fill=BIG,
                             base=-1, pattern=[[1, 2 * P]], channel_multiplier=-1).then_inc(consts_ready, 1)

            def root(n, t0=0, t1=TT):
                po.wait_ge(mean_ready, n)
                po.tensor_tensor(rstd[:, t0:t1], ssum[:, t0:t1], neghalf[:, t0:t1], ALU.pow).then_inc(rstd_ready, 1)

            root(1)

            po.wait_ge(split_ready, 1)
            with po.Fori(0, G) as g:
                po.wait_ge(seg_done, g * 2 + 2)
                for parts, adm in ((dttH, admH), (dttL, admL)):
                    for c in range(TT):
                        part = parts[:, c, ds(g * HG, HG)].bitcast(F32)
                        last = po.tensor_tensor(adm[:, c], part[:, :, None].to_broadcast([P, HG, P]),
                                                triu[:, None, :].to_broadcast([P, HG, P]), ALU.mult)
                last.then_inc(adm_ready, 1)
                po.wait_ge(y_squared, g + 1)
                po.tensor_tensor(ssum[:], ssum[:], inv_w[:], ALU.mult)
                po.drain()
                po.tensor_scalar(ssum[:], ssum[:], EPS, None, ALU.add)
                po.drain()
                po.tensor_tensor(rstd[:], ssum[:], neghalf[:], ALU.pow).then_inc(y_rstd, 1)

            def k_static(h):
                po.tensor_copy(kcur[:], kdup[:, ds(h, 1), :].rearrange("p a n -> p (a n)")).then_inc(k_cur, 1)

            def v_static(h):
                po.tensor_copy(vcur[:], vtok[:, :, ds(h * HD, HD)]).then_inc(v_cur, 1)

            def q_scaled_in(j, pair, n):
                po.wait_ge(pair_free[pair], n)
                q = qT[:, 2 * j:2 * j + 2, :]
                po.tensor_tensor(q, q, rt[:, None, :].to_broadcast([P, 2, SEQ]), ALU.mult).then_inc(q_scaled, 1)

            po.wait_ge(kdup_ready, 1)
            k_static(0)
            v_static(0)
            q_scaled_in(0, A, J_X + 1)
            q_scaled_in(1, B, J_X + 1)
            with po.Fori(1, KVH) as h:
                q_scaled_in(0, A, h + J_Q)
                po.wait_ge(scores_done, h * 4)
                k_static(h)
                q_scaled_in(1, B, h + J_Q)
                po.wait_ge(pv_done, h * 4)
                v_static(h)
            root(2)
            root(3, 0, 1)
            root(4, 1, 2)

        @block.scalar
        def _(act):
            def hi_of(s, d):
                act.wait_ge(raw_landed[s % SLOTS], d * 4 + 16 * (s // SLOTS + 1))
                if s >= SLOTS:
                    act.wait_ge(unit_used, d + (s - SLOTS + 1))
                act.activation(hi[:, s % SLOTS, :], raw[:, s % SLOTS, :], ACT.Copy).then_inc(hi_ready, 1)

            def x_squares(j):
                for t in range(TT):
                    act.wait_ge(x_landed[t][j], 16)
                    act.drain()
                    last = act.activation(xsq[:], x_tok[:, t, j * (D // 2):(j + 1) * (D // 2)], ACT.Square,
                                          accum_out=ss[:, t, j:j + 1])
                return last

            def norm_hi(name, base, panel):
                for k in range(4 * panel, 4 * panel + 4):
                    act.wait_ge(norm_turned, base + k + 1)
                    act.activation(uH[:, k, :], ps[:, M + k % 4, 0:SEQ], ACT.Identity,
                                   scale=pcol(name, k)).then_inc(uh_ready, 1)

            norm_hi("attn_norm", 0, 0)
            hi_of(0, 0)
            x_squares(0)
            for i in range(1, 4):
                norm_hi("attn_norm", 0, i)
                hi_of(i, 0)
            hi_of(4, 0)
            x_squares(1).then_inc(squares_done, 1)
            for u in range(5, 8):
                hi_of(u, 0)
            act.wait_ge(dt_abs, 1)
            act.activation(dtw[:, 1, :], dtw[:, 1, :], ACT.Exp, scale=-1.0)
            act.activation(dtw[:, 7, 0:1], par[0:SH, PC["a_log"]:PC["a_log"] + 1], ACT.Exp).then_inc(dt_exp, 1)
            for u in range(8, 10):
                hi_of(u, 0)

            def q_keep(s, d, j, pair):
                act.wait_ge(unit_used, d + s)
                act.activation(qT[:, 2 * j:2 * j + 2, :], ps[:, pair:pair + 2, 0:SEQ], ACT.Copy,
                               scale=HD ** -0.5).then_inc(pair_free[pair], 1)

            def att_exps(h, i):
                act.wait_ge(max_ready, h * 4 + (i + 1))
                S = stat[:, i]
                for j in range(2):
                    act.activation(lg[:, i, j, 0:P], lg[:, i, j, 0:P], ACT.Exp, bias=S[:, 1, 2 * j:2 * j + 1],
                                   accum_out=S[:, 3, 2 * j:2 * j + 1])
                    act.activation(lg[:, i, j, P:3 * P], lg[:, i, j, P:3 * P], ACT.Exp, bias=S[:, 1, 2 * j + 1:2 * j + 2],
                                   accum_out=S[:, 3, 2 * j + 1:2 * j + 2])
                act.activation(S[:, 2, :], S[:, 2, :], ACT.Exp).then_inc(exps_done, 1)

            def att_turned(h, i):
                act.wait_ge(probs_turned, h * 4 + (i + 1))
                act.activation(pT[:, i % 2], ps[:, M + 2:M + 4, :].rearrange("p b n -> p (b n)")[:, 0:6 * P],
                               ACT.Copy).then_inc(pt_ready, 1)

            def att_keep(h, i):
                act.wait_ge(pv_done, h * 4 + (i + 1))
                act.activation(acts[:, ds(h * 4 + (NSM + i), 1), :].rearrange("p a n -> p (a n)"),
                               ps[:, M + 3, SEQ:2 * SEQ], ACT.Copy).then_inc(attn_out, 1)

            def att_side(h, u, older=True, newer=True):
                if u == 1 and older:
                    att_keep(h - 1, 1)
                    att_turned(h - 1, 2)
                    att_exps(h - 1, 3)
                if u == 3:
                    if older:
                        att_keep(h - 1, 2)
                        att_turned(h - 1, 3)
                    if newer:
                        att_exps(h, 0)
                if u == 5:
                    if older:
                        att_keep(h - 1, 3)
                    if newer:
                        att_turned(h, 0)
                        att_exps(h, 1)
                if u == 7 and newer:
                    att_keep(h, 0)
                    att_turned(h, 1)
                    att_exps(h, 2)

            def conv_start(pair, n, tiles):
                act.wait_ge(pair_free[pair], n)
                for i, (slot, ch) in enumerate(tiles):
                    act.activation(cv[:, slot, :], cs[:, i, :], ACT.Identity,
                                   scale=pcol("conv_w", ch * TAPS + (TAPS - 1)), bias=pcol("conv_b", ch)) \
                        .then_inc(conv_first, 1)

            def silus(k):
                act.wait_ge(unit_used, k * G_UN + (U_G + G_UN))
                for t in range(TT):
                    last = act.activation(szb[:, t, :], ps[:, B + t, :], ACT.Silu, scale=rstd1[:, t:t + 1])
                last.then_inc(pair_free[B], 1)
                act.wait_ge(conv_done, k * 3 + 3)
                act.activation(sv[:].rearrange("p a n -> p (a n)"), cv[:].rearrange("p a n -> p (a n)"),
                               ACT.Silu).then_inc(sv_ready, 1)

            def decays(k, c):
                act.wait_ge(seg_done, k * 2 + (2 + c + 1))
                for b in range(2):
                    act.activation(dec[:, c, 4 * b:4 * b + 4, :].rearrange("p h n -> p (h n)"),
                                   ps[:, M + 2 * c + b, :], ACT.Exp).then_inc(decay_ready, 1)

            def b_keep(k):
                act.wait_ge(x_turned, k + 1)
                act.activation(btok[:], ps[:, M, 2 * P:3 * P], ACT.Copy).then_inc(btok_ready, 1)

            def st_keep(k):
                act.wait_ge(state_done, k + 1)
                act.activation(st[:], ps[:, M + 3, :], ACT.Copy).then_inc(st_ready, 1)

            def y_squares(k):
                act.wait_ge(y_gated, k + 1)
                for c in range(TT):
                    if c:
                        act.drain()
                    last = act.activation(yoff[:], y[:, c, :], ACT.Square, accum_out=ssum[:, c:c + 1])
                last.then_inc(y_squared, 1)

            def y_keep(k):
                act.wait_ge(y_turned, k + 1)
                for i in range(4):
                    last = act.activation(acts[:, ds(k * 4 + i, 1), :].rearrange("p a n -> p (a n)"),
                                          ps[:, M + 2 + i // 2, (i % 2) * SEQ:(i % 2 + 1) * SEQ], ACT.Identity,
                                          scale=pcol("ssm_norm", k * 4 + i))
                last.then_inc(y_kept, 1)

            def group(g, body):
                for u in range(G_UN):
                    hi_of(U_G + u, g * G_UN)
                    if u == 7:
                        conv_start(A, g * 2 + (J_G + 1), ((4, g + 32), (5, g + 40)))
                    if u == 11:
                        conv_start(B, g * 2 + (J_G + 1), ((0, g * 4), (1, g * 4 + 1)))
                    if u == 15:
                        conv_start(A, g * 2 + (J_G + 2), ((2, g * 4 + 2), (3, g * 4 + 3)))
                    body(u)

            def ssd_side(k, u):
                if u == 2:
                    silus(k)
                if u == 5:
                    decays(k, 0)
                if u == 6:
                    decays(k, 1)
                if u == 8:
                    b_keep(k)
                if u == 11:
                    st_keep(k)
                if u == 14:
                    y_squares(k)
                if u == 19:
                    y_keep(k)

            def keys_side(u):
                if u == 2:
                    act.wait_ge(unit_used, U_G)
                    act.wait_ge(rb_ready, 1)
                    for t in range(TT):
                        for i in range(2):
                            act.activation(ktok[:, t, :, i, :],
                                           ps[:, B + t, 0:KVH * HD].rearrange("p (h d) -> p h d", h=KVH), ACT.Copy, scale=rstd1[:, t:t + 1])
                        last = act.activation(vtok[:, t, :], ps[:, B + t, KVH * HD:2 * KVH * HD], ACT.Copy,
                                              scale=rstd1[:, t:t + 1])
                    last.then_inc(pair_free[B], 1)
                if u == 5:
                    act.wait_ge(k_turned, 1)
                    act.activation(kdup[:].rearrange("p (a h) n -> p a (h n)", a=2), ps[:, M + 2:M + 4, :],
                                   ACT.Copy).then_inc(kdup_ready, 1)
                if u == 13:
                    act.wait_ge(cum_done, 1)
                    act.activation(edec[:].rearrange("p a n -> p (a n)"), ps[:, M + 1, 0:2 * SH],
                                   ACT.Exp).then_inc(edec_ready, 1)

            group(0, keys_side)
            with act.Fori(1, G) as g:
                group(g, lambda u: ssd_side(g - 1, u))

            def gate(dst, pair, n, ready):
                act.wait_ge(pair_free[pair], n)
                act.activation(dst[:], dst[:], ACT.Sigmoid).then_inc(ready, 1)

            for u in range(X_UN):
                hi_of(U_X + u, 0)
                ssd_side(G - 1, u)
                if u == 6:
                    q_keep(U_X + 4, 0, 0, A)
                if u == 10:
                    q_keep(U_X + 8, 0, 1, B)

            def q_block(h, body):
                for u in range(Q_UN):
                    hi_of(U_Q + u, h * Q_UN)
                    if u == 6:
                        act.wait_ge(scores_done, h * 4 + 2)
                        q_keep(U_Q + 4, h * Q_UN, 0, A)
                    body(u)

            def q_rest(h, u):
                if u == 2:
                    act.wait_ge(scores_done, h * 4)
                    q_keep(U_Q, h * Q_UN, 1, B)

            def first_head(u):
                if u == 0:
                    gate(sgs, A, J_Q, sgs_ready)
                if u == 2:
                    y_keep(G - 1)
                if u == 3:
                    gate(sga, B, J_Q, sga_ready)
                att_side(0, u, older=False)

            q_block(0, first_head)

            def later_head(h, u):
                q_rest(h, u)
                att_side(h, u)
                if u % 2 == 0:
                    c = ds(h * 16 + (2 * u - 16), 4)
                    act.activation(aHs[:, c, :], acts[:, c, :], ACT.Copy).then_inc(ah_ready, 1)

            with act.Fori(1, KVH - 1) as h:
                q_block(h, lambda u: later_head(h, u))

            def merge_gates(m, u):
                if u == 15:
                    gate(sgs, B, m * 2 + (J_M + 1), sgs_ready)

            def merge_gate_rest(m, u):
                if u == 3:
                    gate(sga, B, m * 2 + J_M, sga_ready)

            def attn_hi(i):
                act.activation(aHa[:, 4 * i:4 * i + 4, :], acts[:, NSM + 4 * i:NSM + 4 * i + 4, :],
                               ACT.Copy).then_inc(ah_ready, 1)

            for u in range(M_UN):
                hi_of(U_M + u, 0)
                if u < 8:
                    q_rest(KVH - 1, u)
                    att_side(KVH - 1, u)
                elif u < 11:
                    att_side(KVH, u - 8, newer=False)
                    if u > 8:
                        attn_hi(u - 9)
                elif u == 11:
                    att_keep(KVH - 1, 2)
                    att_turned(KVH - 1, 3)
                    att_keep(KVH - 1, 3)
                elif u < 14:
                    act.drain()
                    attn_hi(u - 10)
                merge_gates(0, u)
            with act.Fori(1, M_IT - 1) as m:
                for u in range(M_UN):
                    hi_of(U_M + u, m * M_UN)
                    merge_gate_rest(m, u)
                    merge_gates(m, u)
            m = M_IT - 1
            for u in range(12):
                hi_of(U_M + m * M_UN + u, 0)
                merge_gate_rest(m, u)

            def merged_hi(i):
                act.activation(mH[:, 4 * i:4 * i + 4, :], mraw[:, 4 * i:4 * i + 4, :], ACT.Copy).then_inc(mh_ready, 1)

            act.wait_ge(merged, M_IT - 1)
            act.wait_ge(unit_used, U_O - 4)
            for i in range(3):
                merged_hi(i)
            for u in range(SLOTS):
                hi_of(U_O + u, 0)
            act.wait_ge(merged, M_IT)
            merged_hi(3)

            def square_panel(n, j):
                act.wait_ge(panel_added, n)
                for t in range(TT):
                    act.drain()
                    last = act.activation(sqo[:], h1[:, t, j * W5:(j + 1) * W5], ACT.Square, accum_out=ss[:, t, j:j + 1])
                return last

            for j in range(4):
                for u in range(8):
                    if 8 * j + u >= SLOTS:
                        hi_of(U_O + 8 * j + u, 0)
                    if u == 3 and j:
                        square_panel(j, j - 1)
                    if u == 6 and j:
                        norm_hi("ffn_norm", KD, j - 1)
            for u in range(SLOTS - 1):
                hi_of(U_F + u, 0)
            square_panel(4, 3).then_inc(squares_done, 1)
            hi_of(U_F + SLOTS - 1, 0)
            norm_hi("ffn_norm", KD, 3)

            def gate_start(f):
                act.wait_ge(gs_ready, f + 1)
                for i in range(2):
                    act.activation(gv[:, i, :], gs[:, i, :], ACT.Identity,
                                   scale=pcol("ffn_conv_w", f * (2 * FTAPS) + (i * FTAPS + FTAPS - 1)),
                                   bias=pcol("ffn_conv_b", f * 2 + i)).then_inc(fconv_first, 1)

            def gelu(f):
                act.wait_ge(fconv_done, f + 1)
                act.activation(gv[:], gv[:], ACT.Gelu).then_inc(gelu_ready, 1)

            def h_hi(f):
                act.wait_ge(ht_ready, f + 1)
                act.activation(hH[:, ds(f * 2, 2), :], ht[:], ACT.Copy).then_inc(hh_ready, 1)

            for u in range(F_UN):
                if u >= SLOTS:
                    hi_of(U_F + u, 0)
                if u == 7:
                    gate_start(0)
            with act.Fori(1, F_IT) as f:
                for u in range(F_UN):
                    hi_of(U_F + u, f * F_UN)
                    if u == 0:
                        gelu(f - 1)
                    if u == 3:
                        h_hi(f - 1)
                    if u == 7:
                        gate_start(f)

            hi_of(U_E, 0)
            gelu(F_IT - 1)
            for u in range(1, SLOTS):
                hi_of(U_E + u, 0)
            h_hi(F_IT - 1)

            half = E_UN // 2
            for e in range(E_IT):
                for u in range(E_UN):
                    if e or u >= SLOTS:
                        hi_of(U_E + e * E_UN + u, 0)
                    n = 2 * e + u // half
                    if u % half == 4 and n:
                        square_panel(n + 4, n - 1)
            for t in range(TT):
                act.wait_ge(panel_added, 8 + t)
                act.drain()
                act.activation(sqo[:], h1[:, t, 3 * W5:D], ACT.Square, accum_out=ss[:, t, 3:4]).then_inc(squares_done, 1)
                act.wait_ge(rstd_ready, 3 + t)
                act.activation(yw[:, t, OUT_COLS[1]], yw[:, t, OUT_COLS[1]], ACT.Copy,
                               scale=rstd[:, t:t + 1]).then_inc(y_final[1], 1)

        @block.vector
        def _(ve):
            def lo_of(s, d):
                ve.wait_ge(hi_ready, d + (s + 1))
                ve.tensor_tensor(lo[:, s % SLOTS, :], raw[:, s % SLOTS, :], hi[:, s % SLOTS, :].bitcast(F32),
                                 ALU.subtract).then_inc(lo_ready, 1)

            def mean(n, t0=0, t1=TT):
                ve.tensor_reduce(ssum[:, t0:t1, None], ss[:, t0:t1, 0:n], op=ALU.add, axis=AX.X)
                ve.drain()
                ve.tensor_scalar(ssum[:, t0:t1], ssum[:, t0:t1], 1.0 / D, EPS, ALU.mult, ALU.add).then_inc(mean_ready, 1)

            def norm_lo(name, base, panel):
                for k in range(4 * panel, 4 * panel + 4):
                    ve.wait_ge(uh_ready, base + k + 1)
                    ve.scalar_tensor_tensor(out=uL[:, k, :], in0=ps[:, M + k % 4, 0:SEQ], scalar=pcol(name, k),
                                            in1=uH[:, k, :].bitcast(F32), op0=ALU.mult,
                                            op1=ALU.subtract).then_inc(u_ready, 1)

            for i in range(4):
                norm_lo("attn_norm", 0, i)
                lo_of(i, 0)
            lo_of(4, 0)

            def spread(n):
                ve.wait_ge(rstd_ready, n)
                ve.tensor_copy(rb[:], rstd[:, :, None].to_broadcast([P, TT, P])).then_inc(rb_ready, 1)

            def take_rt(n):
                ve.wait_ge(rt_turned, n)
                ve.tensor_copy(rt[:], ps[:, M, 0:SEQ])
                ve.drain()

            def scaled(dst, pair):
                return ve.tensor_tensor(dst, ps[:, pair:pair + 2, 0:SEQ], rt[:, None, :].to_broadcast([P, 2, SEQ]),
                                        ALU.mult)

            ve.wait_ge(squares_done, 1)
            mean(2)
            ve.wait_ge(rstd_ready, 1)
            ve.tensor_copy(rstd1[:], rstd[:])
            ve.drain()
            spread(1)
            lo_of(5, 0)
            lo_of(6, 0)
            take_rt(1)
            W = lambda i: dtw[:, i, :]
            ve.wait_ge(unit_used, U_KV)
            ve.tensor_tensor(W(0), ps[0:SH, A, 0:SEQ], rt[0:SH, :], ALU.mult).then_inc(pair_free[A], 1)
            ve.drain()
            ve.tensor_scalar(W(0), W(0), par[0:SH, PC["dt_bias"]:PC["dt_bias"] + 1], None, ALU.add)
            ve.drain()
            ve.scalar_tensor_tensor(out=W(1), in0=W(0), scalar=-1.0, in1=W(0), op0=ALU.mult,
                                    op1=ALU.max).then_inc(dt_abs, 1)
            ve.tensor_scalar(W(2), W(0), 0.0, None, ALU.max)
            for u in range(7, 9):
                lo_of(u, 0)

            def atanh_start():
                ve.wait_ge(dt_exp, 1)
                ve.tensor_scalar(W(3), W(1), 2.0, None, ALU.add)
                ve.drain()
                ve.reciprocal(W(4), W(3))
                ve.drain()
                ve.tensor_tensor(W(3), W(1), W(4), ALU.mult)
                ve.drain()
                ve.tensor_tensor(W(4), W(3), W(3), ALU.mult)
                ve.drain()
                ve.tensor_scalar(W(5), W(4), 1.0 / 17, None, ALU.mult)
                ve.drain()

            def atanh_terms(*ns):
                for n in ns:
                    ve.scalar_tensor_tensor(out=W(5), in0=W(5), scalar=1.0 / n, in1=W(4), op0=ALU.add, op1=ALU.mult)
                    ve.drain()

            def dt_end():
                ve.scalar_tensor_tensor(out=W(5), in0=W(5), scalar=1.0, in1=W(3), op0=ALU.add, op1=ALU.mult)
                ve.drain()
                ve.scalar_tensor_tensor(out=W(0), in0=W(5), scalar=2.0, in1=W(2), op0=ALU.mult, op1=ALU.add)
                ve.drain()
                ve.tensor_scalar(W(6), W(0), dtw[:, 7, 0:1], -1.0, ALU.mult, ALU.mult).then_inc(dt_done, 1)

            atanh_start()
            lo_of(9, 0)
            ve.wait_ge(consts_ready, 2)

            def dt_side(u):
                if u == 0:
                    atanh_terms(15, 13, 11)
                if u == 1:
                    atanh_terms(9, 7)
                if u == 2:
                    atanh_terms(5, 3)
                if u == 3:
                    dt_end()
                if u == 8:
                    ve.wait_ge(dt_turned, 1)
                    ve.tensor_copy(dtt[:].rearrange("p a c n -> p (a c n)"), ps[:, M, 0:2 * TT * SH]).then_inc(dtt_ready, 1)
                    ve.drain()
                    ve.tensor_copy(dttH[:], dtt[:, 1])
                    ve.drain()
                    ve.tensor_tensor(dttL[:], dtt[:, 1], dttH[:].bitcast(F32), ALU.subtract).then_inc(split_ready, 1)

            def pairs(t):
                return t.rearrange("p (j b) -> p j b", b=2)

            def att_logits(h, i):
                S = stat[:, i]
                ve.wait_ge(scores_done, h * 4 + (i + 1))
                for j in range(2):
                    last = ve.scalar_tensor_tensor(out=lg[:, i, j, :], in0=dist[:],
                                                   scalar=nslope[:, ds(h * HK + (2 * i + j), 1)],
                                                   in1=ps[:, M + j, 0:3 * P], op0=ALU.mult, op1=ALU.add)
                last.then_inc(logits_done, 1)
                ve.drain()
                mx = pairs(S[:, 0, :])
                ve.tensor_reduce(mx[:, :, 0:1], lg[:, i, :, 0:P], op=ALU.max, axis=AX.X)
                ve.tensor_reduce(mx[:, :, 1:2], lg[:, i, :, P:3 * P], op=ALU.max, axis=AX.X)
                ve.drain()
                sink = par[:, ds(h * HK + (PC["sinks"] + 2 * i), 2)][:, :, None].to_broadcast([P, 2, 2])
                ve.tensor_tensor(pairs(S[:, 4, :]), mx, sink, ALU.max)
                ve.drain()
                ve.tensor_scalar(S[:, 1, :], S[:, 4, :], -1.0, None, ALU.mult)
                ve.tensor_tensor(pairs(S[:, 2, :]), sink, pairs(S[:, 4, :]), ALU.subtract).then_inc(max_ready, 1)

            def att_probs(h, i):
                S = stat[:, i]
                ve.wait_ge(exps_done, h * 4 + (i + 1))
                ve.tensor_tensor(S[:, 4, :], S[:, 3, :], S[:, 2, :], ALU.add)
                ve.drain()
                ve.reciprocal(S[:, 5, :], S[:, 4, :])
                ve.drain()
                r = pairs(S[:, 5, :])
                ve.tensor_tensor(lg[:, i, :, 0:P], lg[:, i, :, 0:P], r[:, :, 0:1].to_broadcast([P, 2, P]), ALU.mult)
                ve.tensor_tensor(lg[:, i, :, P:3 * P], lg[:, i, :, P:3 * P], r[:, :, 1:2].to_broadcast([P, 2, 2 * P]),
                                 ALU.mult).then_inc(probs_ready, 1)

            def att_first(h, u, older=True):
                if u in (0, 2) and older:
                    att_probs(h - 1, 2 + u // 2)
                if u in (4, 6):
                    att_probs(h, u // 2 - 2)

            def att_side(h, u, older=True):
                if u == 0 and older:
                    att_logits(h - 1, 3)
                if u in (2, 4, 6):
                    att_logits(h, u // 2 - 1)

            def conv_scaled(pair, done):
                ve.wait_ge(unit_used, done)
                scaled(cs[:], pair).then_inc(pair_free[pair], 1)

            def conv_rest(n0, tiles):
                ve.wait_ge(conv_first, n0 + 2)
                for tap in range(TAPS - 1):
                    sh = TAPS - 1 - tap
                    for i, (slot, ch) in enumerate(tiles):
                        last = ve.scalar_tensor_tensor(out=cv[:, slot, sh:SEQ], in0=cs[:, i, 0:SEQ - sh],
                                                       scalar=pcol("conv_w", ch * TAPS + tap), in1=cv[:, slot, sh:SEQ],
                                                       op0=ALU.mult, op1=ALU.add)
                        if tap == TAPS - 2 and i == 1:
                            last.then_inc(conv_done, 1)
                    ve.drain()

            def group(g, body):
                for u in range(G_UN):
                    lo_of(U_G + u, g * G_UN)
                    if u in (6, 10, 14):
                        conv_scaled(B if u == 10 else A, g * G_UN + (U_G + u - 2))
                    if u == 7:
                        conv_rest(g * 6, ((4, g + 32), (5, g + 40)))
                    if u == 11:
                        conv_rest(g * 6 + 2, ((0, g * 4), (1, g * 4 + 1)))
                    if u == 15:
                        conv_rest(g * 6 + 4, ((2, g * 4 + 2), (3, g * 4 + 3)))
                    body(u)

            def heads(t):
                return t.rearrange("p (h d) -> p h d", h=HG)

            def bc(t):
                return t[:, :, None].to_broadcast([P, HG, HD])

            def ssd_inputs(k):
                ve.wait_ge(btok_ready, k + 1)
                ve.tensor_tensor(cbm[:], ps[:, M, 0:2 * P].rearrange("p (c n) -> p c n", c=TT),
                                 triu[:, None, :].to_broadcast([P, TT, P]), ALU.mult)
                for c in range(TT):
                    ve.tensor_tensor(heads(xd[:, c, :]), heads(ps[:, M + 1 + c, :]), bc(dtt[:, 0, c, ds(k * HG, HG)]),
                                     ALU.mult)
                    ve.tensor_tensor(heads(xD[:, c, :]), heads(ps[:, M + 1 + c, :]),
                                     bc(par[:, ds(k * HG + PC["d_skip"], HG)]), ALU.mult)
                ve.drain()
                ve.tensor_tensor(heads(xds[:]), heads(xd[:, 0, :]), bc(edec[:, 1, ds(k * HG, HG)]), ALU.mult) \
                    .then_inc(xd_ready, 1)
                ve.wait_ge(decay_ready, k * 4 + 4)
                for c in range(TT):
                    last = ve.tensor_tensor(dec[:, c], dec[:, c], cbm[:, c, None, :].to_broadcast([P, HG, P]), ALU.mult)
                last.then_inc(g_ready, 1)

            def ssd_outputs(k):
                ve.wait_ge(y_done, k + 1)
                ve.tensor_tensor(heads(yoff[:]), heads(ps[:, M + 2, :]), bc(edec[:, 0, ds(k * HG, HG)]), ALU.mult)
                ve.tensor_tensor(y[:, 0, :], ps[:, M, :], xD[:, 0, :], ALU.add)
                ve.tensor_tensor(xD[:, 1, :], ps[:, M + 1, :], xD[:, 1, :], ALU.add)
                ve.drain()
                ve.tensor_tensor(y[:, 1, :], yoff[:], xD[:, 1, :], ALU.add)
                ve.drain()
                ve.tensor_tensor(y[:], y[:], szb[:], ALU.mult).then_inc(y_gated, 1)

            def ssd_scale(k):
                ve.wait_ge(y_rstd, k + 1)
                for c in range(TT):
                    last = ve.tensor_scalar(y[:, c, :], y[:, c, :], rstd[:, c:c + 1], None, ALU.mult)
                last.then_inc(yn_ready, 1)

            def ssd_side(k, u):
                if u == 8:
                    ssd_inputs(k)
                if u == 13:
                    ssd_outputs(k)
                if u == 17:
                    ssd_scale(k)

            group(0, dt_side)
            with ve.Fori(1, G) as g:
                group(g, lambda u: ssd_side(g - 1, u))

            def gate_scaled_in(dst, pair, done):
                ve.wait_ge(unit_used, done)
                scaled(dst[:], pair).then_inc(pair_free[pair], 1)

            for u in range(X_UN):
                lo_of(U_X + u, 0)
                ssd_side(G - 1, u)
                if u == 15:
                    gate_scaled_in(sgs, A, U_X + 12)
            ssd_scale(G - 1)

            def branch_lo(n, dst, src, h):
                ve.wait_ge(ah_ready, n)
                ve.tensor_tensor(dst, src, h.bitcast(F32), ALU.subtract).then_inc(al_ready, 1)

            for u in range(Q_UN):
                att_first(0, u, older=False)
                lo_of(U_Q + u, 0)
                if u == 2:
                    gate_scaled_in(sga, B, U_Q)
                att_side(0, u, older=False)
            with ve.Fori(1, KVH - 1) as h:
                for u in range(Q_UN):
                    att_first(h, u)
                    lo_of(U_Q + u, h * Q_UN)
                    att_side(h, u)
                    if u % 2 == 1:
                        c = ds(h * 16 + (2 * (u - 1) - 16), 4)
                        branch_lo(h * 4 + ((u + 1) // 2 - 4), aL[:, c, :], acts[:, c, :], aHs[:, c, :])

            def merge_ssm(m, u):
                if u == 10:
                    ve.wait_ge(unit_used, m * M_UN + (U_M + 8))
                    ve.wait_ge(sgs_ready, m + 1)
                    ve.tensor_tensor(mraw[:, ds(m * 2, 2), :], ps[:, A:A + 2, 0:SEQ], sgs[:], ALU.mult) \
                        .then_inc(pair_free[A], 1)

            def merge_gates(m, u):
                if u == 14:
                    gate_scaled_in(sgs, B, m * M_UN + (U_M + 12))

            def merge_attn(m, done, pair):
                ve.wait_ge(unit_used, done)
                ve.wait_ge(sga_ready, m + 1)
                ve.tensor_tensor(mtmp[:], ps[:, pair:pair + 2, 0:SEQ], sga[:], ALU.mult).then_inc(pair_free[pair], 1)
                ve.drain()
                ve.tensor_tensor(mraw[:, ds(m * 2, 2), :], mraw[:, ds(m * 2, 2), :], mtmp[:], ALU.add) \
                    .then_inc(merged, 1)

            for u in range(M_UN):
                if u < 8:
                    att_first(KVH - 1, u)
                elif u == 8:
                    att_probs(KVH - 1, 2)
                elif u == 10:
                    att_probs(KVH - 1, 3)
                lo_of(U_M + u, 0)
                if u < 8:
                    att_side(KVH - 1, u)
                elif u == 8:
                    att_logits(KVH - 1, 3)
                merge_ssm(0, u)
                if 10 <= u < 14:
                    i = u - 10
                    c = slice(NSM + 4 * i, NSM + 4 * i + 4)
                    branch_lo(9 + i, aL[:, c, :], acts[:, c, :], aHa[:, 4 * i:4 * i + 4, :])
                merge_gates(0, u)
                if u == 18:
                    merge_attn(0, U_M + 16, A)
            with ve.Fori(1, M_IT - 1) as m:
                for u in range(M_UN):
                    lo_of(U_M + u, m * M_UN)
                    if u == 2:
                        gate_scaled_in(sga, B, m * M_UN + U_M)
                    merge_ssm(m, u)
                    merge_gates(m, u)
                    if u == 18:
                        merge_attn(m, m * M_UN + (U_M + 16), A)
            m = M_IT - 1
            for u in range(12):
                lo_of(U_M + m * M_UN + u, 0)
                if u == 2:
                    gate_scaled_in(sga, B, m * M_UN + U_M)
                merge_ssm(m, u)

            def merged_lo(i):
                ve.wait_ge(mh_ready, i + 1)
                ve.tensor_tensor(mL[:, 4 * i:4 * i + 4, :], mraw[:, 4 * i:4 * i + 4, :],
                                 mH[:, 4 * i:4 * i + 4, :].bitcast(F32), ALU.subtract).then_inc(ml_ready, 1)

            for i in range(3):
                merged_lo(i)
            for u in range(SLOTS - 1):
                lo_of(U_O + u, 0)
            merge_attn(m, U_O, B)
            lo_of(U_O + SLOTS - 1, 0)
            merged_lo(3)

            def add_panel(done, pair, j):
                ve.wait_ge(unit_used, done)
                cols = slice(j * W5, (j + 1) * W5)
                ve.tensor_tensor(h1[:, :, cols], h1[:, :, cols], ps[:, pair:pair + 2, :], ALU.add).then_inc(panel_added, 1)

            for j in range(4):
                for u in range(8):
                    if 8 * j + u >= SLOTS:
                        lo_of(U_O + 8 * j + u, 0)
                    if u == 2 and j:
                        if j == 1:
                            for t in range(TT):
                                ve.wait_ge(h1_landed[t], 16)
                        add_panel(U_O + 8 * j, (A, B)[(j - 1) % 2], j - 1)
                    if u == 6 and j:
                        norm_lo("ffn_norm", KD, j - 1)
            for u in range(SLOTS - 1):
                lo_of(U_F + u, 0)
            add_panel(U_F, B, 3)

            lo_of(U_F + SLOTS - 1, 0)
            ve.wait_ge(squares_done, 2)
            mean(4)
            spread(2)
            norm_lo("ffn_norm", KD, 3)

            def gate_scaled(f):
                ve.wait_ge(unit_used, f * F_UN + (U_F + 4))
                scaled(gs[:], A).then_inc(gs_ready, 1)

            def gate_rest(f):
                ve.wait_ge(fconv_first, f * 2 + 2)
                for tap in range(FTAPS - 1):
                    sh = FTAPS - 1 - tap
                    for i in range(2):
                        last = ve.scalar_tensor_tensor(out=gv[:, i, sh:SEQ], in0=gs[:, i, 0:SEQ - sh],
                                                       scalar=pcol("ffn_conv_w", f * (2 * FTAPS) + (i * FTAPS + tap)),
                                                       in1=gv[:, i, sh:SEQ], op0=ALU.mult, op1=ALU.add)
                    if tap < FTAPS - 2:
                        ve.drain()
                last.then_inc(fconv_done, 1)

            def h_of(f):
                ve.wait_ge(unit_used, f * F_UN + (U_F + F_UN))
                scaled(ht[:], B).then_inc(pair_free[B], 1)
                ve.drain()
                ve.wait_ge(gelu_ready, f + 1)
                ve.tensor_tensor(ht[:], ht[:], gv[:], ALU.mult).then_inc(ht_ready, 1)

            def h_lo(f):
                ve.wait_ge(hh_ready, f + 1)
                ve.tensor_tensor(hL[:, ds(f * 2, 2), :], ht[:], hH[:, ds(f * 2, 2), :].bitcast(F32),
                                 ALU.subtract).then_inc(hl_ready, 1)

            for u in range(F_UN):
                if u >= SLOTS:
                    lo_of(U_F + u, 0)
                if u == 6:
                    take_rt(2)
                    gate_scaled(0)
                if u == 7:
                    gate_rest(0)
            with ve.Fori(1, F_IT) as f:
                for u in range(F_UN):
                    lo_of(U_F + u, f * F_UN)
                    if u == 2:
                        h_of(f - 1)
                    if u == 4:
                        h_lo(f - 1)
                    if u == 6:
                        gate_scaled(f)
                    if u == 7:
                        gate_rest(f)

            for u in range(SLOTS - 1):
                lo_of(U_E + u, 0)
            h_of(F_IT - 1)
            lo_of(U_E + SLOTS - 1, 0)
            h_lo(F_IT - 1)

            def weighted(j):
                cols = slice(j * W5, (j + 1) * W5)
                return ve.tensor_tensor(yw[:, :, cols], h1[:, :, cols],
                                        fw[:, None, cols].to_broadcast([P, TT, W5]), ALU.mult)

            ve.wait_ge(fw_landed, 16)
            half = E_UN // 2
            for e in range(E_IT):
                for u in range(E_UN):
                    if e or u >= SLOTS:
                        lo_of(U_E + e * E_UN + u, 0)
                    n = 2 * e + u // half
                    if u % half == 3 and n:
                        add_panel(U_E + half * n, (A, B)[(n - 1) % 2], n - 1)
                    if u % half == 5 and n:
                        weighted(n - 1)
            cols = slice(3 * W5, D)
            for t in range(TT):
                if t == 0:
                    ve.wait_ge(tile0_done, 1)
                else:
                    ve.wait_ge(unit_used, UNITS)
                ve.tensor_tensor(h1[:, t, cols], h1[:, t, cols], ps[:, B + t, :], ALU.add).then_inc(panel_added, 1)
                ve.drain()
                ve.tensor_tensor(yw[:, t, cols], h1[:, t, cols], fw[:, cols], ALU.mult)
                ve.wait_ge(squares_done, 3 + t)
                mean(4, t, t + 1)
                ve.wait_ge(rstd_ready, 3 + t)
                ve.tensor_scalar(yw[:, t, OUT_COLS[0]], yw[:, t, OUT_COLS[0]], rstd[:, t:t + 1], None,
                                 ALU.mult).then_inc(y_final[0], 1)

        @block.tensor
        def _(pe):
            def passes(out, w, x, start, stop):
                pe.matmul(out, w[0], x[0], start=start, stop=False)
                pe.matmul(out, w[0], x[1], start=False, stop=False)
                return pe.matmul(out, w[1], x[0], start=False, stop=stop)

            def columns(s, d, pair, xs, k, kt0, kt, w=W2, before=None, after=None):
                pe.wait_ge(lo_ready, d + (s + 1))
                sl = s % SLOTS
                v = [t[:, sl, :].rearrange("p (k n) -> p k n", n=w) for t in (hi, lo)]
                for i in range(kt):
                    kk = kt0 + i
                    if before:
                        before(kk)
                    for c in range(w // P):
                        last = passes(ps[:, pair + c, 0:SEQ], [t[:, i, c * P:(c + 1) * P] for t in v],
                                      [t[:, kk, :] for t in xs], kk == 0, kk == k - 1)
                    if i == kt - 1:
                        last.then_inc(unit_used, 1)
                    if after:
                        after(kk)

            def rows(s, d, pair, xs, k, kt0, tiles=range(TT)):
                pe.wait_ge(lo_ready, d + (s + 1))
                sl = s % SLOTS
                v = [t[:, sl, :].rearrange("p (k n) -> p k n", n=W5) for t in (hi, lo)]
                for i in range(2):
                    kk = kt0 + i
                    for t in tiles:
                        last = passes(ps[:, pair + t, :], [a[:, kk, t * P:(t + 1) * P] for a in xs],
                                      [w[:, i, :] for w in v], kk == 0, kk == k - 1)
                if TT - 1 in tiles:
                    last.then_inc(unit_used, 1)
                return last

            def job(pair, n):
                pe.wait_ge(pair_free[pair], n)

            U = (uH, uL)

            def turn_norm(src, base, k):
                if base + k >= 4:
                    pe.wait_ge(u_ready, base + k - 3)
                for t in range(TT):
                    last = pe.transpose(ps[:, M + k % 4, t * P:(t + 1) * P], src[:, t, k * P:(k + 1) * P], ident[:])
                last.then_inc(norm_turned, 1)

            def turn_first(k):
                if k < KD:
                    if k % (KD // 2) == 0:
                        for t in range(TT):
                            pe.wait_ge(x_landed[t][k // (KD // 2)], 16)
                    if k == 0:
                        pe.wait_ge(par_landed, 16)
                    turn_norm(x_tok, 0, k)

            def turn_rstd(n):
                pe.wait_ge(rb_ready, n)
                for t in range(TT):
                    last = pe.transpose(ps[:, M, t * P:(t + 1) * P], rb[:, t, :], ident[:])
                last.then_inc(rt_turned, 1)

            def keep_busy(n):
                for _ in range(n):
                    pe.transpose(ps[:, B, 0:P], ident[:], ident[:])

            pe.wait_ge(consts_ready, 1)
            keep_busy(9)
            for k in range(4):
                turn_first(k)
            keep_busy(14)
            for i in range(2):
                columns(U_DT + i, 0, A, U, KD, 8 * i, 8, w=P, before=lambda kk: pe.wait_ge(u_ready, kk + 1),
                        after=lambda kk: turn_first(kk + 4))
            for i in range(8):
                rows(U_KV + i, 0, B, U, KD, 2 * i)
                if i == 2:
                    turn_rstd(1)

            def turn_dt():
                pe.wait_ge(dt_done, 1)
                for a, w in ((0, 0), (1, 6)):
                    for c in range(TT):
                        o = (a * TT + c) * SH
                        last = pe.transpose(ps[:, M, o:o + SH], dtw[:, w, c * P:(c + 1) * P], ident[0:SH, 0:SH])
                last.then_inc(dt_turned, 1)

            def turn_keys():
                pe.wait_ge(pair_free[B], 1)
                for h in range(KVH):
                    for t in range(TT):
                        o = (h % 2) * SEQ + t * P
                        src = ktok[:, t, h].rearrange("p a d -> p (a d)")
                        last = pe.transpose(ps[:, M + 2 + h // 2, o:o + P], src, ident[:])
                last.then_inc(k_turned, 1)

            def cumulate():
                pe.wait_ge(dtt_ready, 1)
                pe.matmul(ps[:, M + 1, 0:SH], triu[:], dtt[:, 1, 1, :], start=True, stop=True)
                pe.matmul(ps[:, M + 1, SH:2 * SH], strict[:], dtt[:, 1, 0, :], start=True, stop=True).then_inc(cum_done, 1)


            def first_head(h):
                return isinstance(h, int) and h == 0

            def scores(h, i):
                if i % 2 == 0:
                    pe.wait_ge(q_scaled, h * 2 + (i // 2 + 1))
                if i == 0:
                    pe.wait_ge(k_cur, h + 1)
                if i or not first_head(h):
                    pe.wait_ge(logits_done, h * 4 + i)
                for blk, cols, keys in ((0, slice(0, P), slice(0, P)), (1, slice(P, 3 * P), slice(0, SEQ))):
                    for j in range(2):
                        r = slice(j * HD, j * HD + HD)
                        last = pe.matmul(ps[:, M + j, cols], qT[r, i, blk * P:(blk + 1) * P], kcur[r, keys],
                                         start=True, stop=True)
                last.then_inc(scores_done, 1)

            def turn_probs(h, i):
                pe.wait_ge(probs_ready, h * 4 + (i + 1))
                if i or not first_head(h):
                    pe.wait_ge(attn_out, h * 4 + i)
                else:
                    pe.wait_ge(y_kept, G + 1)
                for j in range(2):
                    for c in range(3):
                        o = (3 * j + c) * P
                        last = pe.transpose(ps[:, M + 2 + o // 512, o % 512:o % 512 + P],
                                            lg[:, i, j, c * P:(c + 1) * P], ident[:])
                last.then_inc(probs_turned, 1)

            def values(h, i):
                pe.wait_ge(pt_ready, h * 4 + (i + 1))
                if i == 0:
                    pe.wait_ge(v_cur, h + 1)
                for j in range(2):
                    r = slice(j * HD, j * HD + HD)
                    p = pT[:, i % 2, j * 3 * P:(j + 1) * 3 * P]
                    pe.matmul(ps[r, M + 3, SEQ:2 * SEQ], vcur[:, 0, :], p[:, 0:SEQ], start=True, stop=False)
                    last = pe.matmul(ps[r, M + 3, SEQ + P:2 * SEQ], vcur[:, 1, :], p[:, SEQ:3 * P], start=False, stop=True)
                last.then_inc(pv_done, 1)

            def att_before(h, u, older=True):
                if u == 0:
                    if older:
                        values(h - 1, 2)
                    scores(h, 0)
                if u == 1 and older:
                    turn_probs(h - 1, 3)
                if u == 2:
                    if older:
                        values(h - 1, 3)
                    scores(h, 1)
                if u == 3:
                    turn_probs(h, 0)
                if u == 4:
                    values(h, 0)
                    scores(h, 2)
                if u == 5:
                    turn_probs(h, 1)
                if u == 6:
                    values(h, 1)
                    scores(h, 3)
                if u == 7:
                    turn_probs(h, 2)

            def seg(k, c):
                if c == 0:
                    pe.wait_ge(adm_ready, k + 1)
                else:
                    pe.wait_ge(y_kept, k + 1)
                for b in range(2):
                    out = ps[:, M + 2 * c + b, :]
                    part = [t[:, c, 4 * b:4 * b + 4, :].rearrange("p h n -> p (h n)") for t in (admH, admL)]
                    pe.matmul(out, strictR[:], part[0], start=True, stop=False)
                    last = pe.matmul(out, strictR[:], part[1], start=False, stop=True)
                last.then_inc(seg_done, 1)

            def turn_x(k):
                pe.wait_ge(sv_ready, k + 1)
                pe.wait_ge(decay_ready, k * 4 + 3)
                for c in range(TT):
                    pe.matmul(ps[:, M, c * P:(c + 1) * P], sv[:, 4, c * P:(c + 1) * P], sv[:, 5, c * P:(c + 1) * P],
                              start=True, stop=True)
                pe.transpose(ps[:, M, 2 * P:3 * P], sv[:, 4, 0:P], ident[:])
                for c in range(TT):
                    for i in range(4):
                        last = pe.transpose(ps[:, M + 1 + c, i * P:(i + 1) * P], sv[:, i, c * P:(c + 1) * P], ident[:])
                last.then_inc(x_turned, 1)

            def state(k):
                pe.wait_ge(btok_ready, k + 1)
                pe.wait_ge(xd_ready, k + 1)
                pe.wait_ge(decay_ready, k * 4 + 4)
                pe.matmul(ps[:, M + 3, :], btok[:], xds[:], start=True, stop=True).then_inc(state_done, 1)

            def y_of(k):
                pe.wait_ge(g_ready, k + 1)
                for c in range(TT):
                    for h in range(HG):
                        pe.matmul(ps[:, M + c, h * HD:(h + 1) * HD], dec[:, c, h, :], xd[:, c, h * HD:(h + 1) * HD],
                                  start=True, stop=True)
                pe.wait_ge(st_ready, k + 1)
                pe.matmul(ps[:, M + 2, :], sv[:, 5, P:SEQ], st[:], start=True, stop=True).then_inc(y_done, 1)

            def turn_y(k):
                pe.wait_ge(yn_ready, k + 1)
                for i in range(4):
                    for c in range(TT):
                        o = (i % 2) * SEQ + c * P
                        last = pe.transpose(ps[:, M + 2 + i // 2, o:o + P], y[:, c, i * P:(i + 1) * P], ident[:])
                last.then_inc(y_turned, 1)

            def ssd_after(k, u):
                if u == 1:
                    seg(k, 0)
                if u == 2:
                    seg(k, 1)
                if u == 4:
                    turn_x(k)
                if u == 7:
                    state(k)
                if u == 9:
                    y_of(k)
                if u == 15:
                    turn_y(k)

            def keys_after(u):
                if u == 1:
                    turn_keys()
                if u == 5:
                    turn_dt()
                if u == 9:
                    cumulate()

            def group(g, after):
                for u in range(G_UN):
                    if u == 0:
                        job(A, g * 2 + J_G)
                    if u == 4:
                        job(B, g * 2 + J_G)
                    if u == 8:
                        job(A, g * 2 + (J_G + 1))
                    if u == 12:
                        job(B, g * 2 + (J_G + 1))
                    if u < 4:
                        columns(U_G + u, g * G_UN, A + u // 2, U, KD, 8 * (u % 2), 8, w=P)
                    elif u < 12:
                        columns(U_G + u, g * G_UN, (A, B, A)[u // 4], U, KD, 4 * (u % 4), 4)
                    else:
                        rows(U_G + u, g * G_UN, B, U, KD, 2 * (u - 12))
                    after(u)

            group(0, keys_after)
            pe.wait_ge(edec_ready, 1)
            pe.wait_ge(kdup_ready, 1)
            pe.sem_inc(seg_done, 2)
            pe.sem_inc(y_kept, 1)
            with pe.Fori(1, G) as g:
                group(g, lambda u: ssd_after(g - 1, u))

            def quarter(s, d, u, pair, n, xs=U, k=KD):
                if u == 0:
                    job(pair, n)
                columns(s + u, d, pair, xs, k, 4 * u, 4)

            for u in range(X_UN):
                quarter(U_X + u - u % 4, 0, u % 4, (A, B)[u // 4 % 2], J_X + u // 8)
                ssd_after(G - 1, u)
            for u in range(Q_UN):
                att_before(0, u, older=False)
                quarter(U_Q + u - u % 4, 0, u % 4, (A, B)[u // 4], J_Q)
            with pe.Fori(1, KVH - 1) as h:
                for u in range(Q_UN):
                    att_before(h, u)
                    quarter(U_Q + u - u % 4, h * Q_UN, u % 4, (A, B)[u // 4], h + J_Q)

            SSM, ATT = (aHs, aL[:, 0:NSM, :]), (aHa, aL[:, NSM:NA, :])

            def merge(d, j, u):
                if u < 8:
                    quarter(U_M, d, u, A, j + J_M, SSM, NSM)
                elif u < 12:
                    quarter(U_M + 8, d, u - 8, B, j + J_M)
                elif u < 16:
                    quarter(U_M + 12, d, u - 12, A, j + (J_M + 1), ATT)
                else:
                    quarter(U_M + 16, d, u - 16, B, j + (J_M + 1))

            for u in range(M_UN):
                if u < 8:
                    att_before(KVH - 1, u)
                    pe.wait_ge(al_ready, u + 1)
                elif u == 8:
                    values(KVH - 1, 2)
                elif u == 10:
                    turn_probs(KVH - 1, 3)
                elif u == 11:
                    values(KVH - 1, 3)
                elif 12 <= u < 16:
                    pe.wait_ge(al_ready, u - 3)
                merge(0, 0, u)
            with pe.Fori(1, M_IT - 1) as m:
                for u in range(M_UN):
                    merge(m * M_UN, m * 2, u)
            last = (M_IT - 1) * M_UN
            for u in range(8):
                merge(last, 2 * (M_IT - 1), u)
            for u in range(4):
                quarter(U_M + last + 8, 0, u, B, J_O - 1, ATT)

            def turn_panel(j):
                pe.wait_ge(panel_added, j + 1)
                for k in range(4 * j, 4 * j + 4):
                    turn_norm(h1, KD, k)

            for j in range(4):
                if j < 2:
                    job((A, B)[j], J_O)
                else:
                    pe.wait_ge(panel_added, j - 1)
                for u in range(8):
                    if j == 0:
                        pe.wait_ge(ml_ready, u // 2 + 1)
                    rows(U_O + 8 * j + u, 0, (A, B)[j % 2], (mH, mL), KD, 2 * u)
                    if u == 3 and j:
                        turn_panel(j - 1)

            for u in range(F_UN):
                if u == 0:
                    pe.wait_ge(panel_added, 3)
                    pe.wait_ge(u_ready, KD + 12)
                if u == 2:
                    turn_panel(3)
                if u == 4:
                    pe.wait_ge(panel_added, 4)
                    turn_rstd(2)
                columns(U_F + u, 0, (A, B)[u // 4], U, KD, 4 * (u % 4), 4,
                        before=(lambda kk: pe.wait_ge(u_ready, KD + kk + 1)) if u == 3 else None)
            with pe.Fori(1, F_IT) as f:
                for u in range(F_UN):
                    if u == 0:
                        pe.wait_ge(gs_ready, f)
                    if u == 4:
                        job(B, f + J_O)
                    columns(U_F + u, f * F_UN, (A, B)[u // 4], U, KD, 4 * (u % 4), 4)

            half = E_UN // 2
            for n in range(4):
                if n == 0:
                    pe.wait_ge(gs_ready, F_IT)
                elif n == 1:
                    job(B, J_O + F_IT)
                else:
                    pe.wait_ge(panel_added, n + 3)
                for u in range(half):
                    if n == 0 and u >= half - 1:
                        pe.wait_ge(hl_ready, F_IT)
                    elif n == 0 and u == 0:
                        pe.wait_ge(hl_ready, F_IT - 1)
                    if n < 3 or u < half - SLOTS:
                        rows(U_E + half * n + u, 0, (A, B)[n % 2], (hH, hL), KF, 2 * u)
            for t in range(TT):
                for u in range(half - SLOTS, half):
                    last = rows(UNITS - half + u, 0, B, (hH, hL), KF, 2 * u, tiles=(t,))
                if t == 0:
                    last.then_inc(tile0_done, 1)


def kernel(**inputs):
    import numpy as np
    import concourse.bacc as bacc
    from concourse.bass_utils import run_bass_kernel_spmd

    a = {n: np.ascontiguousarray(v) for n, v in inputs.items()}

    def channels(v, tiles):
        return v.reshape(tiles, P, -1).transpose(1, 0, 2).reshape(P, -1)

    def heads(v):
        return np.concatenate([v.reshape(SH, 1), np.zeros((P - SH, 1), np.float32)])

    params = np.ascontiguousarray(np.concatenate([
        channels(a["attn_norm_w"][0], KD), channels(a["ffn_norm_w"][0], KD),
        channels(a["ssm_conv_w"][0].T, 48), channels(a["ssm_conv_b"][0], 48),
        channels(a["ssm_norm_w"][0], DI // P), channels(a["ffn_conv_w"][0].T, KF), channels(a["ffn_conv_b"][0], KF),
        heads(a["dt_bias"][0]), heads(a["a_log"][0]),
        np.broadcast_to(a["d_skip"], (P, SH)), np.broadcast_to(a["attn_sinks"], (P, AH))], axis=1))
    feeds = {
        "x": a["x"].reshape(SEQ, D), "params": params, "w_in": a["w_in"][0], "w_ssm_out": a["w_ssm_out"][0],
        "w_attn_out": a["w_attn_out"][0], "w_o": a["w_o"][0], "w_ffn_in": a["w_ffn_in"][0],
        "w_ffn_out": a["w_ffn_out"][0], "final_norm_w": a["final_norm_w"].reshape(1, D),
    }
    nc = bacc.Bacc("TRN2", target_bir_lowering=False, num_devices=1)
    args = [nc.dram_tensor(n, v.shape, mybir.dt.from_np(v.dtype), kind="ExternalInput").ap() for n, v in feeds.items()]
    out = nc.dram_tensor("out", (SEQ, D), F32, kind="ExternalOutput").ap()
    build(nc, *args, out)
    r = run_bass_kernel_spmd(nc, [feeds], core_ids=[0])
    return r.results[0]["out"].reshape(1, SEQ, D)
```
